# Optimizing a Trainium2 kernel written in Bass

```python
import jax
import jax.numpy as jnp
from jax import lax
import numpy as np

D_MODEL = 1024
BATCH = 1
SEQ = 256
DEPTH = 2

EPS = 1e-6
CONV_WIDTH = 4
LRU_WIDTH = D_MODEL // 2
LRU_BLOCKS = 8
LRU_BLOCK = LRU_WIDTH // LRU_BLOCKS
LRU_C = 8.0
ATT_HEAD_DIM = 64
ATT_Q_HEADS = (D_MODEL // 2) // ATT_HEAD_DIM
ATT_KV_HEADS = 2
ATT_GROUPS = ATT_Q_HEADS // ATT_KV_HEADS
ATT_Q_WIDTH = ATT_Q_HEADS * ATT_HEAD_DIM
ATT_KV_WIDTH = ATT_KV_HEADS * ATT_HEAD_DIM
WINDOW = 128
ROPE_THETA = 10000.0
EVEN_IN_COLS = 2 * LRU_WIDTH + ATT_Q_WIDTH + 2 * ATT_KV_WIDTH
EVEN_MIX_WIDTH = LRU_WIDTH + ATT_Q_WIDTH
D_FF_DENSE = 2816
GDN_HEADS = 8
GDN_HEAD_DIM = 128
GDN_WIDTH = GDN_HEADS * GDN_HEAD_DIM
GDN_CHUNK = 64
ODD_IN_COLS = 4 * GDN_WIDTH + 2 * GDN_HEADS
N_EXPERTS = 8
TOP_K = 2
D_FF_EXPERT = 3584
N_EVEN = (DEPTH + 1) // 2
N_ODD = DEPTH // 2


def rms_norm(x, g):
    xf = x.astype(jnp.float32)
    y = xf * lax.rsqrt(jnp.mean(xf * xf, axis=-1, keepdims=True) + EPS)
    return (y * g.astype(jnp.float32)).astype(x.dtype)

def l2_norm(x):
    return x * lax.rsqrt(jnp.sum(x * x, axis=-1, keepdims=True) + EPS)

def causal_depthwise_conv(x, w):
    seq = x.shape[1]
    xp = jnp.pad(x, ((0, 0), (CONV_WIDTH - 1, 0), (0, 0)))
    return sum(w[j] * xp[:, j:j + seq] for j in range(CONV_WIDTH))

def rope(x, pos):
    half = x.shape[-1] // 2
    inv_freq = ROPE_THETA ** (-jnp.arange(half, dtype=jnp.float32) / half)
    ang = pos.astype(jnp.float32)[:, None] * inv_freq[None, :]
    cos = jnp.cos(ang)[None, :, None, :]
    sin = jnp.sin(ang)[None, :, None, :]
    xf = x.astype(jnp.float32)
    x1, x2 = xf[..., :half], xf[..., half:]
    return jnp.concatenate([x1 * cos - x2 * sin, x2 * cos + x1 * sin], axis=-1)

def swiglu(h, w_gate, w_up, w_down):
    return (jax.nn.silu(h @ w_gate) * (h @ w_up)) @ w_down

def rg_lru(xb, conv_w, conv_b, w_a, b_a, w_i, b_i, lam):
    bsz, seq, _ = xb.shape
    xc = causal_depthwise_conv(xb, conv_w) + conv_b
    xh = xc.reshape(bsz, seq, LRU_BLOCKS, LRU_BLOCK)
    r = jax.nn.sigmoid(jnp.einsum('bshi,hij->bshj', xh, w_a).reshape(bsz, seq, LRU_WIDTH) + b_a)
    gi = jax.nn.sigmoid(jnp.einsum('bshi,hij->bshj', xh, w_i).reshape(bsz, seq, LRU_WIDTH) + b_i)
    log_a = -LRU_C * r * jax.nn.softplus(-lam)
    a = jnp.exp(log_a)
    u = jnp.sqrt(-jnp.expm1(2.0 * log_a)) * (gi * xc)

    def combine(c1, c2):
        a1, b1 = c1
        a2, b2 = c2
        return a1 * a2, a2 * b1 + b2

    _, h = lax.associative_scan(combine, (a, u), axis=1)
    return h

def sliding_window_attention(q, k, v, sinks):
    bsz, seq = q.shape[:2]
    nb = seq // WINDOW
    qb = q.astype(jnp.float32).reshape(bsz, nb, WINDOW, ATT_KV_HEADS, ATT_GROUPS, ATT_HEAD_DIM)

    def with_prev(t):
        tb = t.astype(jnp.float32).reshape(bsz, nb, WINDOW, ATT_KV_HEADS, ATT_HEAD_DIM)
        prev = jnp.pad(tb, ((0, 0), (1, 0), (0, 0), (0, 0), (0, 0)))[:, :-1]
        return jnp.concatenate([prev, tb], axis=2)

    kb, vb = with_prev(k), with_prev(v)
    s = jnp.einsum('bnqhgd,bnkhd->bnhgqk', qb, kb) * (ATT_HEAD_DIM ** -0.5)
    qi = jnp.arange(WINDOW)[:, None] + WINDOW
    kj = jnp.arange(2 * WINDOW)[None, :]
    rel = qi - kj
    band = (rel >= 0) & (rel < WINDOW)
    valid = band[None] & ((jnp.arange(nb)[:, None, None] > 0) | (kj >= WINDOW)[None])
    s = jnp.where(valid[None, :, None, None], s, -1e30)
    sink = sinks.astype(jnp.float32).reshape(ATT_KV_HEADS, ATT_GROUPS)[None, None, :, :, None, None]
    m = jnp.maximum(jnp.max(s, axis=-1, keepdims=True), sink)
    p = jnp.exp(s - m)
    denom = jnp.sum(p, axis=-1, keepdims=True) + jnp.exp(sink - m)
    o = jnp.einsum('bnhgqk,bnkhd->bnqhgd', p / denom, vb)
    return o.reshape(bsz, seq, ATT_Q_WIDTH)

def even_mixer(h, pos, w_in, conv_w, conv_b, w_a, b_a, w_i, b_i, lam, q_norm, k_norm, sinks, w_out):
    bsz, seq, _ = h.shape
    proj = h @ w_in
    cuts = np.cumsum([LRU_WIDTH, LRU_WIDTH, ATT_Q_WIDTH, ATT_KV_WIDTH]).tolist()
    xb, gate, q, k, v = jnp.split(proj, cuts, axis=-1)
    y_lru = rg_lru(xb.astype(jnp.float32), conv_w, conv_b, w_a, b_a, w_i, b_i, lam) \
        * jax.nn.gelu(gate.astype(jnp.float32))
    q = rope(rms_norm(q.reshape(bsz, seq, ATT_Q_HEADS, ATT_HEAD_DIM), q_norm), pos)
    k = rope(rms_norm(k.reshape(bsz, seq, ATT_KV_HEADS, ATT_HEAD_DIM), k_norm), pos)
    v = v.reshape(bsz, seq, ATT_KV_HEADS, ATT_HEAD_DIM)
    y_att = sliding_window_attention(q, k, v, sinks)
    y = jnp.concatenate([y_lru.astype(h.dtype), y_att.astype(h.dtype)], axis=-1)
    return y @ w_out

def gated_deltanet(h, w_in, conv_w, a_log, dt_bias, out_norm, w_out):
    bsz, seq, _ = h.shape
    nc = seq // GDN_CHUNK
    C = GDN_CHUNK
    proj = (h @ w_in).astype(jnp.float32)
    cuts = [3 * GDN_WIDTH, 4 * GDN_WIDTH, 4 * GDN_WIDTH + GDN_HEADS]
    qkv, gate, a_in, b_in = jnp.split(proj, cuts, axis=-1)
    qkv = jax.nn.silu(causal_depthwise_conv(qkv, conv_w.astype(jnp.float32)))
    q, k, v = jnp.split(qkv, 3, axis=-1)
    q = l2_norm(q.reshape(bsz, seq, GDN_HEADS, GDN_HEAD_DIM)) * (GDN_HEAD_DIM ** -0.5)
    k = l2_norm(k.reshape(bsz, seq, GDN_HEADS, GDN_HEAD_DIM))
    v = v.reshape(bsz, seq, GDN_HEADS, GDN_HEAD_DIM)
    beta = jax.nn.sigmoid(b_in)
    g = -jnp.exp(a_log.astype(jnp.float32)) * jax.nn.softplus(a_in + dt_bias.astype(jnp.float32))

    def to_chunks(t):
        return t.reshape(bsz, nc, C, GDN_HEADS, -1).transpose(0, 3, 1, 2, 4)

    qc, kc, vc = to_chunks(q), to_chunks(k), to_chunks(v)
    gc = g.reshape(bsz, nc, C, GDN_HEADS).transpose(0, 3, 1, 2)
    bc = beta.reshape(bsz, nc, C, GDN_HEADS).transpose(0, 3, 1, 2)
    G = jnp.cumsum(gc, axis=-1)
    tri = jnp.tril(jnp.ones((C, C), dtype=bool))
    strict = jnp.tril(jnp.ones((C, C), dtype=bool), -1)
    diff = G[..., :, None] - G[..., None, :]
    decay = jnp.where(tri, jnp.exp(jnp.where(tri, diff, 0.0)), 0.0)
    kk = jnp.einsum('bhnid,bhnjd->bhnij', kc, kc)
    A = jnp.where(strict, bc[..., :, None] * kk * decay, 0.0) + jnp.eye(C, dtype=jnp.float32)
    u = lax.linalg.triangular_solve(A, bc[..., None] * vc, left_side=True, lower=True, unit_diagonal=True)
    w = lax.linalg.triangular_solve(A, bc[..., None] * jnp.exp(G)[..., None] * kc,
                                    left_side=True, lower=True, unit_diagonal=True)
    a_qk = jnp.where(tri, jnp.einsum('bhnid,bhnjd->bhnij', qc, kc) * decay, 0.0)
    q_dec = qc * jnp.exp(G)[..., None]
    k_dec = kc * jnp.exp(G[..., -1:] - G)[..., None]
    g_last = jnp.exp(G[..., -1])
    xs = (jnp.moveaxis(u, 2, 0), jnp.moveaxis(w, 2, 0), jnp.moveaxis(a_qk, 2, 0),
          jnp.moveaxis(q_dec, 2, 0), jnp.moveaxis(k_dec, 2, 0), jnp.moveaxis(g_last, 2, 0))

    def step(state, inp):
        u_c, w_c, a_c, qd_c, kd_c, gl_c = inp
        v_new = u_c - jnp.einsum('bhcd,bhde->bhce', w_c, state)
        o_c = jnp.einsum('bhcd,bhde->bhce', qd_c, state) + jnp.einsum('bhcj,bhje->bhce', a_c, v_new)
        state = state * gl_c[..., None, None] + jnp.einsum('bhcd,bhce->bhde', kd_c, v_new)
        return state, o_c

    s0 = jnp.zeros((bsz, GDN_HEADS, GDN_HEAD_DIM, GDN_HEAD_DIM), jnp.float32)
    _, o = lax.scan(step, s0, xs)
    o = o.transpose(1, 0, 3, 2, 4).reshape(bsz, seq, GDN_HEADS, GDN_HEAD_DIM)
    o = rms_norm(o, out_norm) * jax.nn.silu(gate.reshape(bsz, seq, GDN_HEADS, GDN_HEAD_DIM))
    return o.reshape(bsz, seq, GDN_WIDTH).astype(h.dtype) @ w_out

def moe_swiglu(h, router, w_gate, w_up, w_down):
    bsz, seq, d = h.shape
    t = h.reshape(-1, d)
    logits = (t @ router).astype(jnp.float32)
    top_v, top_i = lax.top_k(logits, TOP_K)
    top_w = jax.nn.softmax(top_v, axis=-1)
    gates = jnp.sum(jax.nn.one_hot(top_i, N_EXPERTS, dtype=jnp.float32) * top_w[..., None], axis=1)
    out = jnp.zeros(t.shape, jnp.float32)
    for e in range(N_EXPERTS):
        y_e = swiglu(t, w_gate[e], w_up[e], w_down[e]).astype(jnp.float32)
        out = out + gates[:, e:e + 1] * y_e
    return out.astype(h.dtype).reshape(bsz, seq, d)

def first_inputs(seed: int = 0) -> dict:
    key = jax.random.key(seed)
    ks = jax.random.split(key, 32)
    f32 = jnp.float32
    D = D_MODEL

    def nrm(k, shape, scale):
        return scale * jax.random.normal(k, shape, f32)

    lru_u = jax.random.uniform(ks[10], (N_EVEN, LRU_WIDTH), f32, minval=0.9, maxval=0.999)
    lru_s = lru_u ** (1.0 / LRU_C)
    dt = jnp.exp(jax.random.uniform(ks[21], (N_ODD, GDN_HEADS), f32,
                                    minval=float(np.log(0.001)), maxval=float(np.log(0.1))))
    return {
        "x": nrm(ks[0], (BATCH, SEQ, D), 1.0),
        "ln_mix": 1.0 + nrm(ks[1], (DEPTH, D), 0.02),
        "ln_ffn": 1.0 + nrm(ks[2], (DEPTH, D), 0.02),
        "e_w_in": nrm(ks[3], (N_EVEN, D, EVEN_IN_COLS), D ** -0.5),
        "e_lru_conv_w": nrm(ks[4], (N_EVEN, CONV_WIDTH, LRU_WIDTH), CONV_WIDTH ** -0.5),
        "e_lru_conv_b": nrm(ks[5], (N_EVEN, LRU_WIDTH), 0.02),
        "e_lru_w_a": nrm(ks[6], (N_EVEN, LRU_BLOCKS, LRU_BLOCK, LRU_BLOCK), LRU_BLOCK ** -0.5),
        "e_lru_b_a": nrm(ks[7], (N_EVEN, LRU_WIDTH), 0.1),
        "e_lru_w_i": nrm(ks[8], (N_EVEN, LRU_BLOCKS, LRU_BLOCK, LRU_BLOCK), LRU_BLOCK ** -0.5),
        "e_lru_b_i": nrm(ks[9], (N_EVEN, LRU_WIDTH), 0.1),
        "e_lru_lambda": jnp.log(lru_s) - jnp.log1p(-lru_s),
        "e_q_norm": 1.0 + nrm(ks[11], (N_EVEN, ATT_HEAD_DIM), 0.02),
        "e_k_norm": 1.0 + nrm(ks[12], (N_EVEN, ATT_HEAD_DIM), 0.02),
        "e_sinks": nrm(ks[13], (N_EVEN, ATT_Q_HEADS), 1.0),
        "e_w_out": nrm(ks[14], (N_EVEN, EVEN_MIX_WIDTH, D), EVEN_MIX_WIDTH ** -0.5),
        "e_ffn_w_gate": nrm(ks[15], (N_EVEN, D, D_FF_DENSE), D ** -0.5),
        "e_ffn_w_up": nrm(ks[16], (N_EVEN, D, D_FF_DENSE), D ** -0.5),
        "e_ffn_w_down": nrm(ks[17], (N_EVEN, D_FF_DENSE, D), D_FF_DENSE ** -0.5),
        "o_w_in": nrm(ks[18], (N_ODD, D, ODD_IN_COLS), D ** -0.5),
        "o_conv_w": nrm(ks[19], (N_ODD, CONV_WIDTH, 3 * GDN_WIDTH), CONV_WIDTH ** -0.5),
        "o_a_log": jnp.log(jax.random.uniform(ks[20], (N_ODD, GDN_HEADS), f32, minval=1.0, maxval=16.0)),
        "o_dt_bias": dt + jnp.log(-jnp.expm1(-dt)),
        "o_out_norm": 1.0 + nrm(ks[22], (N_ODD, GDN_HEAD_DIM), 0.02),
        "o_w_out": nrm(ks[23], (N_ODD, GDN_WIDTH, D), GDN_WIDTH ** -0.5),
        "o_router": nrm(ks[24], (N_ODD, D, N_EXPERTS), D ** -0.5),
        "o_moe_w_gate": nrm(ks[25], (N_ODD, N_EXPERTS, D, D_FF_EXPERT), D ** -0.5),
        "o_moe_w_up": nrm(ks[26], (N_ODD, N_EXPERTS, D, D_FF_EXPERT), D ** -0.5),
        "o_moe_w_down": nrm(ks[27], (N_ODD, N_EXPERTS, D_FF_EXPERT, D), D_FF_EXPERT ** -0.5),
    }

def first_block(x, ln_mix, ln_ffn,
              e_w_in, e_lru_conv_w, e_lru_conv_b, e_lru_w_a, e_lru_b_a, e_lru_w_i, e_lru_b_i,
              e_lru_lambda, e_q_norm, e_k_norm, e_sinks, e_w_out, e_ffn_w_gate, e_ffn_w_up, e_ffn_w_down,
              o_w_in, o_conv_w, o_a_log, o_dt_bias, o_out_norm, o_w_out, o_router,
              o_moe_w_gate, o_moe_w_up, o_moe_w_down):
    pos = jnp.arange(x.shape[1], dtype=jnp.int32)
    h = x
    for layer in range(DEPTH):
        j = layer // 2
        hn = rms_norm(h, ln_mix[layer])
        if layer % 2 == 0:
            h = h + even_mixer(hn, pos, e_w_in[j], e_lru_conv_w[j], e_lru_conv_b[j], e_lru_w_a[j],
                               e_lru_b_a[j], e_lru_w_i[j], e_lru_b_i[j], e_lru_lambda[j],
                               e_q_norm[j], e_k_norm[j], e_sinks[j], e_w_out[j]).astype(h.dtype)
            h = h + swiglu(rms_norm(h, ln_ffn[layer]), e_ffn_w_gate[j], e_ffn_w_up[j],
                           e_ffn_w_down[j]).astype(h.dtype)
        else:
            h = h + gated_deltanet(hn, o_w_in[j], o_conv_w[j], o_a_log[j], o_dt_bias[j],
                                   o_out_norm[j], o_w_out[j]).astype(h.dtype)
            h = h + moe_swiglu(rms_norm(h, ln_ffn[layer]), o_router[j], o_moe_w_gate[j],
                               o_moe_w_up[j], o_moe_w_down[j]).astype(h.dtype)
    return h


DEPTH_2 = 1

N_MEM = 256
D_FF = 2816
HG_HEADS = 4
HG_DK = 128
HG_DV = 128
HG_CHUNK = 64
HG_K = HG_HEADS * HG_DK
HG_V = HG_HEADS * HG_DV
HG_COLS = 2 * HG_K + 2 * HG_V
DIL_GROUPS = ((128, 1), (512, 4), (2048, 16))
DIL_HEADS = 4
DIL_DH = 128
DIL_W = DIL_HEADS * DIL_DH
DIL_COLS = len(DIL_GROUPS) * 3 * DIL_W
ALIBI_HEADS = len(DIL_GROUPS) * DIL_HEADS
MEM_HEADS = 4
MEM_DH = 128
MEM_W = MEM_HEADS * MEM_DH
N_BRANCH = 3
GATE_COLS = N_BRANCH * D_MODEL
SPLITS = (HG_K, 2 * HG_K, 2 * HG_K + HG_V, HG_COLS, HG_COLS + DIL_COLS, HG_COLS + DIL_COLS + MEM_W)
D_IN = HG_COLS + DIL_COLS + MEM_W + GATE_COLS


def rmsnorm(x, w):
    xf = x.astype(jnp.float32)
    y = xf * lax.rsqrt(jnp.mean(xf * xf, axis=-1, keepdims=True) + EPS)
    return (y * w.astype(jnp.float32)).astype(x.dtype)

def swiglu_2(x, w_gu, w_down):
    g, u = jnp.split(x @ w_gu, 2, axis=-1)
    return (jax.nn.silu(g) * u) @ w_down

def alibi_slopes():
    return 2.0 ** (-8.0 * jnp.arange(1, ALIBI_HEADS + 1, dtype=jnp.float32) / ALIBI_HEADS)

def hgrn2(q_raw, f_raw, i_raw, lb):
    B, S = q_raw.shape[:2]
    C = HG_CHUNK
    N = S // C
    f32 = jnp.float32
    q = jax.nn.silu(q_raw.astype(f32)).reshape(B, N, C, HG_HEADS, HG_DK)
    lbh = lb.reshape(HG_HEADS, HG_DK)
    f = lbh + (1.0 - lbh) * jax.nn.sigmoid(f_raw.astype(f32).reshape(B, N, C, HG_HEADS, HG_DK))
    k = 1.0 - f
    v = i_raw.astype(f32).reshape(B, N, C, HG_HEADS, HG_DV)
    b = jnp.cumsum(jnp.log(f), axis=2)
    ref = b[:, :, C // 2 - 1:C // 2]
    scores = jnp.einsum('bnchk,bnshk->bnhcs', q * jnp.exp(b - ref), k * jnp.exp(ref - b))
    causal = jnp.tril(jnp.ones((C, C), dtype=bool))
    scores = jnp.where(causal, scores, 0.0)
    o_intra = jnp.einsum('bnhcs,bnshv->bnchv', scores, v)
    b_last = b[:, :, -1:]
    kv = jnp.einsum('bnshk,bnshv->nbhkv', k * jnp.exp(b_last - b), v)
    decay = jnp.moveaxis(jnp.exp(b_last[:, :, 0]), 1, 0)

    def step(state, inp):
        kv_n, dec_n = inp
        return dec_n[..., None] * state + kv_n, state

    s0 = jnp.zeros((B, HG_HEADS, HG_DK, HG_DV), f32)
    _, s_prev = lax.scan(step, s0, (kv, decay))
    o_inter = jnp.einsum('bnchk,nbhkv->bnchv', q * jnp.exp(b), s_prev)
    return (o_intra + o_inter).reshape(B, S, HG_HEADS, HG_DV)

def dilated_group(q, k, v, window, dil, slopes):
    B, S, H, dh = q.shape
    nk = window // dil
    span = nk * dil
    Sp = -(-S // span) * span
    L = Sp // dil
    nb = L // nk

    def to_sub(t):
        t = jnp.pad(t, ((0, 0), (0, Sp - S), (0, 0), (0, 0)))
        return t.reshape(B, L, dil, H, dh).transpose(0, 2, 1, 3, 4).reshape(B * dil, nb, nk, H, dh)

    qs, ks, vs = to_sub(q), to_sub(k), to_sub(v)
    kb = jnp.concatenate([jnp.pad(ks, ((0, 0), (1, 0), (0, 0), (0, 0), (0, 0)))[:, :-1], ks], axis=2)
    vb = jnp.concatenate([jnp.pad(vs, ((0, 0), (1, 0), (0, 0), (0, 0), (0, 0)))[:, :-1], vs], axis=2)
    s = jnp.einsum('znqhd,znkhd->znhqk', qs, kb).astype(jnp.float32) * (dh ** -0.5)
    qi = jnp.arange(nk)[:, None]
    kj = jnp.arange(2 * nk)[None, :]
    delta = nk + qi - kj
    blk = jnp.arange(nb)[:, None, None]
    valid = (delta >= 0) & (delta <= nk) & ((blk > 0) | (kj >= nk))
    s = s - slopes[:, None, None] * (delta * dil).astype(jnp.float32)
    s = jnp.where(valid[:, None], s, -jnp.inf)
    m = jnp.max(s, axis=-1)
    p = jnp.exp(s - m[..., None])
    l = jnp.sum(p, axis=-1)
    o = jnp.einsum('znhqk,znkhd->znqhd', p.astype(vb.dtype), vb).astype(jnp.float32)
    o = o.reshape(B, dil, L, H, dh).transpose(0, 2, 1, 3, 4).reshape(B, Sp, H, dh)[:, :S]

    def stat_back(t):
        return t.transpose(0, 1, 3, 2).reshape(B, dil, L, H).transpose(0, 2, 1, 3).reshape(B, Sp, H)[:, :S]

    return o, stat_back(m), stat_back(l)

def dilated_attention(dil_cols):
    B, S = dil_cols.shape[:2]
    qkv = dil_cols.reshape(B, S, len(DIL_GROUPS), 3, DIL_HEADS, DIL_DH)
    slopes = alibi_slopes()
    outs, maxs, sums = [], [], []
    for g, (window, dil) in enumerate(DIL_GROUPS):
        o, m, l = dilated_group(qkv[:, :, g, 0], qkv[:, :, g, 1], qkv[:, :, g, 2], window, dil,
                                slopes[g * DIL_HEADS:(g + 1) * DIL_HEADS])
        outs.append(o)
        maxs.append(m)
        sums.append(l)
    m_all = jnp.stack(maxs)
    w = jnp.exp(m_all - jnp.max(m_all, axis=0))
    num = jnp.sum(w[..., None] * jnp.stack(outs), axis=0)
    den = jnp.sum(w * jnp.stack(sums), axis=0)
    return (num / den[..., None]).reshape(B, S, DIL_W).astype(dil_cols.dtype)

def memory_attention(mq, mem, mem_norm_w, w_mem_kv):
    B, S = mq.shape[:2]
    mk, mv = jnp.split(rmsnorm(mem, mem_norm_w) @ w_mem_kv, 2, axis=-1)
    mq = mq.reshape(B, S, MEM_HEADS, MEM_DH)
    mk = mk.reshape(B, N_MEM, MEM_HEADS, MEM_DH)
    mv = mv.reshape(B, N_MEM, MEM_HEADS, MEM_DH)
    s = jnp.einsum('bshd,bmhd->bhsm', mq, mk).astype(jnp.float32) * (MEM_DH ** -0.5)
    p = jax.nn.softmax(s, axis=-1).astype(mv.dtype)
    return jnp.einsum('bhsm,bmhd->bshd', p, mv).reshape(B, S, MEM_W)

def token_mixing(u, mem, w_in, b_gate, lb, hg_norm_w, mem_norm_w, w_mem_kv, w_br_hg, w_br_dil, w_br_mem, w_out):
    B, S, D = u.shape
    proj = u @ w_in
    hq, hf, hi, hog, dcols, mq, gl = jnp.split(proj, SPLITS, axis=-1)
    o_hg = rmsnorm(hgrn2(hq, hf, hi, lb), hg_norm_w)
    o_hg = o_hg * jax.nn.sigmoid(hog.astype(jnp.float32)).reshape(B, S, HG_HEADS, HG_DV)
    y_hg = o_hg.reshape(B, S, HG_V).astype(u.dtype)
    y_dil = dilated_attention(dcols)
    y_mem = memory_attention(mq, mem, mem_norm_w, w_mem_kv)
    gates = jax.nn.sigmoid((gl + b_gate).astype(jnp.float32)).astype(u.dtype).reshape(B, S, N_BRANCH, D)
    y = (gates[:, :, 0] * (y_hg @ w_br_hg)
         + gates[:, :, 1] * (y_dil @ w_br_dil)
         + gates[:, :, 2] * (y_mem @ w_br_mem))
    return y @ w_out

def second_inputs(seed: int = 0) -> dict:
    key = jax.random.key(seed)
    ks = jax.random.split(key, 22)
    f32 = jnp.float32

    def w(k, shape, fan_in):
        return jax.random.normal(k, shape, f32) * (fan_in ** -0.5)

    def gain(k, n):
        return 1.0 + 0.05 * jax.random.normal(k, (DEPTH_2, n), f32)

    return {
        'x': jax.random.normal(ks[0], (BATCH, SEQ, D_MODEL), f32),
        'mem': jax.random.normal(ks[1], (BATCH, N_MEM, D_MODEL), f32),
        'ffn1_pre_w': gain(ks[2], D_MODEL),
        'ffn1_w_gu': w(ks[3], (DEPTH_2, D_MODEL, 2 * D_FF), D_MODEL),
        'ffn1_w_down': w(ks[4], (DEPTH_2, D_FF, D_MODEL), D_FF),
        'ffn1_post_w': gain(ks[5], D_MODEL),
        'mix_pre_w': gain(ks[6], D_MODEL),
        'w_in': w(ks[7], (DEPTH_2, D_MODEL, D_IN), D_MODEL),
        'b_gate': 0.01 * jax.random.normal(ks[8], (DEPTH_2, GATE_COLS), f32),
        'hg_lb_logits': 0.1 * jax.random.normal(ks[9], (DEPTH_2 + 1, HG_K), f32),
        'hg_norm_w': gain(ks[10], HG_DV),
        'mem_norm_w': gain(ks[11], D_MODEL),
        'w_mem_kv': w(ks[12], (DEPTH_2, D_MODEL, 2 * MEM_W), D_MODEL),
        'w_br_hg': w(ks[13], (DEPTH_2, HG_V, D_MODEL), HG_V),
        'w_br_dil': w(ks[14], (DEPTH_2, DIL_W, D_MODEL), DIL_W),
        'w_br_mem': w(ks[15], (DEPTH_2, MEM_W, D_MODEL), MEM_W),
        'w_out': w(ks[16], (DEPTH_2, D_MODEL, D_MODEL), D_MODEL),
        'mix_post_w': gain(ks[17], D_MODEL),
        'ffn2_pre_w': gain(ks[18], D_MODEL),
        'ffn2_w_gu': w(ks[19], (DEPTH_2, D_MODEL, 2 * D_FF), D_MODEL),
        'ffn2_w_down': w(ks[20], (DEPTH_2, D_FF, D_MODEL), D_FF),
        'ffn2_post_w': gain(ks[21], D_MODEL),
    }

def second_block(x, mem, ffn1_pre_w, ffn1_w_gu, ffn1_w_down, ffn1_post_w, mix_pre_w, w_in, b_gate,
              hg_lb_logits, hg_norm_w, mem_norm_w, w_mem_kv, w_br_hg, w_br_dil, w_br_mem, w_out,
              mix_post_w, ffn2_pre_w, ffn2_w_gu, ffn2_w_down, ffn2_post_w):
    lb_all = jnp.cumsum(jax.nn.softmax(hg_lb_logits.astype(jnp.float32), axis=0), axis=0)
    h = x
    for l in range(DEPTH_2):
        h = h + 0.5 * rmsnorm(swiglu_2(rmsnorm(h, ffn1_pre_w[l]), ffn1_w_gu[l], ffn1_w_down[l]), ffn1_post_w[l])
        u = rmsnorm(h, mix_pre_w[l])
        y = token_mixing(u, mem, w_in[l], b_gate[l], lb_all[l], hg_norm_w[l], mem_norm_w[l], w_mem_kv[l],
                         w_br_hg[l], w_br_dil[l], w_br_mem[l], w_out[l])
        h = h + rmsnorm(y, mix_post_w[l])
        h = h + 0.5 * rmsnorm(swiglu_2(rmsnorm(h, ffn2_pre_w[l]), ffn2_w_gu[l], ffn2_w_down[l]), ffn2_post_w[l])
    return h


def setup_inputs(seed=0):
    out = dict(first_inputs(seed))
    for name, value in second_inputs(seed + 1).items():
        if name != "x":
            out[name + "_2"] = value
    return out


def reference(
    x, ln_mix, ln_ffn, e_w_in, e_lru_conv_w, e_lru_conv_b, e_lru_w_a, e_lru_b_a, e_lru_w_i,
    e_lru_b_i, e_lru_lambda, e_q_norm, e_k_norm, e_sinks, e_w_out, e_ffn_w_gate, e_ffn_w_up,
    e_ffn_w_down, o_w_in, o_conv_w, o_a_log, o_dt_bias, o_out_norm, o_w_out, o_router,
    o_moe_w_gate, o_moe_w_up, o_moe_w_down, mem_2, ffn1_pre_w_2, ffn1_w_gu_2, ffn1_w_down_2,
    ffn1_post_w_2, mix_pre_w_2, w_in_2, b_gate_2, hg_lb_logits_2, hg_norm_w_2, mem_norm_w_2,
    w_mem_kv_2, w_br_hg_2, w_br_dil_2, w_br_mem_2, w_out_2, mix_post_w_2, ffn2_pre_w_2,
    ffn2_w_gu_2, ffn2_w_down_2, ffn2_post_w_2,
):
    x = first_block(
        x, ln_mix, ln_ffn, e_w_in, e_lru_conv_w, e_lru_conv_b, e_lru_w_a, e_lru_b_a, e_lru_w_i,
        e_lru_b_i, e_lru_lambda, e_q_norm, e_k_norm, e_sinks, e_w_out, e_ffn_w_gate, e_ffn_w_up,
        e_ffn_w_down, o_w_in, o_conv_w, o_a_log, o_dt_bias, o_out_norm, o_w_out, o_router,
        o_moe_w_gate, o_moe_w_up, o_moe_w_down,
    )
    return second_block(
        x, mem_2, ffn1_pre_w_2, ffn1_w_gu_2, ffn1_w_down_2, ffn1_post_w_2, mix_pre_w_2, w_in_2,
        b_gate_2, hg_lb_logits_2, hg_norm_w_2, mem_norm_w_2, w_mem_kv_2, w_br_hg_2, w_br_dil_2,
        w_br_mem_2, w_out_2, mix_post_w_2, ffn2_pre_w_2, ffn2_w_gu_2, ffn2_w_down_2,
        ffn2_post_w_2,
    )


_drawn_inputs = setup_inputs


def setup_inputs(seed=0):
    import zlib

    import numpy as np

    out = dict(_drawn_inputs(seed))
    spreads = {}
    factors = {'e_q_norm': 3.183,
     'e_k_norm': 8.0,
     'e_sinks': 3.048,
     'o_out_norm': 3.198,
     'ffn1_post_w_2': 3.093,
     'b_gate_2': 38.494,
     'hg_lb_logits_2': 64.0,
     'mem_norm_w_2': 7.358,
     'ffn2_pre_w_2': 2.897,
     'ffn2_post_w_2': 4.257,
     'hg_norm_w_2': 8.0,
     'mix_post_w_2': 2.919}
    for name, (base, spread) in spreads.items():
        noise = np.random.default_rng([zlib.crc32(name.encode()), seed]).standard_normal(out[name].shape)
        drawn = base * np.exp(spread * noise) if base else spread * noise
        out[name] = jnp.asarray(drawn.astype(out[name].dtype))
    for name, factor in factors.items():
        out[name] = (out[name] * factor).astype(out[name].dtype)
    return out
```

```python
import numpy as np
import concourse.bass as bass
from concourse import mybir
from contextlib import ExitStack

F32 = mybir.dt.float32
U32 = mybir.dt.uint32
ALU = mybir.AluOpType
ACT = mybir.ActivationFunctionType
AX = mybir.AxisListType

P = 128
S = 256
NT = S // P
D = 1024
KD = D // P
EPS = 1e-6
CONV = 4
CHUNK = 64
BIG = 1e30
FF = 2816
FFE = 3584
EXPERTS = 8
GH = 8
ATT_SLOTS = 8
DIL = 3
MH = 4

UNIT = 2048
RING = 7
FF_STEPS = FF // 256
FFE_STEPS = FFE // 256
FF_UNITS = 3 * FF_STEPS
FFE_UNITS = 3 * FFE_STEPS
assert FFE_UNITS % RING == 0


def units_before():
    at, n = {}, 0
    for name, count in (("mix0_in", 7), ("mix0_out", 4), ("ffn0", FF_UNITS), ("gdn_in", 16), ("gdn_out", 4),
                        ("moe", EXPERTS * FFE_UNITS), ("ffn1", FF_UNITS), ("mem_kv", 4), ("hg_in", 8),
                        ("dil_in", 18), ("mq_in", 2), ("gl_in", 12), ("branch", 6), ("mix2_out", 4),
                        ("ffn2", FF_UNITS)):
        at[name] = n
        n += count
    at["end"] = n
    return at


AT = units_before()
PAST = {"ffn0": 0, "moe": FF_STEPS, "ffn1": FF_STEPS + EXPERTS * FFE_STEPS, "ffn2": 2 * FF_STEPS + EXPERTS * FFE_STEPS}
UNITS = AT["end"]


def small_layout():
    cols, n = {}, 0
    for name, width in (
            ("ident", P), ("cum", P), ("same", P), ("ones", P), ("low", P), ("up", P), ("level", 6 * P),
            ("band", 2 * P), ("dist", DIL * 2 * P), ("cos", NT * 32), ("sin", NT * 32), ("reset", S),
            ("gain", 8 * KD), ("lru_w", 4 * CONV), ("lru_b", 4), ("lru_wa", 4 * P), ("lru_wi", 4 * P),
            ("lru_ba", 4), ("lru_bi", 4), ("lam", 4), ("q_norm", 64), ("k_norm", 64), ("sinks", ATT_SLOTS),
            ("gdn_conv", 24 * CONV), ("w_ab", KD * 16), ("a_log", GH), ("dt_bias", GH), ("out_norm", P),
            ("router", KD * EXPERTS), ("b_gate", 24), ("hg_logits", 2 * MH), ("hg_norm", P)):
        cols[name] = (n, width)
        n += width
    return cols, n


COLS, SMALL = small_layout()
SLOPES = [2.0 ** (-8.0 * (i + 1) / (DIL * MH)) for i in range(DIL * MH)]


def build(nc, small_d, post_d, w_d, x_d, mem_d, out_d, upto=99):
    ctx = ExitStack()
    with ctx:
        def sb(name, *shape):
            return ctx.enter_context(nc.sbuf_tensor(name, [P, *shape], F32))

        sems = {}

        def sem(name):
            if name not in sems:
                sems[name] = ctx.enter_context(nc.semaphore(name))
            return sems[name]

        small = sb("small_sb", SMALL)
        ring = [sb(f"ring{i}", UNIT) for i in range(RING)]
        h = sb("h", NT, D)
        xnT = sb("xnT", KD, S)
        xn = sb("xn", NT, D)
        buf = [sb(f"buf{i}", 2048) for i in range(12)]
        bank = [ctx.enter_context(nc.psum_tensor(f"bank{i}", [P, 512], F32)) for i in range(8)]
        tiny = sb("tiny", 1024)
        small_conv = sb("small_conv", 4 * S)

        tiny_at = [0]

        def tin(*shape):
            n = int(np.prod(shape))
            a = tiny[:, tiny_at[0]:tiny_at[0] + n]
            tiny_at[0] += n
            assert tiny_at[0] <= 1024
            if len(shape) == 2:
                return a.rearrange("p (a b) -> p a b", b=shape[1])
            return a

        def const(name, *shape):
            o, width = COLS[name]
            a = small[:, o:o + width]
            if len(shape) == 2:
                return a.rearrange("p (a b) -> p a b", b=shape[1])
            return a

        def bview(i, *shape, off=0):
            n = int(np.prod(shape))
            a = buf[i][:, off:off + n]
            if len(shape) == 1:
                return a
            if len(shape) == 2:
                return a.rearrange("p (a b) -> p a b", b=shape[1])
            return a.rearrange("p (a b c) -> p a b c", b=shape[1], c=shape[2])

        def over_heads(a, n, width):
            return a.unsqueeze(2).broadcast_to([P, n, width])

        def per_head(a, n, width):
            return a.unsqueeze(1).broadcast_to([P, n, width])

        ident = const("ident")
        zero_col = tin(1)
        eps_col = tin(1)
        minus_half = tin(8)

        ACTV = nc.scalar.activation
        V = nc.vector
        G = nc.gpsimd
        MM = nc.tensor.matmul

        class Chain:

            def __init__(self, eng, name):
                self.eng, self.name, self.n = eng, name, 0

            def add(self, ins):
                self.n += 1
                ins.then_inc(sem(self.name), 1)
                return ins

            def sync(self):
                self.eng.wait_ge(sem(self.name), self.n)

            def step(self, ins):
                self.add(ins)
                self.sync()

        def unit_ready(pe, n):
            pe.wait_ge(sem(f"unit_in{n % RING}"), 16 * (n // RING + 1))

        def w_cols(n):
            return ring[n % RING][:, :].rearrange("p (k c) -> p k c", k=KD)

        def w_rows(n):
            return ring[n % RING][:, :].rearrange("p (k c) -> p k c", k=2)

        def product_T(n, j, dst, acts, used=True):
            for k in range(KD):
                last = MM(dst, w_cols(n)[:, k, j * P:(j + 1) * P], acts[:, k, :], start=(k == 0), stop=(k == KD - 1))
            return last

        def product(n, t, dst, acts):
            for k in range(KD):
                last = MM(dst, acts[:, k, t * P:(t + 1) * P], w_cols(n)[:, k, :], start=(k == 0), stop=(k == KD - 1))
            return last

        def product_rows(n, lhsT, first, final):
            for kk in range(2):
                for t in range(NT):
                    for c in range(2):
                        last = MM(bank[4 + 2 * t + c][:, :], lhsT[:, kk, t * P:(t + 1) * P],
                                  w_rows(n)[:, kk, c * 512:(c + 1) * 512],
                                  start=first and kk == 0, stop=final and kk == 1)
            return last

        ssq = tin(8, NT)
        rstd = tin(8, NT)

        def norm_square(act, k, src, gain, dstT):
            for t in range(NT):
                ACTV(xn[:, t, :], src[:, t, :], ACT.Square, accum_out=ssq[:, k, t:t + 1]).then_inc(sem("norm_ssq"), 1)

        def norm_pow(pool, k):
            pool.wait_ge(sem("norm_var"), k + 1)
            G.tensor_tensor(rstd[:, k, :], ssq[:, k, :], minus_half[:, 0:NT], ALU.pow).then_inc(sem("norm_rstd"), 1)

        def norm_scale(dve, k, src):
            dve.wait_ge(sem("norm_ssq"), NT * (k + 1))
            V.tensor_scalar(ssq[:, k, :], ssq[:, k, :], 1.0 / D, EPS, ALU.mult, ALU.add).then_inc(sem("norm_var"), 1)
            dve.wait_ge(sem("norm_rstd"), k + 1)
            for t in range(NT):
                V.tensor_scalar(xn[:, t, :], src[:, t, :], rstd[:, k, t:t + 1], None, ALU.mult)\
                    .then_inc(sem("norm_xn"), 1)

        def norm_transpose(pe, k):
            for t in range(NT):
                pe.wait_ge(sem("norm_xn"), NT * k + t + 1)
                for c in range(KD):
                    last = nc.tensor.transpose(bank[c // 2][:, (c % 2) * S + t * P:(c % 2) * S + (t + 1) * P],
                                               xn[:, t, c * P:(c + 1) * P], ident)
            last.then_inc(sem("norm_T"), 1)

        def norm_out_act(act, k, row, dstT):
            act.wait_ge(sem("norm_T"), k + 1)
            for c in (0, 1, 4, 5):
                ACTV(dstT[:, c, :], bank[c // 2][:, (c % 2) * S:(c % 2 + 1) * S], ACT.Copy,
                     scale=const("gain", 8, KD)[:, row, c:c + 1]).then_inc(sem("norm_done"), 1)

        def norm_out_dve(dve, k, row, dstT):
            dve.wait_ge(sem("norm_T"), k + 1)
            for c in (2, 3, 6, 7):
                V.tensor_scalar(dstT[:, c, :], bank[c // 2][:, (c % 2) * S:(c % 2 + 1) * S],
                                const("gain", 8, KD)[:, row, c:c + 1], None, ALU.mult).then_inc(sem("norm_done"), 1)

        def norm_ready(eng, k):
            eng.wait_ge(sem("norm_done"), KD * (k + 1))

        def h_ready(eng, sublayers):
            if sublayers:
                eng.wait_ge(sem("h_done"), NT * sublayers)
            else:
                eng.wait_ge(sem("x_in"), 16)

        def add_rows(dve, tag):
            dve.wait_ge(sem(tag), 1)
            for t in range(NT):
                for c in range(2):
                    last = V.tensor_tensor(h[:, t, c * 512:(c + 1) * 512], h[:, t, c * 512:(c + 1) * 512],
                                           bank[4 + 2 * t + c][:, :], ALU.add)
                last.then_inc(sem("h_done"), 1)

        pssq = tin(3, 4)
        pvar = tin(3, NT)
        prstd = tin(3, NT)

        post_gain = small_conv[:, :]

        def post_square(act, i, units):
            act.wait_ge(sem("unit_used"), units)
            for j in range(4):
                ACTV(xn[:, j // 2, (j % 2) * 512:(j % 2 + 1) * 512], bank[4 + j][:, :], ACT.Square,
                     accum_out=pssq[:, i, j:j + 1]).then_inc(sem("post_ssq"), 1)

        def post_pow(pool, i):
            pool.wait_ge(sem("post_var"), i + 1)
            G.tensor_tensor(prstd[:, i, :], pvar[:, i, :], minus_half[:, 0:NT], ALU.pow).then_inc(sem("post_rstd"), 1)

        def post_add(dve, ch, i, scale):
            dve.wait_ge(sem("post_ssq"), 4 * (i + 1))
            ch.step(V.tensor_tensor(pvar[:, i, :], pssq[:, i, 0:4:2], pssq[:, i, 1:4:2], ALU.add))
            V.tensor_scalar(pvar[:, i, :], pvar[:, i, :], 1.0 / D, EPS, ALU.mult, ALU.add)\
                .then_inc(sem("post_var"), 1)
            dve.wait_ge(sem("post_rstd"), i + 1)
            dve.wait_ge(sem("post_in"), 16 * (i + 1))
            if scale != 1.0:
                ch.step(V.tensor_scalar(prstd[:, i, :], prstd[:, i, :], scale, None, ALU.mult))
            for j in range(4):
                t, c = j // 2, slice((j % 2) * 512, (j % 2 + 1) * 512)
                gain = post_gain[:, c]
                ch.step(V.scalar_tensor_tensor(xn[:, t, c], bank[4 + j][:, :], prstd[:, i, t:t + 1], gain,
                                               ALU.mult, ALU.mult))
                ins = V.tensor_tensor(h[:, t, c], h[:, t, c], xn[:, t, c], ALU.add)
                if j % 2:
                    ins.then_inc(sem("h_done"), 1)

        hidT = bview(0, 4, S)
        silu_g = bview(1, 2, S)

        def swiglu_order(steps):
            gate = [max(3 * s - 1, 0) for s in range(steps)]
            down = [3 * s + 4 if s < steps - 1 else 3 * steps - 1 for s in range(steps)]
            return gate, down

        def ffn_tensor(pe, past, base, steps, acts):
            gate, down = swiglu_order(steps)

            def down_product(s):
                unit_ready(pe, base + down[s])
                pe.wait_ge(sem("ffn_hidden"), 2 * (past + s) + 2)
                product_rows(base + down[s], hidT[:, 2 * (s % 2):2 * (s % 2) + 2, :], s == 0, s == steps - 1)\
                    .then_inc(sem("unit_used"), 1)

            for s in range(steps):
                for which in range(2):
                    n = base + gate[s] + which
                    unit_ready(pe, n)
                    for j in range(2):
                        if s and not which:
                            pe.wait_ge(sem("ffn_hidden"), 2 * (past + s) - 1 + j)
                        last = product_T(n, j, bank[2 * which + j][:, 0:S], acts)
                        if j == 0:
                            last.then_inc(sem("ffn_up" if which else "ffn_gate"), 1)
                    last.then_inc(sem("unit_used"), 1)
                if s:
                    down_product(s - 1)
            down_product(steps - 1)

        def ffn_marks(base, steps):
            gate, _ = swiglu_order(steps)
            return [base + g for g in gate]

        def ffn_scalar(act, past, base, steps):
            gate = ffn_marks(base, steps)
            for s in range(steps):
                for j in range(2):
                    if j == 0:
                        act.wait_ge(sem("ffn_gate"), past + s + 1)
                    else:
                        act.wait_ge(sem("unit_used"), gate[s] + 1)
                    if s:
                        act.wait_ge(sem("ffn_hidden"), 2 * (past + s) + j - 1)
                    ACTV(silu_g[:, j, :], bank[j][:, 0:S], ACT.Silu).then_inc(sem("ffn_silu"), 1)

        def ffn_vector(dve, past, base, steps):
            gate, down = swiglu_order(steps)
            for s in range(steps):
                for j in range(2):
                    dve.wait_ge(sem("ffn_silu"), 2 * (past + s) + j + 1)
                    if j == 0:
                        dve.wait_ge(sem("ffn_up"), past + s + 1)
                    else:
                        dve.wait_ge(sem("unit_used"), base + gate[s] + 2)
                    if s >= 2:
                        dve.wait_ge(sem("unit_used"), base + down[s - 2] + 1)
                    V.tensor_tensor(hidT[:, 2 * (s % 2) + j, :], silu_g[:, j, :], bank[2 + j][:, 0:S], ALU.mult)\
                        .then_inc(sem("ffn_hidden"), 1)

        def ffn_done(eng, base, steps):
            eng.wait_ge(sem("unit_used"), base + 3 * steps)

        sc_sb = bview(9, 2, 1024)
        pr_sb = sc_sb
        pT_sb = bview(11, 2, 1024)
        mxs, nmx, esum, sink_e, rden = tin(2), tin(2), tin(2), tin(2), tin(2)

        def att_tensor(pe, past, units, before):
            before(pe)

            def scores(u):
                if u >= 2:
                    pe.wait_ge(sem("att_masked"), past + u - 1)
                for off, w, lhsT, rhs in units[u]["score"]:
                    last = MM(bank[2 * (u % 2) + off // 512][:, off % 512:off % 512 + w], lhsT, rhs,
                              start=True, stop=True)
                last.then_inc(sem("att_scores"), 1)

            scores(0)
            for u, unit in enumerate(units):
                if u + 1 < len(units):
                    scores(u + 1)
                pe.wait_ge(sem("att_probs"), past + u + 1)
                if u:
                    pe.wait_ge(sem("att_copied"), past + u)
                for b in range(len(unit["values"])):
                    last = nc.tensor.transpose(bank[4 + b // 4][:, (b % 4) * P:(b % 4 + 1) * P],
                                               pr_sb[:, u % 2, unit["block"](b):unit["block"](b) + P], ident)
                last.then_inc(sem("att_T"), 1)
                pe.wait_ge(sem("att_copied"), past + u + 1)
                if u >= 2:
                    pe.wait_ge(sem("att_out"), past + u - 1)
                lo, n = unit["rows"]
                for b, v in enumerate(unit["values"]):
                    last = MM(bank[6 + u % 2][lo:lo + n, 0:P], v, pT_sb[:, u % 2, b * P:(b + 1) * P],
                              start=(b == 0), stop=(b == len(unit["values"]) - 1))
                last.then_inc(sem("att_values"), 1)

        def att_scalar(act, past, units):
            for u, unit in enumerate(units):
                i = u % 2
                act.wait_ge(sem("att_max"), past + u + 1)
                for off, w in unit["spans"]:
                    last = ACTV(pr_sb[:, i, off:off + w], sc_sb[:, i, off:off + w], ACT.Exp, bias=nmx[:, i:i + 1],
                                accum_out=esum[:, i:i + 1])
                if unit["sink"] is not None:
                    last = ACTV(sink_e[:, i:i + 1], unit["sink"], ACT.Exp, bias=nmx[:, i:i + 1])
                last.then_inc(sem("att_exp"), 1)
                act.wait_ge(sem("att_T"), past + u + 1)
                if u >= 2:
                    act.wait_ge(sem("att_values"), past + u - 1)
                nb = len(unit["values"])
                for b in range(0, nb, 4):
                    w = min(4, nb - b) * P
                    last = ACTV(pT_sb[:, i, b * P:b * P + w], bank[4 + b // 4][:, 0:w], ACT.Copy)
                last.then_inc(sem("att_copied"), 1)

        def att_vector(dve, ch, past, units):
            def result(u):
                dve.wait_ge(sem("att_values"), past + u + 1)
                lo, n = units[u]["rows"]
                V.tensor_copy(units[u]["out"], bank[6 + u % 2][lo:lo + n, 0:P]).then_inc(sem("att_out"), 1)

            for u, unit in enumerate(units):
                i = u % 2
                dve.wait_ge(sem("att_scores"), past + u + 1)
                if u >= 2:
                    dve.wait_ge(sem("att_T"), past + u - 1)
                for off, w, mask, slope in unit["mask"]:
                    src = bank[2 * (u % 2) + off // 512][:, off % 512:off % 512 + w]
                    if mask is None:
                        last = V.tensor_copy(sc_sb[:, i, off:off + w], src)
                    else:
                        last = V.scalar_tensor_tensor(sc_sb[:, i, off:off + w], mask, slope, src, ALU.mult, ALU.add)
                last.then_inc(sem("att_masked"), 1)
                dve.wait_ge(sem("att_masked"), past + u + 1)
                (off, w), = unit["spans"]
                if unit["sink"] is None:
                    V.tensor_reduce(nmx[:, i:i + 1], sc_sb[:, i, off:off + w], AX.X, ALU.max, negate=True)\
                        .then_inc(sem("att_max"), 1)
                else:
                    ch.step(V.tensor_reduce(mxs[:, i:i + 1], sc_sb[:, i, off:off + w], AX.X, ALU.max))
                    V.tensor_scalar(nmx[:, i:i + 1], mxs[:, i:i + 1], unit["sink"], -1.0, ALU.max, ALU.mult)\
                        .then_inc(sem("att_max"), 1)
                if u:
                    result(u - 1)
                dve.wait_ge(sem("att_exp"), past + u + 1)
                den = esum[:, i:i + 1]
                if unit["sink"] is not None:
                    ch.step(V.tensor_tensor(esum[:, i:i + 1], esum[:, i:i + 1], sink_e[:, i:i + 1], ALU.add))
                ch.step(V.reciprocal(rden[:, i:i + 1], den))
                V.tensor_scalar(pr_sb[:, i, off:off + w], pr_sb[:, i, off:off + w], rden[:, i:i + 1], None, ALU.mult)\
                    .then_inc(sem("att_probs"), 1)
            result(len(units) - 1)

        def softplus_buffers(n):
            return [tin(n) for _ in range(5)]

        def softplus_vector_a(ch, tag, x, b):
            V.scalar_tensor_tensor(b[0], x, -1.0, x, ALU.mult, ALU.min).then_inc(sem(tag + "_arg"), 1)

        def softplus_scalar(act, tag, b):
            act.wait_ge(sem(tag + "_arg"), 1)
            ACTV(b[1], b[0], ACT.Exp).then_inc(sem(tag + "_z"), 1)
            act.wait_ge(sem(tag + "_w"), 1)
            ACTV(b[3], b[2], ACT.Ln).then_inc(sem(tag + "_ln"), 1)

        def softplus_vector_b(dve, ch, tag, x, b, out):
            dve.wait_ge(sem(tag + "_z"), 1)
            V.tensor_scalar(b[2], b[1], 1.0, None, ALU.add).then_inc(sem(tag + "_w"), 1)
            dve.wait_ge(sem(tag + "_w"), 1)
            dve.wait_ge(sem(tag + "_ln"), 1)
            ch.step(V.tensor_tensor(b[3], b[3], b[1], ALU.mult))
            ch.step(V.tensor_scalar(b[4], b[2], -1.0, None, ALU.add))
            ch.step(V.tensor_scalar(b[2], b[4], 0.0, None, ALU.is_equal))
            ch.step(V.tensor_tensor(b[4], b[4], b[2], ALU.add))
            ch.step(V.reciprocal(b[4], b[4]))
            ch.step(V.tensor_tensor(b[3], b[3], b[4], ALU.mult))
            ch.step(V.tensor_tensor(b[2], b[2], b[1], ALU.mult))
            ch.step(V.tensor_tensor(b[3], b[3], b[2], ALU.add))
            ch.step(V.scalar_tensor_tensor(out, x, 0.0, b[3], ALU.max, ALU.add))

        xcT = bview(0, 4, S)
        gelT = bview(0, 4, S, off=1024)
        lru_r = bview(1, 4, S)
        lru_i = bview(1, 4, S, off=1024)
        lru_a = bview(2, 4, S)
        lru_t = bview(2, 4, S, off=1024)
        qkv = bview(3, NT, 768)
        qT0 = bview(4, 4, S)
        kT0 = bview(4, S, off=1024)
        rope_a = bview(5, NT, 640)
        rope_b = bview(6, NT, 640)
        mixT = bview(7, KD, S)
        lam_s = tin(4)
        lam_b = softplus_buffers(4)
        neg_s, pos_s = tin(4), tin(4)
        qk_ssq, qk_var, qk_rstd = tin(20), tin(20), tin(20)

        def flat(a):
            return a.rearrange("p a b -> p (a b)")

        def mix0_tensor(pe):
            base = AT["mix0_in"]
            norm_ready(pe, 0)
            for i in range(8):
                n = base + i // 2
                unit_ready(pe, n)
                if i >= 4:
                    pe.wait_ge(sem("conv0_done"), i - 3)
                last = product_T(n, i % 2, bank[i % 4][:, 0:S], xnT)
                if i % 2:
                    last.then_inc(sem("unit_used"), 1)
                else:
                    last.then_inc(sem("mix0_even"), 1)
            for i in range(6):
                n = base + 4 + i // 2
                unit_ready(pe, n)
                if i >= 4:
                    pe.wait_ge(sem("qkv_copied"), i - 3)
                last = product(n, i % 2, bank[4 + i % 4][:, 0:256], xnT)
                if i % 2:
                    last.then_inc(sem("unit_used"), 1)
                else:
                    last.then_inc(sem("qkv_even"), 1)
            pe.wait_ge(sem("conv0_done"), 4)
            for c in range(4):
                pe.wait_ge(sem("gelu_done"), c + 1)
                MM(bank[c][:, 0:S], const("lru_wa", 4, P)[:, c, :], xcT[:, c, :], start=True, stop=True)
                MM(bank[c][:, S:2 * S], const("lru_wi", 4, P)[:, c, :], xcT[:, c, :], start=True, stop=True)\
                    .then_inc(sem("lru_gates"), 1)
            pe.wait_ge(sem("rope_done"), 1)
            for t in range(NT):
                for c in range(4):
                    nc.tensor.transpose(bank[4 + t][:, c * P:(c + 1) * P], qkv[:, t, c * P:(c + 1) * P], ident)
                last = nc.tensor.transpose(bank[6][:, t * P:(t + 1) * P], qkv[:, t, 512:640], ident)
            last.then_inc(sem("qk_T"), 1)

        def att0_units():
            units = []
            for t in range(NT):
                for s in range(ATT_SLOTS):
                    c, lo = s // 2, (s % 2) * 64
                    w = (t + 1) * P
                    units.append(dict(
                        score=[(0, w, qT0[lo:lo + 64, c, t * P:(t + 1) * P], kT0[lo:lo + 64, 0:w])],
                        mask=[(0, w, const("band")[:, 2 * P - w:2 * P], 1.0)], spans=[(0, w)],
                        block=lambda b: b * P, sink=const("sinks")[:, s:s + 1],
                        values=[qkv[:, b, 640 + lo:640 + lo + 64] for b in range(t + 1)],
                        rows=(lo, 64), out=mixT[lo:lo + 64, 4 + c, t * P:(t + 1) * P]))
            return units

        att0 = att0_units()

        def att0_before(pe):
            pe.wait_ge(sem("qT0_done"), 1)
            pe.wait_ge(sem("lru_gates_read"), 8)

        def mix0_scalar(act):
            base = AT["mix0_in"]
            for c in range(4):
                if c % 2:
                    act.wait_ge(sem("unit_used"), base + 2 + c // 2 + 1)
                else:
                    act.wait_ge(sem("mix0_even"), 2 + c // 2 + 1)
                ACTV(gelT[:, c, :], bank[c][:, 0:S], ACT.Gelu_apprx_tanh).then_inc(sem("gelu_done"), 1)
            for i in range(6):
                if i % 2:
                    act.wait_ge(sem("unit_used"), base + 4 + i // 2 + 1)
                else:
                    act.wait_ge(sem("qkv_even"), i // 2 + 1)
                ACTV(qkv[:, i % 2, (i // 2) * 256:(i // 2 + 1) * 256], bank[4 + i % 4][:, 0:256], ACT.Copy)\
                    .then_inc(sem("qkv_copied"), 1)
            for c in range(4):
                act.wait_ge(sem("lru_gates"), c + 1)
                ACTV(lru_r[:, c, :], bank[c][:, 0:S], ACT.Sigmoid, bias=const("lru_ba")[:, c:c + 1])\
                    .then_inc(sem("lru_gates_read"), 1)
                ACTV(lru_i[:, c, :], bank[c][:, S:2 * S], ACT.Sigmoid, bias=const("lru_bi")[:, c:c + 1])\
                    .then_inc(sem("lru_gates_read"), 1)
            act.wait_ge(sem("lru_gates_read"), 8)
            act.wait_ge(sem("lam_done"), 1)
            for c in range(4):
                ACTV(lru_a[:, c, :], lru_r[:, c, :], ACT.Exp, scale=neg_s[:, c:c + 1])
                ACTV(lru_t[:, c, :], lru_r[:, c, :], ACT.Tanh, scale=pos_s[:, c:c + 1]).then_inc(sem("lru_at"), 1)
            act.wait_ge(sem("qk_T"), 1)
            ACTV(flat(qT0)[:, :].rearrange("p (c t q) -> p c t q", c=4, t=NT)[:, :, 0, :],
                 bank[4][:, :].rearrange("p (c q) -> p c q", c=4), ACT.Copy, scale=64 ** -0.5)
            ACTV(flat(qT0)[:, :].rearrange("p (c t q) -> p c t q", c=4, t=NT)[:, :, 1, :],
                 bank[5][:, :].rearrange("p (c q) -> p c q", c=4), ACT.Copy, scale=64 ** -0.5)
            ACTV(kT0, bank[6][:, 0:S], ACT.Copy).then_inc(sem("qT0_done"), 1)
            act.wait_ge(sem("lru_m"), 1)
            ACTV(flat(lru_t), flat(lru_t), ACT.Sqrt).then_inc(sem("lru_root"), 1)

        def conv(dve, ch, dst, src, taps, bias, width=S):
            if bias is None:
                ch.step(V.tensor_scalar(dst, src, taps[:, 3:4], None, ALU.mult))
            else:
                ch.step(V.tensor_scalar(dst, src, taps[:, 3:4], bias, ALU.mult, ALU.add))
            for j in (2, 1, 0):
                d = 3 - j
                ins = V.scalar_tensor_tensor(dst[:, d:width], src[:, 0:width - d], taps[:, j:j + 1],
                                             dst[:, d:width], ALU.mult, ALU.add)
                if j:
                    ch.step(ins)
            return ins

        def mix0_vector(dve, ch):
            base = AT["mix0_in"]
            for c in range(4):
                if c % 2:
                    dve.wait_ge(sem("unit_used"), base + c // 2 + 1)
                else:
                    dve.wait_ge(sem("mix0_even"), c // 2 + 1)
                conv(dve, ch, xcT[:, c, :], bank[c][:, 0:S], const("lru_w", 4, CONV)[:, c, :],
                     const("lru_b")[:, c:c + 1]).then_inc(sem("conv0_done"), 1)
            dve.wait_ge(sem("qkv_copied"), 6)
            qk = qkv[:, :, 0:640]
            ch.step(V.tensor_tensor(rope_a, qk, qk, ALU.mult))
            ch.step(V.tensor_reduce(qk_ssq, flat(rope_a).rearrange("p (h d) -> p h d", d=64), AX.X, ALU.add))
            V.tensor_scalar(qk_var, qk_ssq, 1.0 / 64, EPS, ALU.mult, ALU.add).then_inc(sem("qk_var"), 1)
            dve.wait_ge(sem("qk_rstd"), 1)
            for t in range(NT):
                heads = qkv[:, t, 0:640].rearrange("p (h d) -> p h d", d=64)
                ch.step(V.tensor_tensor(heads, heads, over_heads(qk_rstd[:, 10 * t:10 * t + 10], 10, 64), ALU.mult))
                ch.add(V.tensor_tensor(heads[:, 0:8, :], heads[:, 0:8, :], per_head(const("q_norm"), 8, 64), ALU.mult))
                ch.step(V.tensor_tensor(heads[:, 8:10, :], heads[:, 8:10, :], per_head(const("k_norm"), 2, 64),
                                        ALU.mult))
                x1, x2 = heads[:, :, 0:32], heads[:, :, 32:64]
                ta = rope_a[:, t, :].rearrange("p (h d) -> p h d", d=64)
                tb = rope_b[:, t, :].rearrange("p (h d) -> p h d", d=64)
                cos = per_head(const("cos", NT, 32)[:, t, :], 10, 32)
                sin = per_head(const("sin", NT, 32)[:, t, :], 10, 32)
                ch.add(V.tensor_tensor(ta[:, :, 0:32], x1, cos, ALU.mult))
                ch.add(V.tensor_tensor(tb[:, :, 0:32], x2, sin, ALU.mult))
                ch.add(V.tensor_tensor(ta[:, :, 32:64], x2, cos, ALU.mult))
                ch.step(V.tensor_tensor(tb[:, :, 32:64], x1, sin, ALU.mult))
                ch.add(V.tensor_tensor(x1, ta[:, :, 0:32], tb[:, :, 0:32], ALU.subtract))
                ins = V.tensor_tensor(x2, ta[:, :, 32:64], tb[:, :, 32:64], ALU.add)
                if t == NT - 1:
                    ins.then_inc(sem("rope_done"), 1)
                else:
                    ch.add(ins)
            ch.sync()

        def mix0_vector_lru(dve, ch):
            dve.wait_ge(sem("lru_at"), 4)
            gx = flat(lru_i)
            ch.add(V.tensor_tensor(gx, gx, flat(xcT), ALU.mult))
            ch.step(V.tensor_tensor(flat(lru_r), flat(lru_a), flat(lru_a), ALU.mult))
            V.scalar_tensor_tensor(flat(lru_t), flat(lru_r), 1.0, flat(lru_t), ALU.add, ALU.mult)\
                .then_inc(sem("lru_m"), 1)
            dve.wait_ge(sem("lru_root"), 1)
            ch.step(V.tensor_tensor(gx, gx, flat(lru_t), ALU.mult))
            for c in range(4):
                ch.add(V.tensor_tensor_scan(lru_r[:, c, :], lru_a[:, c, :], lru_i[:, c, :], 0.0, ALU.mult, ALU.add))
            ch.sync()
            V.tensor_tensor(mixT[:, 0:4, :], lru_r, gelT, ALU.mult).then_inc(sem("lru_y"), 1)

        def out_tensor(pe, base, tag, ready, acts):
            ready(pe)
            for r in range(4):
                unit_ready(pe, base + r)
                last = product_rows(base + r, acts[:, 2 * r:2 * r + 2, :], r == 0, r == 3)
                last.then_inc(sem("unit_used"), 1)

        def rows_done(eng, base):
            eng.wait_ge(sem("unit_used"), base + 4)

        def add_product(dve, base_end):
            dve.wait_ge(sem("unit_used"), base_end)
            for t in range(NT):
                for c in range(2):
                    last = V.tensor_tensor(h[:, t, c * 512:(c + 1) * 512], h[:, t, c * 512:(c + 1) * 512],
                                           bank[4 + 2 * t + c][:, :], ALU.add)
                    if c:
                        last.then_inc(sem("h_done"), 1)

        NP = NT * GH
        LEVELS = 6
        g_q, g_k, g_v = bview(0, GH, S), bview(1, GH, S), bview(2, GH, S)
        g_gate = bview(3, NP, P)
        g_rows = bview(4, NP, P)
        g_qdT = g_rows
        g_eG = bview(5, NP, P)
        g_A = bview(6, NP, P)
        g_aT = bview(7, NP, P)
        g_T = bview(8, NP, P)
        g_TT = bview(9, NP, P)
        g_sq = [bview(8, GH, S), bview(9, GH, S)]
        g_norm = [bview(10, GH, S), bview(11, GH, S)]
        g_kb, g_kd = bview(10, NP, P), bview(11, NP, P)
        g_vb = flat(xn).rearrange("p (a b) -> p a b", b=P)
        g_YT = bview(0, NP, P)
        g_Ak = [bview(2, NP, P), bview(1, NP, P)]
        g_WT = bview(2, NP, P)
        g_U = bview(8, NP, P)
        g_S = xn[:, 0, :].rearrange("p (a b) -> p a b", b=P)
        g_osq = bview(9, NP, P)
        g_y = bview(10, NP, P)
        conv_out = [silu_c for silu_c in (small_conv[:, i * S:(i + 1) * S] for i in range(4))]
        ab = tin(NT, 16)
        sp_x, sp_out, g_g, g_beta, g_bk = tin(NP), tin(NP), tin(NP), tin(NP), tin(NP)
        sp_b = softplus_buffers(NP)
        ea = tin(GH)
        g_arg, g_exp = tin(2 * NP), tin(2 * NP)
        o_ssq, o_rstd = tin(NP), tin(NP)

        def psum4(i):
            return bank[i][:, :].rearrange("p (a b) -> p a b", b=P)

        def gdn_in_tensor(pe):
            base = AT["gdn_in"]
            norm_ready(pe, 2)
            for t in range(NT):
                for k in range(KD):
                    last = MM(bank[6][:, 16 * t:16 * t + 16], xnT[:, k, t * P:(t + 1) * P],
                              const("w_ab", KD, 16)[:, k, :], start=(k == 0), stop=(k == KD - 1))
            last.then_inc(sem("ab_done"), 1)
            for i in range(24):
                n = base + i // 2
                unit_ready(pe, n)
                if i >= 4:
                    pe.wait_ge(sem("gdn_conv"), i - 3)
                last = product_T(n, i % 2, bank[i % 4][:, 0:S], xnT)
                last.then_inc(sem("unit_used" if i % 2 else "gdn_even"), 1)
            for i in range(8):
                n = base + 12 + i // 2
                unit_ready(pe, n)
                if i >= 2:
                    pe.wait_ge(sem("gate_copied"), i - 1)
                last = product(n, i % 2, bank[4 + i % 2][:, 0:256], xnT)
                last.then_inc(sem("unit_used" if i % 2 else "gate_even"), 1)

        def gdn_in_wait(eng, i, base, even):
            if i % 2:
                eng.wait_ge(sem("unit_used"), base + i // 2 + 1)
            else:
                eng.wait_ge(sem(even), i // 2 + 1)

        def gdn_in_scalar(act):
            softplus_scalar(act, "dt", sp_b)
            ACTV(ea, const("a_log"), ACT.Exp).then_inc(sem("gdn_ea"), 1)
            act.wait_ge(sem("ab_copied"), 1)
            ACTV(g_beta.rearrange("p (t e) -> p t e", t=NT), ab[:, :, 8:16], ACT.Sigmoid).then_inc(sem("beta_done"), 1)
            for i in range(24):
                act.wait_ge(sem("gdn_conv"), i + 1)
                dst = (g_q, g_k, g_v)[i // 8][:, i % 8, :]
                ACTV(dst, conv_out[i % 4], ACT.Silu).then_inc(sem("gdn_silu"), 1)
            for i in range(8):
                gdn_in_wait(act, i, AT["gdn_in"] + 12, "gate_even")
                c = i // 2
                ACTV(g_gate[:, 8 * (i % 2) + 2 * c:8 * (i % 2) + 2 * c + 2, :],
                     bank[4 + i % 2][:, 0:256].rearrange("p (a b) -> p a b", b=P), ACT.Silu)\
                    .then_inc(sem("gate_copied"), 1)

        def gdn_in_vector(dve, ch):
            dve.wait_ge(sem("ab_done"), 1)
            V.tensor_copy(ab, bank[6][:, 0:32].rearrange("p (t e) -> p t e", t=NT)).then_inc(sem("ab_copied"), 1)
            dve.wait_ge(sem("ab_copied"), 1)
            ch.step(V.tensor_tensor(sp_x.rearrange("p (t e) -> p t e", t=NT), ab[:, :, 0:8],
                                    per_head(const("dt_bias"), NT, GH), ALU.add))
            softplus_vector_a(ch, "dt", sp_x, sp_b)
            softplus_vector_b(dve, ch, "dt", sp_x, sp_b, sp_out)
            dve.wait_ge(sem("gdn_ea"), 1)
            ch.step(V.scalar_tensor_tensor(g_g.rearrange("p (t e) -> p t e", t=NT),
                                           sp_out.rearrange("p (t e) -> p t e", t=NT), -1.0,
                                           per_head(ea, NT, GH), ALU.mult, ALU.mult))
            V.tensor_copy(g_rows, over_heads(g_g, NP, P)).then_inc(sem("g_done"), 1)
            for i in range(24):
                gdn_in_wait(dve, i, AT["gdn_in"], "gdn_even")
                if i >= 4:
                    dve.wait_ge(sem("gdn_silu"), i - 3)
                conv(dve, ch, conv_out[i % 4], bank[i % 4][:, 0:S], const("gdn_conv", 24, CONV)[:, i, :], None)\
                    .then_inc(sem("gdn_conv"), 1)

        def gdn_square(pool):
            for i, src in enumerate((g_q, g_k)):
                pool.wait_ge(sem("gdn_silu"), 8 * (i + 1))
                G.tensor_tensor(flat(g_sq[i]), flat(src), flat(src), ALU.mult).then_inc(sem("gdn_sq"), 1)

        def gdn_core_tensor(pe):
            pe.wait_ge(sem("g_done"), 1)
            for t in range(NT):
                MM(bank[6][:, 64 + 8 * t:72 + 8 * t], const("cum"), g_g[:, 8 * t:8 * t + 8], start=True, stop=True)
                last = MM(bank[6][:, 80 + 8 * t:88 + 8 * t], const("same"), g_g[:, 8 * t:8 * t + 8],
                          start=True, stop=True)
            last.then_inc(sem("gcol"), 1)
            for i in range(NP):
                if i == 0:
                    pe.wait_ge(sem("gdn_conv"), 24)
                last = MM(bank[i // 4][:, (i % 4) * P:(i % 4 + 1) * P], g_rows[:, i, :], const("cum"),
                          start=True, stop=True)
                if i % 4 == 3:
                    last.then_inc(sem("grow"), 1)
            pe.wait_ge(sem("gate_copied"), 8)
            pe.wait_ge(sem("gcol_copied"), 1)
            for i in range(2):
                pe.wait_ge(sem("gdn_sq"), i + 1)
                for c in range(4):
                    if i:
                        pe.wait_ge(sem("gdn_root"), c + 1)
                    MM(bank[4 + c][:, :], const("ones"), flat(g_sq[i])[:, c * 512:(c + 1) * 512],
                       start=True, stop=True).then_inc(sem("gdn_sums"), 1)
            pe.wait_ge(sem("grow_read"), 2)
            pe.wait_ge(sem("qk_normed"), 2)
            for i in range(NP):
                t, e = i // GH, i % GH
                kt = g_k[:, e, t * P:(t + 1) * P]
                last = MM(bank[i // 4][:, (i % 4) * P:(i % 4 + 1) * P], kt, kt, start=True, stop=True)
                if i % 4 == 3:
                    last.then_inc(sem("gdn_kk"), 1)
            for i in range(NP):
                t, e = i // GH, i % GH
                last = MM(bank[4 + i // 4][:, (i % 4) * P:(i % 4 + 1) * P], g_k[:, e, t * P:(t + 1) * P],
                          g_q[:, e, t * P:(t + 1) * P], start=True, stop=True)
                if i % 4 == 3:
                    last.then_inc(sem("gdn_qk"), 1)
            for j, src in enumerate((g_k, g_v)):
                for i in range(NP):
                    t, e = i // GH, i % GH
                    if i % 4 == 0:
                        pe.wait_ge(sem("gdn_aT" if j else "gdn_A"), i // 4 + 1)
                    last = nc.tensor.transpose(bank[4 * j + i // 4][:, (i % 4) * P:(i % 4 + 1) * P],
                                               src[:, e, t * P:(t + 1) * P], ident)
                    if i % 4 == 3:
                        last.then_inc(sem("gdn_kvT"), 1)
            pe.wait_ge(sem("gdn_level"), 1)
            for i in range(NP):
                if i % 4 == 0:
                    pe.wait_ge(sem("gdn_kv"), i // 4 + 1)
                last = nc.tensor.transpose(bank[i // 4][:, (i % 4) * P:(i % 4 + 1) * P], g_Ak[0][:, i, :], ident)
                if i % 4 == 3:
                    last.then_inc(sem("gdn_A0T"), 1)
            pe.wait_ge(sem("gdn_kv"), 8)
            for k in range(1, LEVELS):
                pe.wait_ge(sem("gdn_level"), k + 1)
                for t in range(NT):
                    pe.wait_ge(sem("gdn_T"), NT * (k - 1) + t + 1)
                    for e in range(GH):
                        i = GH * t + e
                        last = MM(bank[i // 4][:, (i % 4) * P:(i % 4 + 1) * P], g_Ak[k % 2][:, i, :], g_TT[:, i, :],
                                  start=True, stop=True)
                    last.then_inc(sem("gdn_YT"), 1)
                for t in range(NT):
                    pe.wait_ge(sem("gdn_YT_copied"), NT * (k - 1) + t + 1)
                    if t or k > 1:
                        pe.wait_ge(sem("gdn_T"), NT * k + t)
                    for e in range(GH):
                        i, o = GH * t + e, slice((e % 4) * P, (e % 4 + 1) * P)
                        if k < LEVELS - 1:
                            MM(bank[4 + e // 4][:, o], g_YT[:, i, :], g_T[:, i, :], start=True, stop=True)
                        last = MM(bank[6 + e // 4][:, o], g_T[:, i, :], g_YT[:, i, :], start=True, stop=True)
                    last.then_inc(sem("gdn_Z"), 1)
            pe.wait_ge(sem("gdn_T"), NT * LEVELS)
            for i in range(NP):
                last = MM(bank[i // 4][:, (i % 4) * P:(i % 4 + 1) * P], g_kb[:, i, :], g_TT[:, i, :],
                          start=True, stop=True)
            last.then_inc(sem("gdn_WT"), 1)
            for i in range(NP):
                last = MM(bank[4 + i // 4][:, (i % 4) * P:(i % 4 + 1) * P], g_TT[:, i, :], g_vb[:, i, :],
                          start=True, stop=True)
            last.then_inc(sem("gdn_U"), 1)
            pe.wait_ge(sem("gdn_WT_copied"), 1)
            for c in range(4):
                t, r = c // 2, slice(CHUNK * (c % 2), CHUNK * (c % 2) + CHUNK)
                if c:
                    pe.wait_ge(sem("gdn_S"), c)
                    for e in range(GH):
                        last = MM(bank[e // 4][r, (e % 4) * P:(e % 4 + 1) * P], g_WT[:, GH * t + e, r], g_S[:, e, :],
                                  start=True, stop=True)
                    last.then_inc(sem("gdn_WS"), 1)
                pe.wait_ge(sem("gdn_vn"), c + 1)
                if c < 3:
                    for e in range(GH):
                        last = MM(bank[6 + e // 4][:, (e % 4) * P:(e % 4 + 1) * P], g_kd[r, GH * t + e, :],
                                  g_U[r, GH * t + e, :], start=True, stop=True)
                    last.then_inc(sem("gdn_kv_state"), 1)
                for e in range(GH):
                    i = GH * t + e
                    dst = bank[2 + 2 * t + e // 4][r, (e % 4) * P:(e % 4 + 1) * P]
                    if c:
                        MM(dst, g_qdT[:, i, r], g_S[:, e, :], start=True, stop=False)
                    last = MM(dst, g_aT[r, i, r], g_U[r, i, :], start=(c == 0), stop=True)
                last.then_inc(sem("gdn_O"), 1)
            for t in range(NT):
                pe.wait_ge(sem("gdn_y"), t + 1)
                for e in range(GH):
                    last = nc.tensor.transpose(bank[(0, 1, 6, 7)[e // 2]][:, (e % 2) * S + t * P:(e % 2) * S + t * P + P],
                                               g_y[:, GH * t + e, :], ident)
            last.then_inc(sem("gdn_yT"), 1)

        def gdn_core_scalar(act):
            act.wait_ge(sem("gcol_copied"), 1)
            ACTV(g_exp, g_arg, ACT.Exp).then_inc(sem("gdn_exp"), 1)
            for i in range(4):
                act.wait_ge(sem("grow"), i + 1)
                ACTV(g_eG[:, 4 * i:4 * i + 4, :], psum4(i), ACT.Exp).then_inc(sem("eG_done"), 1)
            act.wait_ge(sem("grow_read"), 1)
            ACTV(flat(g_A), flat(g_A), ACT.Exp, scale=-1.0)
            act.wait_ge(sem("grow_read"), 2)
            ACTV(flat(g_aT), flat(g_aT), ACT.Exp).then_inc(sem("decay_done"), 1)
            for i in range(2):
                for c in range(4):
                    act.wait_ge(sem("gdn_sums"), 4 * i + c + 1)
                    ACTV(flat(g_norm[i])[:, c * 512:(c + 1) * 512], bank[4 + c][:, :], ACT.Sqrt, bias=eps_col)\
                        .then_inc(sem("gdn_root"), 1)
            for k in range(1, LEVELS):
                for t in range(NT):
                    act.wait_ge(sem("gdn_YT"), NT * (k - 1) + t + 1)
                    for j in range(2):
                        last = ACTV(g_YT[:, GH * t + 4 * j:GH * t + 4 * j + 4, :], psum4(2 * t + j), ACT.Copy)
                    last.then_inc(sem("gdn_YT_copied"), 1)
            act.wait_ge(sem("gdn_WT"), 1)
            for j in range(4):
                last = ACTV(g_WT[:, 4 * j:4 * j + 4, :], psum4(j), ACT.Copy)
            last.then_inc(sem("gdn_WT_copied"), 1)
            for t in range(NT):
                act.wait_ge(sem("gdn_O"), 2 * t + 2)
                for j in range(2):
                    last = ACTV(g_osq[:, GH * t + 4 * j:GH * t + 4 * j + 4, :], psum4(2 + 2 * t + j), ACT.Square)
                last.then_inc(sem("gdn_osq"), 1)
            act.wait_ge(sem("gdn_yT"), 1)
            for j in range(2):
                ACTV(mixT[:, 2 * j:2 * j + 2, :], bank[j][:, :].rearrange("p (a b) -> p a b", b=S), ACT.Copy)\
                    .then_inc(sem("gdn_mixT"), 1)

        def gdn_core_vector(dve, ch):
            dve.wait_ge(sem("gcol"), 1)
            ch.step(V.tensor_copy(g_arg, bank[6][:, 64:96]))
            V.tensor_tensor(g_arg[:, NP:2 * NP], g_arg[:, NP:2 * NP], g_arg[:, 0:NP], ALU.subtract)\
                .then_inc(sem("gcol_copied"), 1)
            dve.wait_ge(sem("gcol_copied"), 1)
            for j, (dst, name) in enumerate(((g_A, "low"), (g_aT, "up"))):
                for i in range(NP):
                    dve.wait_ge(sem("eG_done"), i // 4 + 1)
                    last = V.scalar_tensor_tensor(dst[:, i, :], psum4(i // 4)[:, i % 4, :], g_arg[:, i:i + 1],
                                                  const(name), ALU.subtract, ALU.add)
                last.then_inc(sem("grow_read"), 1)
            dve.wait_ge(sem("gdn_exp"), 1)
            dve.wait_ge(sem("beta_done"), 1)
            ch.step(V.tensor_tensor(g_bk, g_beta, g_exp[:, 0:NP], ALU.mult))
            for i, src in enumerate((g_q, g_k)):
                dve.wait_ge(sem("gdn_root"), 4 * (i + 1))
                ch.step(V.reciprocal(flat(g_norm[i]), flat(g_norm[i])))
                V.scalar_tensor_tensor(flat(src), flat(src), 1.0 if i else P ** -0.5, flat(g_norm[i]),
                                       ALU.mult, ALU.mult).then_inc(sem("qk_normed"), 1)
            dve.wait_ge(sem("decay_done"), 1)
            for i in range(NP):
                dve.wait_ge(sem("gdn_kk"), i // 4 + 1)
                last = V.scalar_tensor_tensor(g_A[:, i, :], psum4(i // 4)[:, i % 4, :], g_beta[:, i:i + 1],
                                              g_A[:, i, :], ALU.mult, ALU.mult)
                if i % 4 == 3:
                    last.then_inc(sem("gdn_A"), 1)
            dve.wait_ge(sem("gdn_A"), 4)
            for j in range(4):
                dve.wait_ge(sem("gdn_qk"), j + 1)
                V.tensor_tensor(g_aT[:, 4 * j:4 * j + 4, :], psum4(4 + j), g_aT[:, 4 * j:4 * j + 4, :], ALU.mult)\
                    .then_inc(sem("gdn_aT"), 1)
            for j in range(4):
                dve.wait_ge(sem("gdn_kvT"), j + 1)
                V.tensor_tensor(g_kb[:, 4 * j:4 * j + 4, :], psum4(j), over_heads(g_bk[:, 4 * j:4 * j + 4], 4, P),
                                ALU.mult)
                V.tensor_tensor(g_kd[:, 4 * j:4 * j + 4, :], psum4(j),
                                over_heads(g_exp[:, NP + 4 * j:NP + 4 * j + 4], 4, P), ALU.mult)\
                    .then_inc(sem("gdn_kv"), 1)
            for j in range(4):
                dve.wait_ge(sem("gdn_kvT"), 4 + j + 1)
                V.tensor_tensor(g_vb[:, 4 * j:4 * j + 4, :], psum4(4 + j), over_heads(g_beta[:, 4 * j:4 * j + 4], 4, P),
                                ALU.mult).then_inc(sem("gdn_kv"), 1)
            for t in range(NT):
                if t == 0:
                    dve.wait_ge(sem("gdn_level"), 1)
                sl = slice(GH * t, GH * t + GH)
                ch.add(V.scalar_tensor_tensor(g_T[:, sl, :], g_Ak[0][:, sl, :], -1.0, per_head(ident, GH, P),
                                              ALU.mult, ALU.add))
                dve.wait_ge(sem("gdn_A0T"), 2 * t + 2)
                for j in range(2):
                    b = 2 * t + j
                    last = V.scalar_tensor_tensor(g_TT[:, 4 * b:4 * b + 4, :], psum4(b), -1.0, per_head(ident, 4, P),
                                                  ALU.mult, ALU.add)
                last.then_inc(sem("gdn_T"), 1)
            for k in range(1, LEVELS):
                for t in range(NT):
                    dve.wait_ge(sem("gdn_Z"), NT * (k - 1) + t + 1)
                    dve.wait_ge(sem("gdn_T"), NT * k)
                    for j in range(2):
                        sl = slice(GH * t + 4 * j, GH * t + 4 * j + 4)
                        if k < LEVELS - 1:
                            V.tensor_tensor(g_T[:, sl, :], g_T[:, sl, :], psum4(4 + j), ALU.subtract)
                        last = V.tensor_tensor(g_TT[:, sl, :], g_TT[:, sl, :], psum4(6 + j), ALU.subtract)
                    last.then_inc(sem("gdn_T"), 1)
            dve.wait_ge(sem("gdn_U"), 1)
            for j in range(4):
                last = V.tensor_copy(g_U[:, 4 * j:4 * j + 4, :], psum4(4 + j))
            last.then_inc(sem("gdn_vn"), 1)
            for c in range(4):
                t, r = c // 2, slice(CHUNK * (c % 2), CHUNK * (c % 2) + CHUNK)
                if c:
                    dve.wait_ge(sem("gdn_WS"), c)
                    for j in range(2):
                        sl = slice(GH * t + 4 * j, GH * t + 4 * j + 4)
                        last = V.tensor_tensor(g_U[r, sl, :], g_U[r, sl, :], psum4(j)[r, :, :], ALU.subtract)
                    last.then_inc(sem("gdn_vn"), 1)
                if c < 3:
                    dve.wait_ge(sem("gdn_kv_state"), c + 1)
                    if c == 0:
                        for j in range(2):
                            last = V.tensor_copy(g_S[:, 4 * j:4 * j + 4, :], psum4(6 + j))
                    else:
                        dve.wait_ge(sem("gdn_O"), c + 1)
                        for e in range(GH):
                            i = GH * t + e
                            end = CHUNK * (c % 2) + CHUNK - 1
                            last = V.scalar_tensor_tensor(g_S[:, e, :], g_S[:, e, :], g_eG[:, i, end:end + 1],
                                                          psum4(6 + e // 4)[:, e % 4, :], ALU.mult, ALU.add)
                    last.then_inc(sem("gdn_S"), 1)
                    dve.wait_ge(sem("gdn_S"), c + 1)
            for t in range(NT):
                sl = slice(GH * t, GH * t + GH)
                dve.wait_ge(sem("gdn_osq"), t + 1)
                ch.step(V.tensor_reduce(o_ssq[:, sl], g_osq[:, sl, :], AX.X, ALU.add))
                V.tensor_scalar(o_ssq[:, sl], o_ssq[:, sl], 1.0 / P, EPS, ALU.mult, ALU.add)\
                    .then_inc(sem("gdn_ovar"), 1)
                dve.wait_ge(sem("gdn_orstd"), t + 1)
                for j in range(2):
                    s4 = slice(GH * t + 4 * j, GH * t + 4 * j + 4)
                    ch.add(V.tensor_tensor(g_y[:, s4, :], psum4(2 + 2 * t + j), over_heads(o_rstd[:, s4], 4, P),
                                           ALU.mult))
                ch.sync()
                ch.step(V.tensor_tensor(g_y[:, sl, :], g_y[:, sl, :], per_head(const("out_norm"), GH, P), ALU.mult))
                V.tensor_tensor(g_y[:, sl, :], g_y[:, sl, :], g_gate[:, sl, :], ALU.mult).then_inc(sem("gdn_y"), 1)
            dve.wait_ge(sem("gdn_yT"), 1)
            for j in range(2):
                V.tensor_copy(mixT[:, 4 + 2 * j:6 + 2 * j, :], bank[6 + j][:, :].rearrange("p (a b) -> p a b", b=S))\
                    .then_inc(sem("gdn_mixT"), 1)

        def gdn_core_pool(pool):
            pool.wait_ge(sem("qk_normed"), 1)
            pool.wait_ge(sem("eG_done"), 4)
            for t in range(NT):
                G.tensor_tensor(g_qdT[:, GH * t:GH * t + GH, :], g_q[:, :, t * P:(t + 1) * P],
                                g_eG[:, GH * t:GH * t + GH, :], ALU.mult).then_inc(sem("gdn_qd"), 1)
            pool.wait_ge(sem("gdn_A"), 4)
            for k in range(LEVELS):
                if k < 2:
                    pool.wait_ge(sem("gdn_kvT"), 8)
                else:
                    pool.wait_ge(sem("gdn_Z"), NT * (k - 2) + 0 if k == 2 else NT * (k - 2))
                if k == 2:
                    pool.wait_ge(sem("gdn_A0T"), 4)
                    pool.wait_ge(sem("gdn_T"), NT)
                G.tensor_tensor(g_Ak[k % 2], g_A, per_head(const("level", 6, P)[:, k, :], NP, P), ALU.mult)\
                    .then_inc(sem("gdn_level"), 1)
            for t in range(NT):
                pool.wait_ge(sem("gdn_ovar"), t + 1)
                G.tensor_tensor(o_rstd[:, GH * t:GH * t + GH], o_ssq[:, GH * t:GH * t + GH], minus_half, ALU.pow)\
                    .then_inc(sem("gdn_orstd"), 1)

        logits, top8, m_ge, m_gt = tin(NT, 8), tin(NT, 8), tin(NT, 8), tin(NT, 8)
        m_eq, m_cum, gates, n_gt = tin(NT, 8), tin(NT, 8), tin(NT, 8), tin(NT, 4)

        def router_tensor(pe):
            norm_ready(pe, 3)
            for t in range(NT):
                for k in range(KD):
                    last = MM(bank[0][:, 8 * t:8 * t + 8], xnT[:, k, t * P:(t + 1) * P],
                              const("router", KD, EXPERTS)[:, k, :], start=(k == 0), stop=(k == KD - 1))
            last.then_inc(sem("logits"), 1)

        def router_scalar(act):
            act.wait_ge(sem("top_diff"), 1)
            ACTV(gates, gates, ACT.Exp).then_inc(sem("top_exp"), 1)

        def router_vector(dve, ch):
            dve.wait_ge(sem("logits"), 1)
            ch.step(V.tensor_copy(logits, bank[0][:, 0:16].rearrange("p (t e) -> p t e", t=NT)))
            for t in range(NT):
                ch.add(V.max(top8[:, t, :], logits[:, t, :]))
            ch.sync()
            for t in range(NT):
                l, v1, v2 = logits[:, t, :], top8[:, t, 0:1], top8[:, t, 1:2]
                ch.add(V.tensor_scalar(gates[:, t, :], l, v1, None, ALU.subtract))
                ch.add(V.tensor_scalar(m_gt[:, t, :], l, v2, None, ALU.is_gt))
                ch.add(V.tensor_scalar(m_eq[:, t, :], l, v2, None, ALU.is_equal))
            ch.sync()
            V.tensor_copy(m_ge[:, :, 0:1], m_eq[:, :, 0:1]).then_inc(sem("top_diff"), 1)
            dve.wait_ge(sem("top_diff"), 1)
            for t in range(NT):
                ch.add(V.tensor_reduce(n_gt[:, t, 0:1], m_gt[:, t, :], AX.X, ALU.add))
                ch.add(V.tensor_tensor_scan(m_cum[:, t, :], const("ones")[:, 0:8], m_eq[:, t, :], 0.0,
                                            ALU.mult, ALU.add))
            ch.sync()
            for t in range(NT):
                ch.add(V.tensor_scalar(m_ge[:, t, :], m_cum[:, t, :], n_gt[:, t, 0:1], 2.0, ALU.add, ALU.is_le))
            ch.sync()
            ch.step(V.tensor_tensor(m_eq, m_eq, m_ge, ALU.mult))
            ch.step(V.tensor_tensor(m_eq, m_eq, m_gt, ALU.add))
            dve.wait_ge(sem("top_exp"), 1)
            ch.step(V.tensor_tensor(gates, gates, m_eq, ALU.mult))
            for t in range(NT):
                ch.add(V.tensor_reduce(n_gt[:, t, 1:2], gates[:, t, :], AX.X, ALU.add))
            ch.sync()
            ch.step(V.reciprocal(n_gt[:, :, 1:2], n_gt[:, :, 1:2]))
            for t in range(NT):
                last = V.tensor_scalar(gates[:, t, :], gates[:, t, :], n_gt[:, t, 1:2], None, ALU.mult)
            last.then_inc(sem("moe_added"), 1)
            dve.wait_ge(sem("moe_added"), 1)

        def unit_ready_in(pe, base, e, i):
            n = base + i
            pe.wait_ge(sem(f"unit_in{n % RING}"), e * (16 * FFE_UNITS // RING) + 16 * (n // RING + 1))

        def moe_tensor(pe):
            base, steps, past = AT["moe"], FFE_STEPS, PAST["moe"]
            gate, down = swiglu_order(steps)
            pe.wait_ge(sem("top_diff"), 1)
            with pe.Fori(0, EXPERTS) as e:
                def down_product(s):
                    unit_ready_in(pe, base, e, down[s])
                    pe.wait_ge(sem("ffn_hidden"), e * (2 * steps) + (2 * (past + s) + 2))
                    if s == 0:
                        pe.wait_ge(sem("moe_added"), e + 1)
                    product_rows(base + down[s], hidT[:, 2 * (s % 2):2 * (s % 2) + 2, :], s == 0, s == steps - 1)\
                        .then_inc(sem("unit_used"), 1)

                for s in range(steps):
                    for which in range(2):
                        unit_ready_in(pe, base, e, gate[s] + which)
                        for j in range(2):
                            if s and not which:
                                pe.wait_ge(sem("ffn_hidden"), e * (2 * steps) + (2 * (past + s) - 1 + j))
                            last = product_T(base + gate[s] + which, j, bank[2 * which + j][:, 0:S], xnT)
                            if j == 0:
                                last.then_inc(sem("ffn_up" if which else "ffn_gate"), 1)
                        last.then_inc(sem("unit_used"), 1)
                    if s:
                        down_product(s - 1)
                down_product(steps - 1)

        def moe_scalar(act):
            base, steps, past = AT["moe"], FFE_STEPS, PAST["moe"]
            gate, _ = swiglu_order(steps)
            with act.Fori(0, EXPERTS) as e:
                for s in range(steps):
                    for j in range(2):
                        if j == 0:
                            act.wait_ge(sem("ffn_gate"), e * steps + (past + s + 1))
                        else:
                            act.wait_ge(sem("unit_used"), e * FFE_UNITS + (base + gate[s] + 1))
                        act.wait_ge(sem("ffn_hidden"), e * (2 * steps) + (2 * past + (2 * s + j - 1 if s else 0)))
                        ACTV(silu_g[:, j, :], bank[j][:, 0:S], ACT.Silu).then_inc(sem("ffn_silu"), 1)

        def moe_vector(dve, ch):
            base, steps, past = AT["moe"], FFE_STEPS, PAST["moe"]
            gate, down = swiglu_order(steps)
            with dve.Fori(0, EXPERTS) as e:
                for s in range(steps):
                    for j in range(2):
                        dve.wait_ge(sem("ffn_silu"), e * (2 * steps) + (2 * (past + s) + j + 1))
                        if j == 0:
                            dve.wait_ge(sem("ffn_up"), e * steps + (past + s + 1))
                        else:
                            dve.wait_ge(sem("unit_used"), e * FFE_UNITS + (base + gate[s] + 2))
                        if s >= 2:
                            dve.wait_ge(sem("unit_used"), e * FFE_UNITS + (base + down[s - 2] + 1))
                        V.tensor_tensor(hidT[:, 2 * (s % 2) + j, :], silu_g[:, j, :], bank[2 + j][:, 0:S], ALU.mult)\
                            .then_inc(sem("ffn_hidden"), 1)
                dve.wait_ge(sem("unit_used"), e * FFE_UNITS + (base + FFE_UNITS))
                for t in range(NT):
                    for c in range(2):
                        o = slice(c * 512, (c + 1) * 512)
                        last = V.scalar_tensor_tensor(h[:, t, o], bank[4 + 2 * t + c][:, :],
                                                      gates[:, t, bass.ds(e, 1)], h[:, t, o], ALU.mult, ALU.add)
                last.then_inc(sem("moe_added"), 1)
            dve.wait_ge(sem("moe_added"), EXPERTS + 1)
            V.tensor_copy(n_gt[:, :, 2:3], n_gt[:, :, 1:2]).then_inc(sem("h_done"), NT)

        mem_rows = bview(8, NT, D)
        memT = bview(7, KD, S)
        mem_kT = bview(3, MH, S)
        mem_v = bview(3, NT, 512, off=1024)
        hg_q, hg_k = bview(0, MH, S), bview(0, MH, S, off=1024)
        hg_qs, hg_b = bview(1, MH, S), bview(1, MH, S, off=1024)
        hg_ks, hg_kl = bview(2, MH, S), bview(2, MH, S, off=1024)
        hg_kl_rows, hg_scores = bview(4, 8, P), bview(4, 8, P, off=1024)
        hg_v, hg_gate = bview(5, NT, 512), bview(5, NT, 512, off=1024)
        hg_sq, hg_y = bview(2, 8, P), bview(2, 8, P, off=1024)
        hg_S = [buf[11][:, i * 512:(i + 1) * 512].rearrange("p (a b) -> p a b", b=P) for i in range(3)]
        xn_a = xn[:, 0, :].rearrange("p (a b) -> p a b", b=S)
        xn_b = xn[:, 1, :].rearrange("p (a b) -> p a b", b=S)
        dil_q = [bview(6, MH, S), bview(7, MH, S, off=1024), xn_a]
        dil_k = [bview(6, MH, S, off=1024), bview(8, MH, S), xn_b]
        dil_v = [bview(7, NT, 512), bview(8, NT, 512, off=1024), bview(10, NT, 512)]
        mem_q = bview(10, MH, S, off=1024)
        y_hgT, y_dilT, y_memT = bview(0, MH, S, off=1024), bview(4, MH, S), bview(5, MH, S)
        gl = [bview(6 + i, KD, S) for i in range(3)]
        mixed = bview(10, KD, S)
        mix_t = bview(11, 2, S)
        lb, one_lb, lg_d, lg_e = tin(MH), tin(MH), tin(2 * MH), tin(2 * MH)
        hg_ssq, hg_rstd = tin(8), tin(8)

        def product_any(n, kind, j, dst, acts):
            return product_T(n, j, dst, acts) if kind == "T" else product(n, j, dst, acts)

        def in_jobs(base, parts):
            jobs = []
            for kind, units in parts:
                for u in range(units):
                    for j in range(2):
                        jobs.append((base, kind, j))
                    base += 1
            return jobs

        def jobs_tensor(pe, tag, jobs, acts, banks):
            for i, (n, kind, j) in enumerate(jobs):
                unit_ready(pe, n)
                if i >= len(banks):
                    pe.wait_ge(sem(tag + "_read"), i - len(banks) + 1)
                last = product_any(n, kind, j, bank[banks[i % len(banks)]][:, 0:S], acts)
                last.then_inc(sem("unit_used" if j else tag + "_even"), 1)

        def jobs_scalar(act, tag, jobs, banks, first, outs):
            for i, (dst, func, scale, bias) in enumerate(outs, first):
                n, _, j = jobs[i]
                if j:
                    act.wait_ge(sem("unit_used"), n + 1)
                else:
                    act.wait_ge(sem(tag + "_even"), i // 2 + 1)
                src = bank[banks[i % len(banks)]][:, 0:S]
                if bias is None:
                    ins = ACTV(dst, src, func, scale=scale)
                else:
                    ins = ACTV(dst, src, func, scale=scale, bias=bias)
                ins.then_inc(sem(tag + "_read"), 1)

        def outs_T(dst, func=ACT.Copy, scale=1.0):
            return [(dst[:, c, :], func, scale, None) for c in range(MH)]

        def outs_rows(dst, func=ACT.Copy):
            return [(dst[:, t, u * 256:(u + 1) * 256], func, 1.0, None) for u in range(2) for t in range(NT)]

        kv_jobs = in_jobs(AT["mem_kv"], [("T", 2), ("rows", 2)])
        kv_outs = outs_T(mem_kT) + outs_rows(mem_v)
        hg_jobs = in_jobs(AT["hg_in"], [("T", 4), ("rows", 4)] + [("T", 4), ("rows", 2)] * DIL + [("T", 2)])
        hg_outs = outs_T(hg_q, ACT.Silu) + outs_T(hg_k, ACT.Sigmoid) + outs_rows(hg_v) + outs_rows(hg_gate, ACT.Sigmoid)
        dil_outs = []
        for g in range(DIL):
            dil_outs += outs_T(dil_q[g], scale=P ** -0.5) + outs_T(dil_k[g]) + outs_rows(dil_v[g])
        dil_outs += outs_T(mem_q, scale=P ** -0.5)
        gl_jobs = in_jobs(AT["gl_in"], [("T", 12)])
        gl_outs = [(gl[i // KD][:, i % KD, :], ACT.Sigmoid, 1.0, const("b_gate")[:, i:i + 1]) for i in range(24)]
        FOUR = (0, 1, 2, 3)

        def chunks(a):
            return flat(a).rearrange("p (a b) -> p a b", b=CHUNK)

        def hg_prepare(dve, ch):
            l = const("hg_logits")
            ch.step(V.tensor_tensor(lb, l[:, 0:MH], l[:, MH:2 * MH], ALU.max))
            ch.step(V.tensor_tensor(lg_d[:, 0:MH], l[:, 0:MH], lb, ALU.subtract))
            V.tensor_tensor(lg_d[:, MH:2 * MH], l[:, MH:2 * MH], lb, ALU.subtract).then_inc(sem("lb_arg"), 1)
            dve.wait_ge(sem("lb_exp"), 1)
            ch.step(V.tensor_tensor(one_lb, lg_e[:, 0:MH], lg_e[:, MH:2 * MH], ALU.add))
            ch.step(V.reciprocal(one_lb, one_lb))
            ch.step(V.tensor_tensor(lb, lg_e[:, 0:MH], one_lb, ALU.mult))
            ch.step(V.tensor_scalar(one_lb, lb, -1.0, 1.0, ALU.mult, ALU.add))

        def hg_prepare_scalar(act):
            act.wait_ge(sem("lb_arg"), 1)
            ACTV(lg_e, lg_d, ACT.Exp).then_inc(sem("lb_exp"), 1)

        def hg_decay_scalar(act):
            act.wait_ge(sem("hg_f"), 1)
            ACTV(flat(hg_qs), flat(hg_k), ACT.Ln).then_inc(sem("hg_ln"), 1)
            act.wait_ge(sem("hg_sums"), 1)
            ACTV(flat(hg_ks), flat(hg_qs), ACT.Exp, scale=-1.0).then_inc(sem("hg_exp"), 1)
            ACTV(flat(hg_kl), flat(hg_kl), ACT.Exp).then_inc(sem("hg_exp"), 1)
            act.wait_ge(sem("hg_exp"), 1)
            ACTV(flat(hg_qs), flat(hg_qs), ACT.Exp).then_inc(sem("hg_exp"), 1)
            ACTV(flat(hg_b), flat(hg_b), ACT.Exp).then_inc(sem("hg_exp"), 1)

        def hg_decay_vector(dve, ch):
            dve.wait_ge(sem("mix2_read"), 16)
            ch.add(V.memset(flat(hg_scores), 0.0))
            for c in range(MH):
                last = V.tensor_scalar(hg_k[:, c, :], hg_k[:, c, :], one_lb[:, c:c + 1], lb[:, c:c + 1],
                                       ALU.mult, ALU.add)
            last.then_inc(sem("hg_f"), 1)
            dve.wait_ge(sem("hg_ln"), 1)
            ch.add(V.tensor_scalar(flat(hg_k), flat(hg_k), -1.0, 1.0, ALU.mult, ALU.add))
            for c in range(MH):
                ch.add(V.tensor_tensor_scan(hg_b[:, c, :], const("reset"), hg_qs[:, c, :], 0.0, ALU.mult, ALU.add))
            ch.sync()
            b = chunks(hg_b)
            mid = b[:, :, CHUNK // 2 - 1:CHUNK // 2].broadcast_to([P, 16, CHUNK])
            end = b[:, :, CHUNK - 1:CHUNK].broadcast_to([P, 16, CHUNK])
            V.tensor_tensor(chunks(hg_qs), b, mid, ALU.subtract)
            V.tensor_tensor(chunks(hg_kl), end, b, ALU.subtract).then_inc(sem("hg_sums"), 1)
            dve.wait_ge(sem("hg_exp"), 1)
            ch.add(V.tensor_tensor(flat(hg_ks), flat(hg_ks), flat(hg_k), ALU.mult))
            dve.wait_ge(sem("hg_exp"), 2)
            ch.add(V.tensor_tensor(flat(hg_kl), flat(hg_kl), flat(hg_k), ALU.mult))
            dve.wait_ge(sem("hg_exp"), 3)
            ch.add(V.tensor_tensor(flat(hg_qs), flat(hg_qs), flat(hg_q), ALU.mult))
            dve.wait_ge(sem("hg_exp"), 4)
            ch.sync()
            V.tensor_tensor(flat(hg_q), flat(hg_q), flat(hg_b), ALU.mult).then_inc(sem("hg_factors"), 1)

        def hg_tensor(pe):
            pe.wait_ge(sem("hg_factors"), 1)
            pe.wait_ge(sem("mix2_read"), len(hg_jobs))
            for i in range(8):
                t, e = i // MH, i % MH
                last = nc.tensor.transpose(bank[i // 4][:, e * P:(e + 1) * P], hg_kl[:, e, t * P:(t + 1) * P], ident)
            last.then_inc(sem("hg_klT"), 1)
            for i in range(8):
                t, e = i // MH, i % MH
                last = MM(bank[2 + i // 4][:, e * P:(e + 1) * P], hg_ks[:, e, t * P:(t + 1) * P],
                          hg_qs[:, e, t * P:(t + 1) * P], start=True, stop=True)
            last.then_inc(sem("hg_ST"), 1)
            pe.wait_ge(sem("hg_kl_rows"), 1)
            for c in range(3):
                t, r = c // 2, slice(CHUNK * (c % 2), CHUNK * (c % 2) + CHUNK)
                for e in range(MH):
                    last = MM(bank[4 + c][:, e * P:(e + 1) * P], hg_kl_rows[r, MH * t + e, :],
                              hg_v[r, t, e * P:(e + 1) * P], start=True, stop=True)
            last.then_inc(sem("hg_kv"), 1)
            pe.wait_ge(sem("hg_masked"), 1)
            pe.wait_ge(sem("hg_states"), 1)
            for i in range(8):
                t, e = i // MH, i % MH
                dst = bank[t][:, e * P:(e + 1) * P]
                MM(dst, hg_scores[:, i, :], hg_v[:, t, e * P:(e + 1) * P], start=True, stop=True)
                for c in (2 * t, 2 * t + 1):
                    if c:
                        r = slice(CHUNK * (c % 2), CHUNK * (c % 2) + CHUNK)
                        last = MM(bank[t][r, e * P:(e + 1) * P],
                                  hg_q[:, e, c * CHUNK:(c + 1) * CHUNK], hg_S[c - 1][:, e, :],
                                  start=False, stop=True, skip_group_check=True)
            last.then_inc(sem("hg_o"), 1)
            pe.wait_ge(sem("hg_y"), 1)
            for i in range(8):
                t, e = i // MH, i % MH
                last = nc.tensor.transpose(bank[2 + e // 2][:, (e % 2) * S + t * P:(e % 2) * S + (t + 1) * P],
                                           hg_y[:, i, :], ident)
            last.then_inc(sem("hg_yT"), 1)

        def hg_scalar(act):
            act.wait_ge(sem("hg_o"), 1)
            for t in range(NT):
                last = ACTV(hg_sq[:, MH * t:MH * t + MH, :], psum4(t), ACT.Square)
            last.then_inc(sem("hg_osq"), 1)

        def hg_vector(dve, ch):
            dve.wait_ge(sem("hg_klT"), 1)
            for j in range(2):
                last = V.tensor_copy(hg_kl_rows[:, 4 * j:4 * j + 4, :], psum4(j))
            last.then_inc(sem("hg_kl_rows"), 1)
            dve.wait_ge(sem("hg_ST"), 1)
            mask = per_head(const("cum").bitcast(U32), 4, P)
            for j in range(2):
                last = V.copy_predicated(hg_scores[:, 4 * j:4 * j + 4, :], mask, psum4(2 + j))
            last.then_inc(sem("hg_masked"), 1)
            dve.wait_ge(sem("hg_kv"), 1)
            ch.step(V.tensor_copy(hg_S[0], psum4(4)))
            for c in (1, 2):
                for e in range(MH):
                    end = (c + 1) * CHUNK - 1
                    last = V.scalar_tensor_tensor(hg_S[c][:, e, :], hg_S[c - 1][:, e, :], hg_b[:, e, end:end + 1],
                                                  psum4(4 + c)[:, e, :], ALU.mult, ALU.add)
                    if c == 1:
                        ch.add(last)
                ch.sync()
            last.then_inc(sem("hg_states"), 1)
            dve.wait_ge(sem("hg_osq"), 1)
            ch.step(V.tensor_reduce(hg_ssq, hg_sq, AX.X, ALU.add))
            V.tensor_scalar(hg_ssq, hg_ssq, 1.0 / P, EPS, ALU.mult, ALU.add).then_inc(sem("hg_var"), 1)
            dve.wait_ge(sem("hg_rstd"), 1)
            for t in range(NT):
                ch.add(V.tensor_tensor(hg_y[:, MH * t:MH * t + MH, :], psum4(t),
                                       over_heads(hg_rstd[:, MH * t:MH * t + MH], MH, P), ALU.mult))
            ch.sync()
            ch.step(V.tensor_tensor(hg_y, hg_y, per_head(const("hg_norm"), 8, P), ALU.mult))
            V.tensor_tensor(hg_y, hg_y, flat(hg_gate).rearrange("p (a b) -> p a b", b=P), ALU.mult)\
                .then_inc(sem("hg_y"), 1)
            dve.wait_ge(sem("hg_yT"), 1)
            for j in range(2):
                V.tensor_copy(y_hgT[:, 2 * j:2 * j + 2, :], bank[2 + j][:, :].rearrange("p (a b) -> p a b", b=S))\
                    .then_inc(sem("hg_out"), 1)

        def hg_pool(pool):
            pool.wait_ge(sem("hg_var"), 1)
            G.tensor_tensor(hg_rstd, hg_ssq, minus_half, ALU.pow).then_inc(sem("hg_rstd"), 1)

        def att2_units():
            units = []
            for t in range(NT):
                w = (t + 1) * P
                q = slice(t * P, (t + 1) * P)
                for e in range(MH):
                    units.append(dict(
                        score=[(g * w, w, dil_q[g][:, e, q], dil_k[g][:, e, 0:w]) for g in range(DIL)],
                        mask=[(g * w, w, const("dist", DIL, 2 * P)[:, g, 2 * P - w:2 * P], SLOPES[MH * g + e])
                              for g in range(DIL)],
                        spans=[(0, DIL * w)], block=lambda b: b * P, sink=None,
                        values=[dil_v[g][:, b, e * P:(e + 1) * P] for g in range(DIL) for b in range(t + 1)],
                        rows=(0, P), out=y_dilT[:, e, q]))
                    units.append(dict(
                        score=[(0, S, mem_q[:, e, q], mem_kT[:, e, :])], mask=[(0, S, None, None)],
                        spans=[(0, S)], block=lambda b: b * P, sink=None,
                        values=[mem_v[:, b, e * P:(e + 1) * P] for b in range(2)],
                        rows=(0, P), out=y_memT[:, e, q]))
            return units

        att2 = att2_units()

        def att2_before(pe):
            pe.wait_ge(sem("hg_out"), 2)

        def branch_tensor(pe):
            pe.wait_ge(sem("att_out"), len(att0) + len(att2))
            for i in range(24):
                b, d = i // KD, i % KD
                n = AT["branch"] + i // 4
                unit_ready(pe, n)
                w = ring[n % RING][:, :].rearrange("p (k c) -> p k c", k=4)
                if i >= 4:
                    pe.wait_ge(sem("branch_read"), i - 3)
                else:
                    pe.wait_ge(sem("gl_read"), 24)
                acts = (y_hgT, y_dilT, y_memT)[b]
                for k in range(4):
                    last = MM(bank[i % 4][:, 0:S], w[:, k, (i % 4) * P:(i % 4 + 1) * P], acts[:, k, :],
                              start=(k == 0), stop=(k == 3))
                last.then_inc(sem("unit_used" if i % 4 == 3 else "branch_done"), 1)

        def branch_vector(dve, ch):
            dve.wait_ge(sem("gl_read"), 24)
            for i in range(24):
                b, d = i // KD, i % KD
                if i % 4 == 3:
                    dve.wait_ge(sem("unit_used"), AT["branch"] + i // 4 + 1)
                else:
                    dve.wait_ge(sem("branch_done"), 3 * (i // 4) + i % 4 + 1)
                if b == 0:
                    V.tensor_tensor(mixed[:, d, :], gl[b][:, d, :], bank[i % 4][:, 0:S], ALU.mult)\
                        .then_inc(sem("branch_read"), 1)
                else:
                    ins = V.tensor_tensor(mix_t[:, i % 2, :], gl[b][:, d, :], bank[i % 4][:, 0:S], ALU.mult)
                    ins.then_inc(sem("branch_read"), 1)
                    dve.wait_ge(sem("branch_read"), i + 1)
                    ins = V.tensor_tensor(mixed[:, d, :], mixed[:, d, :], mix_t[:, i % 2, :], ALU.add)
                    if b == 2:
                        ins.then_inc(sem("mixed_done"), 1)
                    else:
                        ch.add(ins)
                if i % KD == KD - 1:
                    ch.sync()

        def load_post(act, i):
            act.dma_start(post_gain, post_d[i, :, :]).then_inc(sem("post_in"), 16)

        block = ctx.enter_context(nc.Block())

        @block.sync
        def _(sp):
            sp.dma_start(small[:, :], small_d).then_inc(sem("small_in"), 16)
            sp.dma_start(h[:, :, :], x_d.rearrange("(t p) d -> p t d", p=P)).then_inc(sem("x_in"), 16)
            for s in range(RING):
                sp.dma_start(ring[s][:, :], w_d[s, :, :]).then_inc(sem(f"unit_in{s}"), 16)
            last_unit = {1: AT["ffn0"], 2: AT["gdn_in"], 3: AT["moe"], 4: AT["ffn1"], 5: AT["mem_kv"], 6: AT["ffn2"]}.get(upto, UNITS)
            whole = max(last_unit // RING, 2)
            with sp.Fori(1, whole) as g:
                for s in range(RING):
                    sp.wait_ge(sem("unit_used"), g * RING + (s + 1 - RING))
                    sp.dma_start(ring[s][:, :], w_d[g * RING + s, :, :]).then_inc(sem(f"unit_in{s}"), 16)
            for n in range(whole * RING, last_unit):
                sp.wait_ge(sem("unit_used"), n - RING + 1)
                sp.dma_start(ring[n % RING][:, :], w_d[n, :, :]).then_inc(sem(f"unit_in{n % RING}"), 16)
            h_ready(sp, min(upto, 7))
            sp.dma_start(out_d.rearrange("(t p) d -> p t d", p=P), h[:, :, :]).then_inc(sem("out_written"), 16)
            sp.wait_ge(sem("out_written"), 16)

        @block.tensor
        def _(pe):
            pe.wait_ge(sem("small_in"), 16)
            norm_transpose(pe, 0)
            mix0_tensor(pe)
            att_tensor(pe, 0, att0, att0_before)

            def mix0_ready(pe):
                pe.wait_ge(sem("att_out"), len(att0))
                pe.wait_ge(sem("lru_y"), 1)
            out_tensor(pe, AT["mix0_out"], "mix0", mix0_ready, mixT)
            if upto > 1:
                norm_transpose(pe, 1)
                norm_ready(pe, 1)
                ffn_tensor(pe, PAST["ffn0"], AT["ffn0"], FF_STEPS, xnT)
            if upto > 2:
                norm_transpose(pe, 2)
                gdn_in_tensor(pe)
                gdn_core_tensor(pe)
                out_tensor(pe, AT["gdn_out"], "gdn", lambda pe: pe.wait_ge(sem("gdn_mixT"), 4), mixT)
            if upto > 3:
                norm_transpose(pe, 3)
                router_tensor(pe)
                moe_tensor(pe)
            if upto > 4:
                norm_transpose(pe, 4)
                norm_transpose(pe, 5)
                norm_ready(pe, 5)
                ffn_tensor(pe, PAST["ffn1"], AT["ffn1"], FF_STEPS, xnT)
            if upto > 5:
                jobs_tensor(pe, "mem_kv", kv_jobs, memT, FOUR)
                norm_transpose(pe, 6)
                norm_ready(pe, 6)
                jobs_tensor(pe, "mix2", hg_jobs, xnT, FOUR)
                hg_tensor(pe)
                att_tensor(pe, len(att0), att2, att2_before)
                pe.wait_ge(sem("att_out"), len(att0) + len(att2))
                jobs_tensor(pe, "gl", gl_jobs, xnT, FOUR)
                branch_tensor(pe)
                out_tensor(pe, AT["mix2_out"], "mix2", lambda pe: pe.wait_ge(sem("mixed_done"), KD), mixed)
            if upto > 6:
                norm_transpose(pe, 7)
                norm_ready(pe, 7)
                ffn_tensor(pe, PAST["ffn2"], AT["ffn2"], FF_STEPS, xnT)

        @block.scalar
        def _(act):
            act.wait_ge(sem("small_in"), 16)
            softplus_scalar(act, "lam", lam_b)
            h_ready(act, 0)
            norm_square(act, 0, h, 0, xnT)
            norm_out_act(act, 0, 0, xnT)
            mix0_scalar(act)
            att_scalar(act, 0, att0)
            if upto > 1:
                h_ready(act, 1)
                norm_square(act, 1, h, 1, xnT)
                norm_out_act(act, 1, 1, xnT)
                ffn_scalar(act, PAST["ffn0"], AT["ffn0"], FF_STEPS)
            if upto > 2:
                h_ready(act, 2)
                norm_square(act, 2, h, 2, xnT)
                norm_out_act(act, 2, 2, xnT)
                gdn_in_scalar(act)
                gdn_core_scalar(act)
            if upto > 3:
                h_ready(act, 3)
                act.dma_start(mem_rows, mem_d.rearrange("(t p) d -> p t d", p=P)).then_inc(sem("mem_in"), 16)
                load_post(act, 0)
                norm_square(act, 3, h, 3, xnT)
                norm_out_act(act, 3, 3, xnT)
                router_scalar(act)
                moe_scalar(act)
            if upto > 4:
                act.wait_ge(sem("mem_in"), 16)
                norm_square(act, 4, mem_rows, 7, memT)
                norm_out_act(act, 4, 7, memT)
                h_ready(act, 4)
                norm_square(act, 5, h, 4, xnT)
                norm_out_act(act, 5, 4, xnT)
                ffn_scalar(act, PAST["ffn1"], AT["ffn1"], FF_STEPS)
                post_square(act, 0, AT["mem_kv"])
            if upto > 5:
                hg_prepare_scalar(act)
                jobs_scalar(act, "mem_kv", kv_jobs, FOUR, 0, kv_outs)
                h_ready(act, 5)
                load_post(act, 1)
                norm_square(act, 6, h, 5, xnT)
                norm_out_act(act, 6, 5, xnT)
                jobs_scalar(act, "mix2", hg_jobs, FOUR, 0, hg_outs)
                hg_decay_scalar(act)
                jobs_scalar(act, "mix2", hg_jobs, FOUR, len(hg_outs), dil_outs)
                hg_scalar(act)
                att_scalar(act, len(att0), att2)
                act.wait_ge(sem("att_out"), len(att0) + len(att2))
                jobs_scalar(act, "gl", gl_jobs, FOUR, 0, gl_outs)
                post_square(act, 1, AT["ffn2"])
            if upto > 6:
                h_ready(act, 6)
                load_post(act, 2)
                norm_square(act, 7, h, 6, xnT)
                norm_out_act(act, 7, 6, xnT)
                ffn_scalar(act, PAST["ffn2"], AT["ffn2"], FF_STEPS)
                post_square(act, 2, AT["end"])

        @block.vector
        def _(dve):
            ch = Chain(dve, "dve_step")
            V.memset(eps_col, EPS)
            V.memset(minus_half, -0.5).then_inc(sem("half_set"), 1)
            dve.wait_ge(sem("small_in"), 16)
            softplus_vector_a(ch, "lam", const("lam"), lam_b)
            dve.wait_ge(sem("lam_z"), 1)
            neg_lam = lam_b[0]
            ch.step(V.tensor_scalar(neg_lam, const("lam"), -1.0, None, ALU.mult))
            softplus_vector_b(dve, ch, "lam", neg_lam, lam_b, lam_s)
            ch.step(V.tensor_scalar(neg_s, lam_s, -8.0, None, ALU.mult))
            V.tensor_scalar(pos_s, lam_s, 8.0, None, ALU.mult).then_inc(sem("lam_done"), 1)
            dve.wait_ge(sem("x_in"), 16)
            norm_scale(dve, 0, h)
            norm_out_dve(dve, 0, 0, xnT)
            mix0_vector(dve, ch)
            mix0_vector_lru(dve, ch)
            att_vector(dve, ch, 0, att0)
            add_product(dve, AT["mix0_out"] + 4)
            if upto > 1:
                dve.wait_ge(sem("h_done"), NT)
                norm_scale(dve, 1, h)
                norm_out_dve(dve, 1, 1, xnT)
                ffn_vector(dve, PAST["ffn0"], AT["ffn0"], FF_STEPS)
                add_product(dve, AT["gdn_in"])
            if upto > 2:
                dve.wait_ge(sem("h_done"), 2 * NT)
                norm_scale(dve, 2, h)
                norm_out_dve(dve, 2, 2, xnT)
                gdn_in_vector(dve, ch)
                gdn_core_vector(dve, ch)
                add_product(dve, AT["moe"])
            if upto > 3:
                dve.wait_ge(sem("h_done"), 3 * NT)
                norm_scale(dve, 3, h)
                norm_out_dve(dve, 3, 3, xnT)
                router_vector(dve, ch)
                moe_vector(dve, ch)
            if upto > 4:
                dve.wait_ge(sem("mem_in"), 16)
                norm_scale(dve, 4, mem_rows)
                norm_out_dve(dve, 4, 7, memT)
                dve.wait_ge(sem("h_done"), 4 * NT)
                norm_scale(dve, 5, h)
                norm_out_dve(dve, 5, 4, xnT)
                ffn_vector(dve, PAST["ffn1"], AT["ffn1"], FF_STEPS)
                post_add(dve, ch, 0, 0.5)
            if upto > 5:
                hg_prepare(dve, ch)
                dve.wait_ge(sem("h_done"), 5 * NT)
                norm_scale(dve, 6, h)
                norm_out_dve(dve, 6, 5, xnT)
                hg_decay_vector(dve, ch)
                hg_vector(dve, ch)
                att_vector(dve, ch, len(att0), att2)
                branch_vector(dve, ch)
                post_add(dve, ch, 1, 1.0)
            if upto > 6:
                dve.wait_ge(sem("h_done"), 6 * NT)
                norm_scale(dve, 7, h)
                norm_out_dve(dve, 7, 6, xnT)
                ffn_vector(dve, PAST["ffn2"], AT["ffn2"], FF_STEPS)
                post_add(dve, ch, 2, 0.5)

        @block.gpsimd
        def _(pool):
            pool.wait_ge(sem("half_set"), 1)
            norm_pow(pool, 0)
            pool.wait_ge(sem("qk_var"), 1)
            G.tensor_tensor(qk_rstd, qk_var, minus_half[:, 0:1].broadcast_to([P, 20]), ALU.pow)\
                .then_inc(sem("qk_rstd"), 1)
            if upto > 1:
                norm_pow(pool, 1)
            if upto > 2:
                norm_pow(pool, 2)
                gdn_square(pool)
                gdn_core_pool(pool)
            if upto > 3:
                norm_pow(pool, 3)
            if upto > 4:
                norm_pow(pool, 4)
                norm_pow(pool, 5)
                post_pow(pool, 0)
            if upto > 5:
                norm_pow(pool, 6)
                hg_pool(pool)
                post_pow(pool, 1)
            if upto > 6:
                norm_pow(pool, 7)
                post_pow(pool, 2)


def col(v):
    return v.reshape(-1, P).T


def row(v):
    return np.broadcast_to(v.reshape(1, -1), (P, v.size))


def rows_of(w):
    k, n = w.shape
    return w.reshape(k // P, P, n).transpose(1, 0, 2).reshape(P, -1)


def block_diagonal(w):
    out = np.zeros((4, P, P), w.dtype)
    out[:, 0:64, 0:64] = w[0::2]
    out[:, 64:128, 64:128] = w[1::2]
    return out.transpose(1, 0, 2).reshape(P, -1)


def shape_constants():
    f = np.float32
    i = np.arange(P)
    p, c = i[:, None], i[None, :]
    same = (p // CHUNK) == (c // CHUNK)
    level = [(((p >> k) & 1) == 1) & ((p >> k) == (c >> k) + 1) for k in range(6)]
    q2, k2 = P + p, np.arange(2 * P)[None, :]
    dist = q2 - k2
    steps = [(dist >= 0) & (dist <= 128), (dist >= 0) & (dist % 4 == 0), (dist >= 0) & (dist % 16 == 0)]
    inv = (f(10000.0) ** (-np.arange(32, dtype=f) / f(32))).astype(f)
    ang = np.arange(S, dtype=f)[:, None] * inv[None, :]
    return {
        "ident": np.eye(P), "cum": same & (p <= c), "same": same, "ones": np.ones((P, P)),
        "low": np.where(same & (p >= c), 0, BIG), "up": np.where(same & (p <= c), 0, -BIG),
        "level": np.concatenate(level, 1), "band": np.where((dist >= 0) & (dist < P), 0, -BIG),
        "dist": np.concatenate([np.where(m, -dist, -BIG) for m in steps], 1),
        "cos": rows_of(np.cos(ang)), "sin": rows_of(np.sin(ang)), "reset": row((np.arange(S) % CHUNK != 0) * 1.0),
    }


def pack_small(a):
    heads = [h for c in range(4) for h in (c, c + 4)]
    tiles = dict(shape_constants())
    tiles["gain"] = np.concatenate([col(v) for v in (
        a["ln_mix"][0], a["ln_ffn"][0], a["ln_mix"][1], a["ln_ffn"][1], a["ffn1_pre_w_2"][0], a["mix_pre_w_2"][0],
        a["ffn2_pre_w_2"][0], a["mem_norm_w_2"][0])], 1)
    tiles["lru_w"] = rows_of(np.ascontiguousarray(a["e_lru_conv_w"][0].T))
    tiles["lru_b"] = col(a["e_lru_conv_b"][0])
    tiles["lru_wa"] = block_diagonal(a["e_lru_w_a"][0])
    tiles["lru_wi"] = block_diagonal(a["e_lru_w_i"][0])
    tiles["lru_ba"], tiles["lru_bi"] = col(a["e_lru_b_a"][0]), col(a["e_lru_b_i"][0])
    tiles["lam"] = col(a["e_lru_lambda"][0])
    tiles["q_norm"], tiles["k_norm"] = row(a["e_q_norm"][0]), row(a["e_k_norm"][0])
    tiles["sinks"] = row(a["e_sinks"][0][heads])
    tiles["gdn_conv"] = rows_of(np.ascontiguousarray(a["o_conv_w"][0].T))
    tiles["w_ab"] = rows_of(a["o_w_in"][0][:, 4096:])
    tiles["a_log"], tiles["dt_bias"] = row(a["o_a_log"][0]), row(a["o_dt_bias"][0])
    tiles["out_norm"] = row(a["o_out_norm"][0])
    tiles["router"] = rows_of(a["o_router"][0])
    tiles["b_gate"] = col(a["b_gate_2"][0])
    tiles["hg_logits"] = np.concatenate([col(a["hg_lb_logits_2"][0]), col(a["hg_lb_logits_2"][1])], 1)
    tiles["hg_norm"] = row(a["hg_norm_w_2"][0])
    out = np.empty((P, SMALL), np.float32)
    for name, (o, width) in COLS.items():
        assert tiles[name].shape == (P, width), (name, tiles[name].shape, width)
        out[:, o:o + width] = tiles[name]
    return out


def pack_post(a):
    return np.stack([row(a[k][0]) for k in ("ffn1_post_w_2", "mix_post_w_2", "ffn2_post_w_2")])


def pack_weights(a):
    out = np.empty((UNITS, P, UNIT), np.float32)
    at = [0]

    def cols(w, perm=None):
        k, n = w.shape
        m = n // 256
        out[at[0]:at[0] + m].reshape(m, P, k // P, 256)[:] = w.reshape(k // P, P, m, 256).transpose(2, 1, 0, 3)
        at[0] += m

    def rows(w):
        k, n = w.shape
        m = k // 256
        out[at[0]:at[0] + m].reshape(m, P, 2, n)[:] = w.reshape(m, 2, P, n).transpose(0, 2, 1, 3)
        at[0] += m

    def half_cols(w):
        out[at[0]:at[0] + 2].reshape(2, P, 4, 512)[:] = w.reshape(4, P, 2, 512).transpose(2, 1, 0, 3)
        at[0] += 2

    def swiglu(gate, up, down):
        steps = down.shape[0] // 256
        for s in range(steps):
            cols(gate[:, s * 256:(s + 1) * 256])
            cols(up[:, s * 256:(s + 1) * 256])
            if s:
                rows(down[(s - 1) * 256:s * 256])
        rows(down[(steps - 1) * 256:])

    heads = [h for c in range(4) for h in (c, c + 4)]
    w = a["e_w_in"][0]
    q = w[:, 1024:1536].reshape(D, 8, 64)[:, heads].reshape(D, 512)
    cols(w[:, 0:1024])
    cols(q)
    cols(w[:, 1536:])
    w = a["e_w_out"][0]
    rows(w[0:512])
    rows(w[512:].reshape(8, 64, D)[heads].reshape(512, D))
    swiglu(a["e_ffn_w_gate"][0], a["e_ffn_w_up"][0], a["e_ffn_w_down"][0])
    assert at[0] == AT["gdn_in"]
    cols(a["o_w_in"][0][:, 0:4096])
    rows(a["o_w_out"][0])
    for e in range(EXPERTS):
        swiglu(a["o_moe_w_gate"][0, e], a["o_moe_w_up"][0, e], a["o_moe_w_down"][0, e])
    assert at[0] == AT["ffn1"]
    swiglu(a["ffn1_w_gu_2"][0][:, :FF], a["ffn1_w_gu_2"][0][:, FF:], a["ffn1_w_down_2"][0])
    cols(a["w_mem_kv_2"][0])
    cols(a["w_in_2"][0])
    assert at[0] == AT["branch"]
    for name in ("w_br_hg_2", "w_br_dil_2", "w_br_mem_2"):
        half_cols(a[name][0])
    rows(a["w_out_2"][0])
    swiglu(a["ffn2_w_gu_2"][0][:, :FF], a["ffn2_w_gu_2"][0][:, FF:], a["ffn2_w_down_2"][0])
    assert at[0] == UNITS
    return out


def kernel(**inputs):
    import concourse.bacc as bacc
    from concourse.bass_utils import run_bass_kernel_spmd

    a = {k: np.asarray(v) for k, v in inputs.items()}
    arrays = {"small": pack_small(a), "post": pack_post(a), "weights": pack_weights(a), "x": a["x"][0], "mem": a["mem_2"][0]}
    nc = bacc.Bacc("TRN2", target_bir_lowering=False, num_devices=1)
    args = [nc.dram_tensor(n, v.shape, F32, kind="ExternalInput").ap() for n, v in arrays.items()]
    out = nc.dram_tensor("out", (S, D), F32, kind="ExternalOutput").ap()
    build(nc, *args, out)
    r = run_bass_kernel_spmd(nc, [arrays], core_ids=[0])
    return r.results[0]["out"].reshape(1, S, D)
```

```python
import numpy as np
import concourse.bass as bass
from concourse import mybir
from contextlib import ExitStack

F32 = mybir.dt.float32
F32R = mybir.dt.float32r
U32 = mybir.dt.uint32
ALU = mybir.AluOpType
ACT = mybir.ActivationFunctionType
AX = mybir.AxisListType

P = 128
S = 256
NT = S // P
D = 1024
KD = D // P
EPS = 1e-6
CONV = 4
CHUNK = 64
BIG = 1e30
FF = 2816
FFE = 3584
EXPERTS = 8
GH = 8
ATT_SLOTS = 8
DIL = 3
MH = 4

UNIT = 2048
RING = 7
FF_STEPS = FF // 256
FFE_STEPS = FFE // 256
FF_UNITS = 3 * FF_STEPS
FFE_UNITS = 3 * FFE_STEPS
assert FFE_UNITS % RING == 0


def units_before():
    at, n = {}, 0
    for name, count in (("mix0_in", 7), ("mix0_out", 4), ("ffn0", FF_UNITS), ("gdn_in", 16), ("gdn_out", 4),
                        ("moe", EXPERTS * FFE_UNITS), ("ffn1", FF_UNITS), ("mem_kv", 4), ("hg_in", 8),
                        ("dil_in", 18), ("mq_in", 2), ("gl_in", 12), ("branch", 6), ("mix2_out", 4),
                        ("ffn2", FF_UNITS)):
        at[name] = n
        n += count
    at["end"] = n
    return at


AT = units_before()
PAST = {"ffn0": 0, "ffn1": FF_STEPS, "ffn2": 2 * FF_STEPS}
UNITS = AT["end"]
SPLITS = {"ffn0": 0, "moe": FF_UNITS, "ffn1": FF_UNITS + EXPERTS * FFE_UNITS,
          "ffn2": 2 * FF_UNITS + EXPERTS * FFE_UNITS}
HI_BUFS = (2, 6, 9, 10, 11, 1)
AHEAD = 3
assert FFE_UNITS % len(HI_BUFS) == 0


def small_layout():
    cols, n = {}, 0
    for name, width in (
            ("ident", P), ("cum", P), ("same", P), ("ones", P), ("before", P), ("iota", P), ("low", P), ("up", P), ("level", 6 * P),
            ("band", 2 * P), ("dist", DIL * 2 * P), ("cos", NT * 32), ("sin", NT * 32), ("reset", S),
            ("gain", 8 * KD), ("lru_w", 4 * CONV), ("lru_b", 4), ("lru_wa", 4 * P), ("lru_wi", 4 * P),
            ("lru_ba", 4), ("lru_bi", 4), ("lam", 4), ("q_norm", 64), ("k_norm", 64), ("sinks", ATT_SLOTS),
            ("gdn_conv", 24 * CONV), ("w_ab", KD * 16), ("a_log", GH), ("dt_bias", GH), ("out_norm", P),
            ("router", KD * EXPERTS), ("b_gate", 24), ("hg_logits", 2 * MH), ("hg_norm", P)):
        cols[name] = (n, width)
        n += width
    return cols, n


COLS, SMALL = small_layout()
SLOPES = [2.0 ** (-8.0 * (i + 1) / (DIL * MH)) for i in range(DIL * MH)]


def build(nc, small_d, post_d, w_d, x_d, mem_d, out_d, upto=99):
    ctx = ExitStack()
    with ctx:
        def sb(name, *shape):
            return ctx.enter_context(nc.sbuf_tensor(name, [P, *shape], F32))

        sems = {}

        def sem(name):
            if name not in sems:
                sems[name] = ctx.enter_context(nc.semaphore(name))
            return sems[name]

        def sb_twice(name, *shape):
            a = sb(name, *shape)
            at = nc.sbuf_base - 4 * int(np.prod(shape))
            return a, nc.alloc_sbuf_tensor_at(name + "_r", [P, *shape], F32R, offset=at)

        small = sb("small_sb", SMALL)
        ring, ring_r = zip(*[sb_twice(f"ring{i}", UNIT) for i in range(RING)])
        h = sb("h", NT, D)
        xnT, xnT_r = sb_twice("xnT", KD, S)
        xn = sb("xn", NT, D)
        buf, buf_r = zip(*[sb_twice(f"buf{i}", 2048) for i in range(12)])
        bank = [ctx.enter_context(nc.psum_tensor(f"bank{i}", [P, 512], F32)) for i in range(8)]
        tiny = sb("tiny", 1024)
        small_conv = sb("small_conv", 4 * S)
        crowded = ctx.enter_context(nc.sbuf_tensor("crowded", [P, 1], mybir.dt.int32))

        tiny_at = [0]

        def tin(*shape):
            n = int(np.prod(shape))
            a = tiny[:, tiny_at[0]:tiny_at[0] + n]
            tiny_at[0] += n
            assert tiny_at[0] <= 1024
            if len(shape) == 2:
                return a.rearrange("p (a b) -> p a b", b=shape[1])
            return a

        def const(name, *shape):
            o, width = COLS[name]
            a = small[:, o:o + width]
            if len(shape) == 2:
                return a.rearrange("p (a b) -> p a b", b=shape[1])
            return a

        def bview(i, *shape, off=0, of=buf):
            n = int(np.prod(shape))
            a = of[i][:, off:off + n]
            if len(shape) == 1:
                return a
            if len(shape) == 2:
                return a.rearrange("p (a b) -> p a b", b=shape[1])
            return a.rearrange("p (a b c) -> p a b c", b=shape[1], c=shape[2])

        def bview_r(i, *shape, off=0):
            return bview(i, *shape, off=off, of=buf_r)

        def over_heads(a, n, width):
            return a.unsqueeze(2).broadcast_to([P, n, width])

        def per_head(a, n, width):
            return a.unsqueeze(1).broadcast_to([P, n, width])

        ident = const("ident")
        zero_col = tin(1)
        eps_col = tin(1)
        minus_half = tin(8)

        ACTV = nc.scalar.activation
        V = nc.vector
        G = nc.gpsimd
        MM = nc.tensor.matmul

        class Chain:

            def __init__(self, eng, name):
                self.eng, self.name, self.n = eng, name, 0

            def add(self, ins):
                self.n += 1
                ins.then_inc(sem(self.name), 1)
                return ins

            def sync(self):
                self.eng.wait_ge(sem(self.name), self.n)

            def step(self, ins):
                self.add(ins)
                self.sync()

        def unit_ready(pe, n):
            pe.wait_ge(sem(f"unit_in{n % RING}"), 16 * (n // RING + 1))

        def w_cols(n):
            return ring[n % RING][:, :].rearrange("p (k c) -> p k c", k=KD)

        def w_rows(n):
            return ring[n % RING][:, :].rearrange("p (k c) -> p k c", k=2)

        def product_T(n, j, dst, acts, used=True):
            for k in range(KD):
                last = MM(dst, w_cols(n)[:, k, j * P:(j + 1) * P], acts[:, k, :], start=(k == 0), stop=(k == KD - 1))
            return last

        def product(n, t, dst, acts):
            for k in range(KD):
                last = MM(dst, acts[:, k, t * P:(t + 1) * P], w_cols(n)[:, k, :], start=(k == 0), stop=(k == KD - 1))
            return last

        def product_rows(n, lhsT, first, final):
            for kk in range(2):
                for t in range(NT):
                    for c in range(2):
                        last = MM(bank[4 + 2 * t + c][:, :], lhsT[:, kk, t * P:(t + 1) * P],
                                  w_rows(n)[:, kk, c * 512:(c + 1) * 512],
                                  start=first and kk == 0, stop=final and kk == 1)
            return last

        HALVES = [n for a, b in (("mix0_in", "mix0_out"), ("gdn_in", "gdn_out"), ("mem_kv", "branch"))
                  for n in range(AT[a], AT[b])]

        def half_done(eng, n):
            eng.wait_ge(sem("half_done"), HALVES.index(n) + 1)

        ssq = tin(8, NT)
        rstd = tin(8, NT)

        def norm_square(act, k, src, gain, dstT):
            for t in range(NT):
                ACTV(xn[:, t, :], src[:, t, :], ACT.Square, accum_out=ssq[:, k, t:t + 1]).then_inc(sem("norm_ssq"), 1)

        def norm_pow(pool, k):
            pool.wait_ge(sem("norm_var"), k + 1)
            G.tensor_tensor(rstd[:, k, :], ssq[:, k, :], minus_half[:, 0:NT], ALU.pow).then_inc(sem("norm_rstd"), 1)

        def norm_scale(dve, k, src):
            dve.wait_ge(sem("norm_ssq"), NT * (k + 1))
            V.tensor_scalar(ssq[:, k, :], ssq[:, k, :], 1.0 / D, EPS, ALU.mult, ALU.add).then_inc(sem("norm_var"), 1)
            dve.wait_ge(sem("norm_rstd"), k + 1)
            for t in range(NT):
                V.tensor_scalar(xn[:, t, :], src[:, t, :], rstd[:, k, t:t + 1], None, ALU.mult)\
                    .then_inc(sem("norm_xn"), 1)

        def norm_transpose(pe, k):
            for t in range(NT):
                pe.wait_ge(sem("norm_xn"), NT * k + t + 1)
                for c in range(KD):
                    last = nc.tensor.transpose(bank[c // 2][:, (c % 2) * S + t * P:(c % 2) * S + (t + 1) * P],
                                               xn[:, t, c * P:(c + 1) * P], ident)
            last.then_inc(sem("norm_T"), 1)

        def norm_out_act(act, k, row, dstT):
            act.wait_ge(sem("norm_T"), k + 1)
            for c in (0, 1, 4, 5):
                ACTV(dstT[:, c, :], bank[c // 2][:, (c % 2) * S:(c % 2 + 1) * S], ACT.Copy,
                     scale=const("gain", 8, KD)[:, row, c:c + 1]).then_inc(sem("norm_done"), 1)

        def norm_out_dve(dve, k, row, dstT):
            dve.wait_ge(sem("norm_T"), k + 1)
            for c in (2, 3, 6, 7):
                V.tensor_scalar(dstT[:, c, :], bank[c // 2][:, (c % 2) * S:(c % 2 + 1) * S],
                                const("gain", 8, KD)[:, row, c:c + 1], None, ALU.mult).then_inc(sem("norm_done"), 1)

        x_lo = bview_r(3, KD, S)
        SPLIT_NORMS = (1, 5, 7)

        def norm_high(act, k, row):
            act.wait_ge(sem("norm_T"), k + 1)
            for c in range(KD):
                ACTV(xnT_r[:, c, :], bank[c // 2][:, (c % 2) * S:(c % 2 + 1) * S], ACT.Copy,
                     scale=const("gain", 8, KD)[:, row, c:c + 1]).then_inc(sem("norm_high"), 1)

        def norm_low(dve, k, row):
            for c in range(KD):
                dve.wait_ge(sem("norm_high"), KD * SPLIT_NORMS.index(k) + c + 2 - c % 2)
                V.scalar_tensor_tensor(x_lo[:, c, :], bank[c // 2][:, (c % 2) * S:(c % 2 + 1) * S],
                                       const("gain", 8, KD)[:, row, c:c + 1], xnT_r[:, c, :].bitcast(F32),
                                       ALU.mult, ALU.subtract).then_inc(sem("norm_done"), 1)

        def norm_ready(eng, k):
            eng.wait_ge(sem("norm_done"), KD * (k + 1))

        def h_ready(eng, sublayers):
            if sublayers:
                eng.wait_ge(sem("h_done"), NT * sublayers)
            else:
                eng.wait_ge(sem("x_in"), 16)

        pssq = tin(3, 4)
        pvar = tin(3, NT)
        prstd = tin(3, NT)

        post_gain = small_conv[:, :]

        def post_square(act, i, units):
            act.wait_ge(sem("unit_used"), units)
            for j in range(4):
                ACTV(xn[:, j // 2, (j % 2) * 512:(j % 2 + 1) * 512], bank[4 + j][:, :], ACT.Square,
                     accum_out=pssq[:, i, j:j + 1]).then_inc(sem("post_ssq"), 1)

        def post_pow(pool, i):
            pool.wait_ge(sem("post_var"), i + 1)
            G.tensor_tensor(prstd[:, i, :], pvar[:, i, :], minus_half[:, 0:NT], ALU.pow).then_inc(sem("post_rstd"), 1)

        def post_add(dve, ch, i, scale):
            dve.wait_ge(sem("post_ssq"), 4 * (i + 1))
            ch.step(V.tensor_tensor(pvar[:, i, :], pssq[:, i, 0:4:2], pssq[:, i, 1:4:2], ALU.add))
            V.tensor_scalar(pvar[:, i, :], pvar[:, i, :], 1.0 / D, EPS, ALU.mult, ALU.add)\
                .then_inc(sem("post_var"), 1)
            dve.wait_ge(sem("post_rstd"), i + 1)
            dve.wait_ge(sem("post_in"), 16 * (i + 1))
            if scale != 1.0:
                ch.step(V.tensor_scalar(prstd[:, i, :], prstd[:, i, :], scale, None, ALU.mult))
            for j in range(4):
                t, c = j // 2, slice((j % 2) * 512, (j % 2 + 1) * 512)
                gain = post_gain[:, c]
                ch.step(V.scalar_tensor_tensor(xn[:, t, c], bank[4 + j][:, :], prstd[:, i, t:t + 1], gain,
                                               ALU.mult, ALU.mult))
                ins = V.tensor_tensor(h[:, t, c], h[:, t, c], xn[:, t, c], ALU.add)
                if j % 2:
                    ins.then_inc(sem("h_done"), 1)

        HI = len(HI_BUFS)

        def high(n, i, k):
            return buf_r[HI_BUFS[i % HI]][:, :].rearrange("p (k c) -> p k c", k=k)

        def low(n, i, k):
            return ring_r[n % RING][:, :].rearrange("p (k c) -> p k c", k=k)

        def split_high(act, stage, i):
            n = AT[stage] + i
            unit_ready(act, n)
            if i >= HI:
                act.wait_ge(sem("unit_used"), n - HI + 1)
            ACTV(buf_r[HI_BUFS[i % HI]][:, :], ring[n % RING][:, :], ACT.Copy)\
                .then_inc(sem("split_high"), 1)

        def split_low(dve, stage, i):
            n = AT[stage] + i
            dve.wait_ge(sem("split_high"), SPLITS[stage] + i + 1)
            V.tensor_tensor(ring_r[n % RING][:, :], ring[n % RING][:, :], buf_r[HI_BUFS[i % HI]][:, :].bitcast(F32),
                            ALU.subtract).then_inc(sem("split_low"), 1)

        def split_ready(pe, stage, i):
            pe.wait_ge(sem("split_low"), SPLITS[stage] + i + 1)

        def three_passes(dst, stationary, moving, start, stop):
            MM(dst, stationary[0], moving[0], start=start, stop=False)
            MM(dst, stationary[0], moving[1], start=False, stop=False)
            return MM(dst, stationary[1], moving[0], start=False, stop=stop)

        ffn_hid = bview_r(0, 4, S), bview_r(0, 4, S, off=1024)
        ffn_silu = bview(4, 2, S)
        ffn_prod = bview(4, 2, S, off=512)

        def swiglu_order(steps):
            gate = [max(3 * s - 1, 0) for s in range(steps)]
            down = [3 * s + 4 if s < steps - 1 else 3 * steps - 1 for s in range(steps)]
            return gate, down

        def parts(pair, *index):
            return [a[index] for a in pair]

        def ffn_tensor(pe, past, stage, acts):
            steps, base = FF_STEPS, AT[stage]
            gate, down = swiglu_order(steps)
            every = slice(None)

            def down_product(s):
                i = down[s]
                split_ready(pe, stage, i)
                pe.wait_ge(sem("ffn_hidden"), 2 * (past + s) + 2)
                hi, lo = high(base + i, i, 2), low(base + i, i, 2)
                for kk in range(2):
                    for t in range(NT):
                        hid = parts(ffn_hid, every, 2 * (s % 2) + kk, slice(t * P, (t + 1) * P))
                        for c in range(2):
                            o = slice(c * 512, (c + 1) * 512)
                            last = three_passes(bank[4 + 2 * t + c][:, :], hid, (hi[:, kk, o], lo[:, kk, o]),
                                                s == 0 and kk == 0, s == steps - 1 and kk == 1)
                last.then_inc(sem("unit_used"), 1)

            for s in range(steps):
                for q in range(4):
                    if s and q < 2:
                        pe.wait_ge(sem("ffn_hidden"), 2 * (past + s) - 1 + q)
                    for k in range(KD):
                        i = gate[s] + k // 4
                        if q == 0 and k % 4 == 0:
                            split_ready(pe, stage, i)
                        o = slice(q * P, (q + 1) * P)
                        last = three_passes(bank[q][:, 0:S], (high(base + i, i, 4)[:, k % 4, o],
                                                              low(base + i, i, 4)[:, k % 4, o]),
                                            parts(acts, every, k, every), k == 0, k == KD - 1)
                    if q == 3:
                        last.then_inc(sem("unit_used"), 2)
                    else:
                        last.then_inc(sem("ffn_up" if q == 2 else "ffn_gate"), 1)
                if s:
                    down_product(s - 1)
            down_product(steps - 1)

        FIRST_SPLITS = 5

        def ffn_splits(s):
            return range(FIRST_SPLITS + 3 * s, min(FIRST_SPLITS + 3 * s + 3, FF_UNITS))

        def ffn_scalar(act, past, stage):
            for s in range(FF_STEPS):
                for j in range(2):
                    act.wait_ge(sem("ffn_gate"), 2 * (past + s) + j + 1)
                    if s:
                        act.wait_ge(sem("ffn_hidden"), 2 * (past + s) + j - 1)
                    ACTV(ffn_silu[:, j, :], bank[j][:, 0:S], ACT.Silu).then_inc(sem("ffn_silu"), 1)
                for i in ffn_splits(s):
                    split_high(act, stage, i)

        def ffn_vector(dve, ch, past, stage):
            base = AT[stage]
            gate, down = swiglu_order(FF_STEPS)
            for s in range(FF_STEPS):
                for j in range(2):
                    dve.wait_ge(sem("ffn_silu"), 2 * (past + s) + j + 1)
                    if j == 0:
                        dve.wait_ge(sem("ffn_up"), past + s + 1)
                    else:
                        dve.wait_ge(sem("unit_used"), base + gate[s] + 2)
                    if s >= 2:
                        dve.wait_ge(sem("unit_used"), base + down[s - 2] + 1)
                    hi, lo = (a[:, 2 * (s % 2) + j, :] for a in ffn_hid)
                    ch.step(V.tensor_tensor(ffn_prod[:, j, :], ffn_silu[:, j, :], bank[2 + j][:, 0:S], ALU.mult))
                    ch.step(V.tensor_copy(hi, ffn_prod[:, j, :]))
                    V.tensor_tensor(lo, ffn_prod[:, j, :], hi.bitcast(F32), ALU.subtract)\
                        .then_inc(sem("ffn_hidden"), 1)
                for i in ffn_splits(s):
                    split_low(dve, stage, i)

        sc_sb = bview(9, 2, 1024)
        pr_sb = sc_sb
        pT_sb = bview(11, 2, 1024)
        mxs, nmx, esum, sink_e, rden = tin(2), tin(2), tin(2), tin(2), tin(2)

        def att_tensor(pe, past, units, before):
            before(pe)

            def scores(u):
                if u >= 2:
                    pe.wait_ge(sem("att_masked"), past + u - 1)
                for off, w, lhsT, rhs in units[u]["score"]:
                    last = MM(bank[2 * (u % 2) + off // 512][:, off % 512:off % 512 + w], lhsT, rhs,
                              start=True, stop=True)
                last.then_inc(sem("att_scores"), 1)

            scores(0)
            for u, unit in enumerate(units):
                if u + 1 < len(units):
                    scores(u + 1)
                pe.wait_ge(sem("att_probs"), past + u + 1)
                if u:
                    pe.wait_ge(sem("att_copied"), past + u)
                for b in range(len(unit["values"])):
                    last = nc.tensor.transpose(bank[4 + b // 4][:, (b % 4) * P:(b % 4 + 1) * P],
                                               pr_sb[:, u % 2, unit["block"](b):unit["block"](b) + P], ident)
                last.then_inc(sem("att_T"), 1)
                pe.wait_ge(sem("att_copied"), past + u + 1)
                if u >= 2:
                    pe.wait_ge(sem("att_out"), past + u - 1)
                lo, n = unit["rows"]
                for b, v in enumerate(unit["values"]):
                    last = MM(bank[6 + u % 2][lo:lo + n, 0:P], v, pT_sb[:, u % 2, b * P:(b + 1) * P],
                              start=(b == 0), stop=(b == len(unit["values"]) - 1))
                last.then_inc(sem("att_values"), 1)

        def att_scalar(act, past, units):
            for u, unit in enumerate(units):
                i = u % 2
                act.wait_ge(sem("att_max"), past + u + 1)
                for off, w in unit["spans"]:
                    last = ACTV(pr_sb[:, i, off:off + w], sc_sb[:, i, off:off + w], ACT.Exp, bias=nmx[:, i:i + 1],
                                accum_out=esum[:, i:i + 1])
                if unit["sink"] is not None:
                    last = ACTV(sink_e[:, i:i + 1], unit["sink"], ACT.Exp, bias=nmx[:, i:i + 1])
                last.then_inc(sem("att_exp"), 1)
                act.wait_ge(sem("att_T"), past + u + 1)
                if u >= 2:
                    act.wait_ge(sem("att_values"), past + u - 1)
                nb = len(unit["values"])
                for b in range(0, nb, 4):
                    w = min(4, nb - b) * P
                    last = ACTV(pT_sb[:, i, b * P:b * P + w], bank[4 + b // 4][:, 0:w], ACT.Copy)
                last.then_inc(sem("att_copied"), 1)

        def att_vector(dve, ch, past, units):
            def result(u):
                dve.wait_ge(sem("att_values"), past + u + 1)
                lo, n = units[u]["rows"]
                V.tensor_copy(units[u]["out"], bank[6 + u % 2][lo:lo + n, 0:P]).then_inc(sem("att_out"), 1)

            for u, unit in enumerate(units):
                i = u % 2
                dve.wait_ge(sem("att_scores"), past + u + 1)
                if u >= 2:
                    dve.wait_ge(sem("att_T"), past + u - 1)
                for off, w, mask, slope in unit["mask"]:
                    src = bank[2 * (u % 2) + off // 512][:, off % 512:off % 512 + w]
                    if mask is None:
                        last = V.tensor_copy(sc_sb[:, i, off:off + w], src)
                    else:
                        last = V.scalar_tensor_tensor(sc_sb[:, i, off:off + w], mask, slope, src, ALU.mult, ALU.add)
                last.then_inc(sem("att_masked"), 1)
                dve.wait_ge(sem("att_masked"), past + u + 1)
                (off, w), = unit["spans"]
                if unit["sink"] is None:
                    V.tensor_reduce(nmx[:, i:i + 1], sc_sb[:, i, off:off + w], AX.X, ALU.max, negate=True)\
                        .then_inc(sem("att_max"), 1)
                else:
                    ch.step(V.tensor_reduce(mxs[:, i:i + 1], sc_sb[:, i, off:off + w], AX.X, ALU.max))
                    V.tensor_scalar(nmx[:, i:i + 1], mxs[:, i:i + 1], unit["sink"], -1.0, ALU.max, ALU.mult)\
                        .then_inc(sem("att_max"), 1)
                if u:
                    result(u - 1)
                dve.wait_ge(sem("att_exp"), past + u + 1)
                den = esum[:, i:i + 1]
                if unit["sink"] is not None:
                    ch.step(V.tensor_tensor(esum[:, i:i + 1], esum[:, i:i + 1], sink_e[:, i:i + 1], ALU.add))
                ch.step(V.reciprocal(rden[:, i:i + 1], den))
                V.tensor_scalar(pr_sb[:, i, off:off + w], pr_sb[:, i, off:off + w], rden[:, i:i + 1], None, ALU.mult)\
                    .then_inc(sem("att_probs"), 1)
            result(len(units) - 1)

        def softplus_buffers(n):
            return [tin(n) for _ in range(5)]

        def softplus_vector_a(ch, x, b):
            V.scalar_tensor_tensor(b[0], x, -1.0, x, ALU.mult, ALU.min).then_inc(sem("softplus_arg"), 1)

        def softplus_scalar(act, use, b):
            act.wait_ge(sem("softplus_arg"), use)
            ACTV(b[1], b[0], ACT.Exp).then_inc(sem("softplus_z"), 1)
            act.wait_ge(sem("softplus_w"), use)
            ACTV(b[3], b[2], ACT.Ln).then_inc(sem("softplus_ln"), 1)

        def softplus_vector_b(dve, ch, use, x, b, out):
            dve.wait_ge(sem("softplus_z"), use)
            V.tensor_scalar(b[2], b[1], 1.0, None, ALU.add).then_inc(sem("softplus_w"), 1)
            dve.wait_ge(sem("softplus_w"), use)
            dve.wait_ge(sem("softplus_ln"), use)
            ch.step(V.tensor_tensor(b[3], b[3], b[1], ALU.mult))
            ch.step(V.tensor_scalar(b[4], b[2], -1.0, None, ALU.add))
            ch.step(V.tensor_scalar(b[2], b[4], 0.0, None, ALU.is_equal))
            ch.step(V.tensor_tensor(b[4], b[4], b[2], ALU.add))
            ch.step(V.reciprocal(b[4], b[4]))
            ch.step(V.tensor_tensor(b[3], b[3], b[4], ALU.mult))
            ch.step(V.tensor_tensor(b[2], b[2], b[1], ALU.mult))
            ch.step(V.tensor_tensor(b[3], b[3], b[2], ALU.add))
            ch.step(V.scalar_tensor_tensor(out, x, 0.0, b[3], ALU.max, ALU.add))

        xcT = bview(0, 4, S)
        gelT = bview(0, 4, S, off=1024)
        lru_r = bview(1, 4, S)
        lru_i = bview(1, 4, S, off=1024)
        lru_a = bview(2, 4, S)
        lru_t = bview(2, 4, S, off=1024)
        qkv = bview(3, NT, 768)
        qT0 = bview(4, 4, S)
        kT0 = bview(4, S, off=1024)
        rope_a = bview(5, NT, 640)
        rope_b = bview(6, NT, 640)
        mixT = bview(7, KD, S)
        lam_s = tin(4)
        lam_b = softplus_buffers(4)
        neg_s, pos_s = tin(4), tin(4)
        qk_ssq, qk_var, qk_rstd = tin(20), tin(20), tin(20)

        def flat(a):
            return a.rearrange("p a b -> p (a b)")

        def mix0_tensor(pe):
            base = AT["mix0_in"]
            norm_ready(pe, 0)
            for i in range(8):
                n = base + i // 2
                unit_ready(pe, n)
                if i >= 4:
                    pe.wait_ge(sem("conv0_done"), i - 3)
                last = product_T(n, i % 2, bank[i % 4][:, 0:S], xnT)
                if i % 2:
                    last.then_inc(sem("unit_used"), 1)
                else:
                    last.then_inc(sem("half_done"), 1)
            for i in range(6):
                n = base + 4 + i // 2
                unit_ready(pe, n)
                if i >= 4:
                    pe.wait_ge(sem("qkv_copied"), i - 3)
                last = product(n, i % 2, bank[4 + i % 4][:, 0:256], xnT)
                if i % 2:
                    last.then_inc(sem("unit_used"), 1)
                else:
                    last.then_inc(sem("half_done"), 1)
            pe.wait_ge(sem("conv0_done"), 4)
            for c in range(4):
                pe.wait_ge(sem("gelu_done"), c + 1)
                MM(bank[c][:, 0:S], const("lru_wa", 4, P)[:, c, :], xcT[:, c, :], start=True, stop=True)
                MM(bank[c][:, S:2 * S], const("lru_wi", 4, P)[:, c, :], xcT[:, c, :], start=True, stop=True)\
                    .then_inc(sem("lru_gates"), 1)
            pe.wait_ge(sem("rope_done"), 1)
            for t in range(NT):
                for c in range(4):
                    nc.tensor.transpose(bank[4 + t][:, c * P:(c + 1) * P], qkv[:, t, c * P:(c + 1) * P], ident)
                last = nc.tensor.transpose(bank[6][:, t * P:(t + 1) * P], qkv[:, t, 512:640], ident)
            last.then_inc(sem("qk_T"), 1)

        def att0_units():
            units = []
            for t in range(NT):
                for s in range(ATT_SLOTS):
                    c, lo = s // 2, (s % 2) * 64
                    w = (t + 1) * P
                    units.append(dict(
                        score=[(0, w, qT0[lo:lo + 64, c, t * P:(t + 1) * P], kT0[lo:lo + 64, 0:w])],
                        mask=[(0, w, const("band")[:, 2 * P - w:2 * P], 1.0)], spans=[(0, w)],
                        block=lambda b: b * P, sink=const("sinks")[:, s:s + 1],
                        values=[qkv[:, b, 640 + lo:640 + lo + 64] for b in range(t + 1)],
                        rows=(lo, 64), out=mixT[lo:lo + 64, 4 + c, t * P:(t + 1) * P]))
            return units

        att0 = att0_units()

        def att0_before(pe):
            pe.wait_ge(sem("qT0_done"), 1)
            pe.wait_ge(sem("lru_gates_read"), 8)

        def mix0_scalar(act):
            base = AT["mix0_in"]
            for c in range(4):
                if c % 2:
                    act.wait_ge(sem("unit_used"), base + 2 + c // 2 + 1)
                else:
                    half_done(act, base + 2 + c // 2)
                ACTV(gelT[:, c, :], bank[c][:, 0:S], ACT.Gelu_apprx_tanh).then_inc(sem("gelu_done"), 1)
            for i in range(6):
                if i % 2:
                    act.wait_ge(sem("unit_used"), base + 4 + i // 2 + 1)
                else:
                    half_done(act, base + 4 + i // 2)
                ACTV(qkv[:, i % 2, (i // 2) * 256:(i // 2 + 1) * 256], bank[4 + i % 4][:, 0:256], ACT.Copy)\
                    .then_inc(sem("qkv_copied"), 1)
            for c in range(4):
                act.wait_ge(sem("lru_gates"), c + 1)
                ACTV(lru_r[:, c, :], bank[c][:, 0:S], ACT.Sigmoid, bias=const("lru_ba")[:, c:c + 1])\
                    .then_inc(sem("lru_gates_read"), 1)
                ACTV(lru_i[:, c, :], bank[c][:, S:2 * S], ACT.Sigmoid, bias=const("lru_bi")[:, c:c + 1])\
                    .then_inc(sem("lru_gates_read"), 1)
            act.wait_ge(sem("lru_gates_read"), 8)
            act.wait_ge(sem("lam_done"), 1)
            for c in range(4):
                ACTV(lru_a[:, c, :], lru_r[:, c, :], ACT.Exp, scale=neg_s[:, c:c + 1])
                ACTV(lru_t[:, c, :], lru_r[:, c, :], ACT.Tanh, scale=pos_s[:, c:c + 1]).then_inc(sem("lru_at"), 1)
            act.wait_ge(sem("qk_T"), 1)
            ACTV(flat(qT0)[:, :].rearrange("p (c t q) -> p c t q", c=4, t=NT)[:, :, 0, :],
                 bank[4][:, :].rearrange("p (c q) -> p c q", c=4), ACT.Copy, scale=64 ** -0.5)
            ACTV(flat(qT0)[:, :].rearrange("p (c t q) -> p c t q", c=4, t=NT)[:, :, 1, :],
                 bank[5][:, :].rearrange("p (c q) -> p c q", c=4), ACT.Copy, scale=64 ** -0.5)
            ACTV(kT0, bank[6][:, 0:S], ACT.Copy).then_inc(sem("qT0_done"), 1)
            act.wait_ge(sem("lru_m"), 1)
            ACTV(flat(lru_t), flat(lru_t), ACT.Sqrt).then_inc(sem("lru_root"), 1)

        def conv(dve, ch, dst, src, taps, bias, width=S):
            if bias is None:
                ch.step(V.tensor_scalar(dst, src, taps[:, 3:4], None, ALU.mult))
            else:
                ch.step(V.tensor_scalar(dst, src, taps[:, 3:4], bias, ALU.mult, ALU.add))
            for j in (2, 1, 0):
                d = 3 - j
                ins = V.scalar_tensor_tensor(dst[:, d:width], src[:, 0:width - d], taps[:, j:j + 1],
                                             dst[:, d:width], ALU.mult, ALU.add)
                if j:
                    ch.step(ins)
            return ins

        def mix0_vector(dve, ch):
            base = AT["mix0_in"]
            for c in range(4):
                if c % 2:
                    dve.wait_ge(sem("unit_used"), base + c // 2 + 1)
                else:
                    half_done(dve, base + c // 2)
                conv(dve, ch, xcT[:, c, :], bank[c][:, 0:S], const("lru_w", 4, CONV)[:, c, :],
                     const("lru_b")[:, c:c + 1]).then_inc(sem("conv0_done"), 1)
            dve.wait_ge(sem("qkv_copied"), 6)
            qk = qkv[:, :, 0:640]
            ch.step(V.tensor_tensor(rope_a, qk, qk, ALU.mult))
            ch.step(V.tensor_reduce(qk_ssq, flat(rope_a).rearrange("p (h d) -> p h d", d=64), AX.X, ALU.add))
            V.tensor_scalar(qk_var, qk_ssq, 1.0 / 64, EPS, ALU.mult, ALU.add).then_inc(sem("head_var"), 1)
            dve.wait_ge(sem("head_rstd"), 1)
            for t in range(NT):
                heads = qkv[:, t, 0:640].rearrange("p (h d) -> p h d", d=64)
                ch.step(V.tensor_tensor(heads, heads, over_heads(qk_rstd[:, 10 * t:10 * t + 10], 10, 64), ALU.mult))
                ch.add(V.tensor_tensor(heads[:, 0:8, :], heads[:, 0:8, :], per_head(const("q_norm"), 8, 64), ALU.mult))
                ch.step(V.tensor_tensor(heads[:, 8:10, :], heads[:, 8:10, :], per_head(const("k_norm"), 2, 64),
                                        ALU.mult))
                x1, x2 = heads[:, :, 0:32], heads[:, :, 32:64]
                ta = rope_a[:, t, :].rearrange("p (h d) -> p h d", d=64)
                tb = rope_b[:, t, :].rearrange("p (h d) -> p h d", d=64)
                cos = per_head(const("cos", NT, 32)[:, t, :], 10, 32)
                sin = per_head(const("sin", NT, 32)[:, t, :], 10, 32)
                ch.add(V.tensor_tensor(ta[:, :, 0:32], x1, cos, ALU.mult))
                ch.add(V.tensor_tensor(tb[:, :, 0:32], x2, sin, ALU.mult))
                ch.add(V.tensor_tensor(ta[:, :, 32:64], x2, cos, ALU.mult))
                ch.step(V.tensor_tensor(tb[:, :, 32:64], x1, sin, ALU.mult))
                ch.add(V.tensor_tensor(x1, ta[:, :, 0:32], tb[:, :, 0:32], ALU.subtract))
                ins = V.tensor_tensor(x2, ta[:, :, 32:64], tb[:, :, 32:64], ALU.add)
                if t == NT - 1:
                    ins.then_inc(sem("rope_done"), 1)
                else:
                    ch.add(ins)
            ch.sync()

        def mix0_vector_lru(dve, ch):
            dve.wait_ge(sem("lru_at"), 4)
            gx = flat(lru_i)
            ch.add(V.tensor_tensor(gx, gx, flat(xcT), ALU.mult))
            ch.step(V.tensor_tensor(flat(lru_r), flat(lru_a), flat(lru_a), ALU.mult))
            V.scalar_tensor_tensor(flat(lru_t), flat(lru_r), 1.0, flat(lru_t), ALU.add, ALU.mult)\
                .then_inc(sem("lru_m"), 1)
            dve.wait_ge(sem("lru_root"), 1)
            ch.step(V.tensor_tensor(gx, gx, flat(lru_t), ALU.mult))
            for c in range(4):
                ch.add(V.tensor_tensor_scan(lru_r[:, c, :], lru_a[:, c, :], lru_i[:, c, :], 0.0, ALU.mult, ALU.add))
            ch.sync()
            V.tensor_tensor(mixT[:, 0:4, :], lru_r, gelT, ALU.mult).then_inc(sem("lru_y"), 1)

        def out_tensor(pe, base, ready, acts):
            ready(pe)
            for r in range(4):
                unit_ready(pe, base + r)
                last = product_rows(base + r, acts[:, 2 * r:2 * r + 2, :], r == 0, r == 3)
                last.then_inc(sem("unit_used"), 1)

        def rows_done(eng, base):
            eng.wait_ge(sem("unit_used"), base + 4)

        def add_product(dve, base_end):
            dve.wait_ge(sem("unit_used"), base_end)
            for t in range(NT):
                for c in range(2):
                    last = V.tensor_tensor(h[:, t, c * 512:(c + 1) * 512], h[:, t, c * 512:(c + 1) * 512],
                                           bank[4 + 2 * t + c][:, :], ALU.add)
                    if c:
                        last.then_inc(sem("h_done"), 1)

        NP = NT * GH
        LEVELS = 6
        g_q, g_k, g_v = bview(0, GH, S), bview(1, GH, S), bview(2, GH, S)
        g_gate = bview(3, NP, P)
        g_rows = bview(4, NP, P)
        g_qdT = g_rows
        g_eG = bview(5, NP, P)
        g_A = bview(6, NP, P)
        g_aT = bview(7, NP, P)
        g_T = bview(8, NP, P)
        g_TT = bview(9, NP, P)
        g_sq = [bview(8, GH, S), bview(9, GH, S)]
        g_norm = [bview(10, GH, S), bview(11, GH, S)]
        g_kb, g_kd = bview(10, NP, P), bview(11, NP, P)
        g_vb = flat(xn).rearrange("p (a b) -> p a b", b=P)
        g_YT = bview(0, NP, P)
        g_Ak = [bview(2, NP, P), bview(1, NP, P)]
        g_WT = bview(2, NP, P)
        g_U = bview(8, NP, P)
        g_S = xn[:, 0, :].rearrange("p (a b) -> p a b", b=P)
        g_osq = bview(9, NP, P)
        g_y = bview(10, NP, P)
        conv_out = [silu_c for silu_c in (small_conv[:, i * S:(i + 1) * S] for i in range(4))]
        ab = tin(NT, 16)
        sp_x, sp_out, g_g, g_beta, g_bk = tin(NP), tin(NP), tin(NP), tin(NP), tin(NP)
        sp_b = softplus_buffers(NP)
        ea = tin(GH)
        g_arg, g_exp = tin(2 * NP), tin(2 * NP)
        o_ssq, o_rstd = tin(NP), tin(NP)

        def psum4(i):
            return bank[i][:, :].rearrange("p (a b) -> p a b", b=P)

        def gdn_in_tensor(pe):
            base = AT["gdn_in"]
            norm_ready(pe, 2)
            for t in range(NT):
                for k in range(KD):
                    last = MM(bank[6][:, 16 * t:16 * t + 16], xnT[:, k, t * P:(t + 1) * P],
                              const("w_ab", KD, 16)[:, k, :], start=(k == 0), stop=(k == KD - 1))
            last.then_inc(sem("ab_done"), 1)
            for i in range(24):
                n = base + i // 2
                unit_ready(pe, n)
                if i >= 4:
                    pe.wait_ge(sem("gdn_conv"), i - 3)
                last = product_T(n, i % 2, bank[i % 4][:, 0:S], xnT)
                last.then_inc(sem("unit_used" if i % 2 else "half_done"), 1)
            for i in range(8):
                n = base + 12 + i // 2
                unit_ready(pe, n)
                if i >= 2:
                    pe.wait_ge(sem("gate_copied"), i - 1)
                last = product(n, i % 2, bank[4 + i % 2][:, 0:256], xnT)
                last.then_inc(sem("unit_used" if i % 2 else "half_done"), 1)

        def gdn_in_wait(eng, i, base):
            if i % 2:
                eng.wait_ge(sem("unit_used"), base + i // 2 + 1)
            else:
                half_done(eng, base + i // 2)

        def gdn_in_scalar(act):
            softplus_scalar(act, 2, sp_b)
            ACTV(ea, const("a_log"), ACT.Exp).then_inc(sem("gdn_ea"), 1)
            act.wait_ge(sem("ab_copied"), 1)
            ACTV(g_beta.rearrange("p (t e) -> p t e", t=NT), ab[:, :, 8:16], ACT.Sigmoid).then_inc(sem("beta_done"), 1)
            for i in range(24):
                act.wait_ge(sem("gdn_conv"), i + 1)
                dst = (g_q, g_k, g_v)[i // 8][:, i % 8, :]
                ACTV(dst, conv_out[i % 4], ACT.Silu).then_inc(sem("gdn_silu"), 1)
            for i in range(8):
                gdn_in_wait(act, i, AT["gdn_in"] + 12)
                c = i // 2
                ACTV(g_gate[:, 8 * (i % 2) + 2 * c:8 * (i % 2) + 2 * c + 2, :],
                     bank[4 + i % 2][:, 0:256].rearrange("p (a b) -> p a b", b=P), ACT.Silu)\
                    .then_inc(sem("gate_copied"), 1)

        def gdn_in_vector(dve, ch):
            dve.wait_ge(sem("ab_done"), 1)
            V.tensor_copy(ab, bank[6][:, 0:32].rearrange("p (t e) -> p t e", t=NT)).then_inc(sem("ab_copied"), 1)
            dve.wait_ge(sem("ab_copied"), 1)
            ch.step(V.tensor_tensor(sp_x.rearrange("p (t e) -> p t e", t=NT), ab[:, :, 0:8],
                                    per_head(const("dt_bias"), NT, GH), ALU.add))
            softplus_vector_a(ch, sp_x, sp_b)
            softplus_vector_b(dve, ch, 2, sp_x, sp_b, sp_out)
            dve.wait_ge(sem("gdn_ea"), 1)
            ch.step(V.scalar_tensor_tensor(g_g.rearrange("p (t e) -> p t e", t=NT),
                                           sp_out.rearrange("p (t e) -> p t e", t=NT), -1.0,
                                           per_head(ea, NT, GH), ALU.mult, ALU.mult))
            V.tensor_copy(g_rows, over_heads(g_g, NP, P)).then_inc(sem("g_done"), 1)
            for i in range(24):
                gdn_in_wait(dve, i, AT["gdn_in"])
                if i >= 4:
                    dve.wait_ge(sem("gdn_silu"), i - 3)
                conv(dve, ch, conv_out[i % 4], bank[i % 4][:, 0:S], const("gdn_conv", 24, CONV)[:, i, :], None)\
                    .then_inc(sem("gdn_conv"), 1)

        def gdn_square(pool):
            for i, src in enumerate((g_q, g_k)):
                pool.wait_ge(sem("gdn_silu"), 8 * (i + 1))
                G.tensor_tensor(flat(g_sq[i]), flat(src), flat(src), ALU.mult).then_inc(sem("gdn_sq"), 1)

        def gdn_core_tensor(pe):
            pe.wait_ge(sem("g_done"), 1)
            for t in range(NT):
                MM(bank[6][:, 64 + 8 * t:72 + 8 * t], const("cum"), g_g[:, 8 * t:8 * t + 8], start=True, stop=True)
                last = MM(bank[6][:, 80 + 8 * t:88 + 8 * t], const("same"), g_g[:, 8 * t:8 * t + 8],
                          start=True, stop=True)
            last.then_inc(sem("gcol"), 1)
            for i in range(NP):
                if i == 0:
                    pe.wait_ge(sem("gdn_conv"), 24)
                last = MM(bank[i // 4][:, (i % 4) * P:(i % 4 + 1) * P], g_rows[:, i, :], const("cum"),
                          start=True, stop=True)
                if i % 4 == 3:
                    last.then_inc(sem("grow"), 1)
            pe.wait_ge(sem("gate_copied"), 8)
            pe.wait_ge(sem("gcol_copied"), 1)
            for i in range(2):
                pe.wait_ge(sem("gdn_sq"), i + 1)
                for c in range(4):
                    if i:
                        pe.wait_ge(sem("gdn_root"), c + 1)
                    MM(bank[4 + c][:, :], const("ones"), flat(g_sq[i])[:, c * 512:(c + 1) * 512],
                       start=True, stop=True).then_inc(sem("gdn_sums"), 1)
            pe.wait_ge(sem("grow_read"), 2)
            pe.wait_ge(sem("qk_normed"), 2)
            for i in range(NP):
                t, e = i // GH, i % GH
                kt = g_k[:, e, t * P:(t + 1) * P]
                last = MM(bank[i // 4][:, (i % 4) * P:(i % 4 + 1) * P], kt, kt, start=True, stop=True)
                if i % 4 == 3:
                    last.then_inc(sem("gdn_kk"), 1)
            for i in range(NP):
                t, e = i // GH, i % GH
                last = MM(bank[4 + i // 4][:, (i % 4) * P:(i % 4 + 1) * P], g_k[:, e, t * P:(t + 1) * P],
                          g_q[:, e, t * P:(t + 1) * P], start=True, stop=True)
                if i % 4 == 3:
                    last.then_inc(sem("gdn_qk"), 1)
            for j, src in enumerate((g_k, g_v)):
                for i in range(NP):
                    t, e = i // GH, i % GH
                    if i % 4 == 0:
                        pe.wait_ge(sem("gdn_aT" if j else "gdn_A"), i // 4 + 1)
                    last = nc.tensor.transpose(bank[4 * j + i // 4][:, (i % 4) * P:(i % 4 + 1) * P],
                                               src[:, e, t * P:(t + 1) * P], ident)
                    if i % 4 == 3:
                        last.then_inc(sem("gdn_kvT"), 1)
            pe.wait_ge(sem("gdn_level"), 1)
            for i in range(NP):
                if i % 4 == 0:
                    pe.wait_ge(sem("gdn_kv"), i // 4 + 1)
                last = nc.tensor.transpose(bank[i // 4][:, (i % 4) * P:(i % 4 + 1) * P], g_Ak[0][:, i, :], ident)
                if i % 4 == 3:
                    last.then_inc(sem("gdn_A0T"), 1)
            pe.wait_ge(sem("gdn_kv"), 8)
            for k in range(1, LEVELS):
                pe.wait_ge(sem("gdn_level"), k + 1)
                for t in range(NT):
                    pe.wait_ge(sem("gdn_T"), NT * (k - 1) + t + 1)
                    for e in range(GH):
                        i = GH * t + e
                        last = MM(bank[i // 4][:, (i % 4) * P:(i % 4 + 1) * P], g_Ak[k % 2][:, i, :], g_TT[:, i, :],
                                  start=True, stop=True)
                    last.then_inc(sem("gdn_YT"), 1)
                for t in range(NT):
                    pe.wait_ge(sem("gdn_YT_copied"), NT * (k - 1) + t + 1)
                    if t or k > 1:
                        pe.wait_ge(sem("gdn_T"), NT * k + t)
                    for e in range(GH):
                        i, o = GH * t + e, slice((e % 4) * P, (e % 4 + 1) * P)
                        if k < LEVELS - 1:
                            MM(bank[4 + e // 4][:, o], g_YT[:, i, :], g_T[:, i, :], start=True, stop=True)
                        last = MM(bank[6 + e // 4][:, o], g_T[:, i, :], g_YT[:, i, :], start=True, stop=True)
                    last.then_inc(sem("gdn_Z"), 1)
            pe.wait_ge(sem("gdn_T"), NT * LEVELS)
            for i in range(NP):
                last = MM(bank[i // 4][:, (i % 4) * P:(i % 4 + 1) * P], g_kb[:, i, :], g_TT[:, i, :],
                          start=True, stop=True)
            last.then_inc(sem("gdn_WT"), 1)
            for i in range(NP):
                last = MM(bank[4 + i // 4][:, (i % 4) * P:(i % 4 + 1) * P], g_TT[:, i, :], g_vb[:, i, :],
                          start=True, stop=True)
            last.then_inc(sem("gdn_U"), 1)
            pe.wait_ge(sem("gdn_WT_copied"), 1)
            for c in range(4):
                t, r = c // 2, slice(CHUNK * (c % 2), CHUNK * (c % 2) + CHUNK)
                if c:
                    pe.wait_ge(sem("gdn_S"), c)
                    for e in range(GH):
                        last = MM(bank[e // 4][r, (e % 4) * P:(e % 4 + 1) * P], g_WT[:, GH * t + e, r], g_S[:, e, :],
                                  start=True, stop=True)
                    last.then_inc(sem("gdn_WS"), 1)
                pe.wait_ge(sem("gdn_vn"), c + 1)
                if c < 3:
                    for e in range(GH):
                        last = MM(bank[6 + e // 4][:, (e % 4) * P:(e % 4 + 1) * P], g_kd[r, GH * t + e, :],
                                  g_U[r, GH * t + e, :], start=True, stop=True)
                    last.then_inc(sem("gdn_kv_state"), 1)
                for e in range(GH):
                    i = GH * t + e
                    dst = bank[2 + 2 * t + e // 4][r, (e % 4) * P:(e % 4 + 1) * P]
                    if c:
                        MM(dst, g_qdT[:, i, r], g_S[:, e, :], start=True, stop=False)
                    last = MM(dst, g_aT[r, i, r], g_U[r, i, :], start=(c == 0), stop=True)
                last.then_inc(sem("gdn_O"), 1)
            for t in range(NT):
                pe.wait_ge(sem("gdn_y"), t + 1)
                for e in range(GH):
                    last = nc.tensor.transpose(bank[(0, 1, 6, 7)[e // 2]][:, (e % 2) * S + t * P:(e % 2) * S + t * P + P],
                                               g_y[:, GH * t + e, :], ident)
            last.then_inc(sem("gdn_yT"), 1)

        def gdn_core_scalar(act):
            act.wait_ge(sem("gcol_copied"), 1)
            ACTV(g_exp, g_arg, ACT.Exp).then_inc(sem("gdn_exp"), 1)
            for i in range(4):
                act.wait_ge(sem("grow"), i + 1)
                ACTV(g_eG[:, 4 * i:4 * i + 4, :], psum4(i), ACT.Exp).then_inc(sem("eG_done"), 1)
            act.wait_ge(sem("grow_read"), 1)
            ACTV(flat(g_A), flat(g_A), ACT.Exp, scale=-1.0)
            act.wait_ge(sem("grow_read"), 2)
            ACTV(flat(g_aT), flat(g_aT), ACT.Exp).then_inc(sem("decay_done"), 1)
            for i in range(2):
                for c in range(4):
                    act.wait_ge(sem("gdn_sums"), 4 * i + c + 1)
                    ACTV(flat(g_norm[i])[:, c * 512:(c + 1) * 512], bank[4 + c][:, :], ACT.Sqrt, bias=eps_col)\
                        .then_inc(sem("gdn_root"), 1)
            for k in range(1, LEVELS):
                for t in range(NT):
                    act.wait_ge(sem("gdn_YT"), NT * (k - 1) + t + 1)
                    for j in range(2):
                        last = ACTV(g_YT[:, GH * t + 4 * j:GH * t + 4 * j + 4, :], psum4(2 * t + j), ACT.Copy)
                    last.then_inc(sem("gdn_YT_copied"), 1)
            act.wait_ge(sem("gdn_WT"), 1)
            for j in range(4):
                last = ACTV(g_WT[:, 4 * j:4 * j + 4, :], psum4(j), ACT.Copy)
            last.then_inc(sem("gdn_WT_copied"), 1)
            for t in range(NT):
                act.wait_ge(sem("gdn_O"), 2 * t + 2)
                for j in range(2):
                    last = ACTV(g_osq[:, GH * t + 4 * j:GH * t + 4 * j + 4, :], psum4(2 + 2 * t + j), ACT.Square)
                last.then_inc(sem("gdn_osq"), 1)
            act.wait_ge(sem("gdn_yT"), 1)
            for j in range(2):
                ACTV(mixT[:, 2 * j:2 * j + 2, :], bank[j][:, :].rearrange("p (a b) -> p a b", b=S), ACT.Copy)\
                    .then_inc(sem("gdn_mixT"), 1)

        def gdn_core_vector(dve, ch):
            dve.wait_ge(sem("gcol"), 1)
            ch.step(V.tensor_copy(g_arg, bank[6][:, 64:96]))
            V.tensor_tensor(g_arg[:, NP:2 * NP], g_arg[:, NP:2 * NP], g_arg[:, 0:NP], ALU.subtract)\
                .then_inc(sem("gcol_copied"), 1)
            dve.wait_ge(sem("gcol_copied"), 1)
            for j, (dst, name) in enumerate(((g_A, "low"), (g_aT, "up"))):
                for i in range(NP):
                    dve.wait_ge(sem("eG_done"), i // 4 + 1)
                    last = V.scalar_tensor_tensor(dst[:, i, :], psum4(i // 4)[:, i % 4, :], g_arg[:, i:i + 1],
                                                  const(name), ALU.subtract, ALU.add)
                last.then_inc(sem("grow_read"), 1)
            dve.wait_ge(sem("gdn_exp"), 1)
            dve.wait_ge(sem("beta_done"), 1)
            ch.step(V.tensor_tensor(g_bk, g_beta, g_exp[:, 0:NP], ALU.mult))
            for i, src in enumerate((g_q, g_k)):
                dve.wait_ge(sem("gdn_root"), 4 * (i + 1))
                ch.step(V.reciprocal(flat(g_norm[i]), flat(g_norm[i])))
                V.scalar_tensor_tensor(flat(src), flat(src), 1.0 if i else P ** -0.5, flat(g_norm[i]),
                                       ALU.mult, ALU.mult).then_inc(sem("qk_normed"), 1)
            dve.wait_ge(sem("decay_done"), 1)
            for i in range(NP):
                dve.wait_ge(sem("gdn_kk"), i // 4 + 1)
                last = V.scalar_tensor_tensor(g_A[:, i, :], psum4(i // 4)[:, i % 4, :], g_beta[:, i:i + 1],
                                              g_A[:, i, :], ALU.mult, ALU.mult)
                if i % 4 == 3:
                    last.then_inc(sem("gdn_A"), 1)
            dve.wait_ge(sem("gdn_A"), 4)
            for j in range(4):
                dve.wait_ge(sem("gdn_qk"), j + 1)
                V.tensor_tensor(g_aT[:, 4 * j:4 * j + 4, :], psum4(4 + j), g_aT[:, 4 * j:4 * j + 4, :], ALU.mult)\
                    .then_inc(sem("gdn_aT"), 1)
            for j in range(4):
                dve.wait_ge(sem("gdn_kvT"), j + 1)
                V.tensor_tensor(g_kb[:, 4 * j:4 * j + 4, :], psum4(j), over_heads(g_bk[:, 4 * j:4 * j + 4], 4, P),
                                ALU.mult)
                V.tensor_tensor(g_kd[:, 4 * j:4 * j + 4, :], psum4(j),
                                over_heads(g_exp[:, NP + 4 * j:NP + 4 * j + 4], 4, P), ALU.mult)\
                    .then_inc(sem("gdn_kv"), 1)
            for j in range(4):
                dve.wait_ge(sem("gdn_kvT"), 4 + j + 1)
                V.tensor_tensor(g_vb[:, 4 * j:4 * j + 4, :], psum4(4 + j), over_heads(g_beta[:, 4 * j:4 * j + 4], 4, P),
                                ALU.mult).then_inc(sem("gdn_kv"), 1)
            for t in range(NT):
                if t == 0:
                    dve.wait_ge(sem("gdn_level"), 1)
                sl = slice(GH * t, GH * t + GH)
                ch.add(V.scalar_tensor_tensor(g_T[:, sl, :], g_Ak[0][:, sl, :], -1.0, per_head(ident, GH, P),
                                              ALU.mult, ALU.add))
                dve.wait_ge(sem("gdn_A0T"), 2 * t + 2)
                for j in range(2):
                    b = 2 * t + j
                    last = V.scalar_tensor_tensor(g_TT[:, 4 * b:4 * b + 4, :], psum4(b), -1.0, per_head(ident, 4, P),
                                                  ALU.mult, ALU.add)
                last.then_inc(sem("gdn_T"), 1)
            for k in range(1, LEVELS):
                for t in range(NT):
                    dve.wait_ge(sem("gdn_Z"), NT * (k - 1) + t + 1)
                    dve.wait_ge(sem("gdn_T"), NT * k)
                    for j in range(2):
                        sl = slice(GH * t + 4 * j, GH * t + 4 * j + 4)
                        if k < LEVELS - 1:
                            V.tensor_tensor(g_T[:, sl, :], g_T[:, sl, :], psum4(4 + j), ALU.subtract)
                        last = V.tensor_tensor(g_TT[:, sl, :], g_TT[:, sl, :], psum4(6 + j), ALU.subtract)
                    last.then_inc(sem("gdn_T"), 1)
            dve.wait_ge(sem("gdn_U"), 1)
            for j in range(4):
                last = V.tensor_copy(g_U[:, 4 * j:4 * j + 4, :], psum4(4 + j))
            last.then_inc(sem("gdn_vn"), 1)
            for c in range(4):
                t, r = c // 2, slice(CHUNK * (c % 2), CHUNK * (c % 2) + CHUNK)
                if c:
                    dve.wait_ge(sem("gdn_WS"), c)
                    for j in range(2):
                        sl = slice(GH * t + 4 * j, GH * t + 4 * j + 4)
                        last = V.tensor_tensor(g_U[r, sl, :], g_U[r, sl, :], psum4(j)[r, :, :], ALU.subtract)
                    last.then_inc(sem("gdn_vn"), 1)
                if c < 3:
                    dve.wait_ge(sem("gdn_kv_state"), c + 1)
                    if c == 0:
                        for j in range(2):
                            last = V.tensor_copy(g_S[:, 4 * j:4 * j + 4, :], psum4(6 + j))
                    else:
                        dve.wait_ge(sem("gdn_O"), c + 1)
                        for e in range(GH):
                            i = GH * t + e
                            end = CHUNK * (c % 2) + CHUNK - 1
                            last = V.scalar_tensor_tensor(g_S[:, e, :], g_S[:, e, :], g_eG[:, i, end:end + 1],
                                                          psum4(6 + e // 4)[:, e % 4, :], ALU.mult, ALU.add)
                    last.then_inc(sem("gdn_S"), 1)
                    dve.wait_ge(sem("gdn_S"), c + 1)
            for t in range(NT):
                sl = slice(GH * t, GH * t + GH)
                dve.wait_ge(sem("gdn_osq"), t + 1)
                ch.step(V.tensor_reduce(o_ssq[:, sl], g_osq[:, sl, :], AX.X, ALU.add))
                V.tensor_scalar(o_ssq[:, sl], o_ssq[:, sl], 1.0 / P, EPS, ALU.mult, ALU.add)\
                    .then_inc(sem("head_var"), 1)
                dve.wait_ge(sem("head_rstd"), t + 2)
                for j in range(2):
                    s4 = slice(GH * t + 4 * j, GH * t + 4 * j + 4)
                    ch.add(V.tensor_tensor(g_y[:, s4, :], psum4(2 + 2 * t + j), over_heads(o_rstd[:, s4], 4, P),
                                           ALU.mult))
                ch.sync()
                ch.step(V.tensor_tensor(g_y[:, sl, :], g_y[:, sl, :], per_head(const("out_norm"), GH, P), ALU.mult))
                V.tensor_tensor(g_y[:, sl, :], g_y[:, sl, :], g_gate[:, sl, :], ALU.mult).then_inc(sem("gdn_y"), 1)
            dve.wait_ge(sem("gdn_yT"), 1)
            for j in range(2):
                V.tensor_copy(mixT[:, 4 + 2 * j:6 + 2 * j, :], bank[6 + j][:, :].rearrange("p (a b) -> p a b", b=S))\
                    .then_inc(sem("gdn_mixT"), 1)

        def gdn_core_pool(pool):
            pool.wait_ge(sem("qk_normed"), 1)
            pool.wait_ge(sem("eG_done"), 4)
            for t in range(NT):
                G.tensor_tensor(g_qdT[:, GH * t:GH * t + GH, :], g_q[:, :, t * P:(t + 1) * P],
                                g_eG[:, GH * t:GH * t + GH, :], ALU.mult).then_inc(sem("gdn_qd"), 1)
            pool.wait_ge(sem("gdn_A"), 4)
            for k in range(LEVELS):
                if k < 2:
                    pool.wait_ge(sem("gdn_kvT"), 8)
                else:
                    pool.wait_ge(sem("gdn_Z"), NT * (k - 2) + 0 if k == 2 else NT * (k - 2))
                if k == 2:
                    pool.wait_ge(sem("gdn_A0T"), 4)
                    pool.wait_ge(sem("gdn_T"), NT)
                G.tensor_tensor(g_Ak[k % 2], g_A, per_head(const("level", 6, P)[:, k, :], NP, P), ALU.mult)\
                    .then_inc(sem("gdn_level"), 1)
            for t in range(NT):
                pool.wait_ge(sem("head_var"), t + 2)
                G.tensor_tensor(o_rstd[:, GH * t:GH * t + GH], o_ssq[:, GH * t:GH * t + GH], minus_half, ALU.pow)\
                    .then_inc(sem("head_rstd"), 1)

        sel = tin(NT, EXPERTS + 1)
        logits, top8, m_ge, m_gt = tin(NT, 8), tin(NT, 8), tin(NT, 8), tin(NT, 8)
        m_eq, m_cum, gates, n_gt = tin(NT, 8), tin(NT, 8), tin(NT, 8), tin(NT, 4)

        def router_tensor(pe):
            norm_ready(pe, 3)
            for t in range(NT):
                for k in range(KD):
                    last = MM(bank[0][:, 8 * t:8 * t + 8], xnT[:, k, t * P:(t + 1) * P],
                              const("router", KD, EXPERTS)[:, k, :], start=(k == 0), stop=(k == KD - 1))
            last.then_inc(sem("logits"), 1)

        def router_scalar(act):
            act.wait_ge(sem("top_diff"), 1)
            ACTV(gates, gates, ACT.Exp).then_inc(sem("top_exp"), 1)

        def router_vector(dve, ch):
            dve.wait_ge(sem("logits"), 1)
            ch.step(V.tensor_copy(logits, bank[0][:, 0:16].rearrange("p (t e) -> p t e", t=NT)))
            for t in range(NT):
                ch.add(V.max(top8[:, t, :], logits[:, t, :]))
            ch.sync()
            for t in range(NT):
                l, v1, v2 = logits[:, t, :], top8[:, t, 0:1], top8[:, t, 1:2]
                ch.add(V.tensor_scalar(gates[:, t, :], l, v1, None, ALU.subtract))
                ch.add(V.tensor_scalar(m_gt[:, t, :], l, v2, None, ALU.is_gt))
                ch.add(V.tensor_scalar(m_eq[:, t, :], l, v2, None, ALU.is_equal))
            ch.sync()
            V.tensor_copy(m_ge[:, :, 0:1], m_eq[:, :, 0:1]).then_inc(sem("top_diff"), 1)
            dve.wait_ge(sem("top_diff"), 1)
            for t in range(NT):
                ch.add(V.tensor_reduce(n_gt[:, t, 0:1], m_gt[:, t, :], AX.X, ALU.add))
                ch.add(V.tensor_tensor_scan(m_cum[:, t, :], const("ones")[:, 0:8], m_eq[:, t, :], 0.0,
                                            ALU.mult, ALU.add))
            ch.sync()
            for t in range(NT):
                ch.add(V.tensor_scalar(m_ge[:, t, :], m_cum[:, t, :], n_gt[:, t, 0:1], 2.0, ALU.add, ALU.is_le))
            ch.sync()
            ch.step(V.tensor_tensor(m_eq, m_eq, m_ge, ALU.mult))
            V.memset(sel[:, :, 8:9], 0.0).then_inc(sem("pads_set"), 1)
            V.tensor_tensor(sel[:, :, 0:8], m_eq, m_gt, ALU.add).then_inc(sem("sel_done"), 1)
            dve.wait_ge(sem("sel_done"), 1)
            dve.wait_ge(sem("top_exp"), 1)
            ch.step(V.tensor_tensor(gates, gates, sel[:, :, 0:8], ALU.mult))
            for t in range(NT):
                ch.add(V.tensor_reduce(n_gt[:, t, 1:2], gates[:, t, :], AX.X, ALU.add))
            ch.sync()
            ch.step(V.reciprocal(n_gt[:, :, 1:2], n_gt[:, :, 1:2]))
            for t in range(NT):
                ch.add(V.tensor_scalar(gates[:, t, :], gates[:, t, :], n_gt[:, t, 1:2], None, ALU.mult))
            ch.sync()

        def unit_ready_in(pe, base, e, i):
            n = base + i
            pe.wait_ge(sem(f"unit_in{n % RING}"), e * (16 * FFE_UNITS // RING) + 16 * (n // RING + 1))

        hidT = bview(0, 4, S)
        silu_g = bview(1, 2, S)

        def gate_up_T(n, q, dst, acts):
            for k in range(KD):
                w = ring[(n + k // 4) % RING][:, :].rearrange("p (k c) -> p k c", k=4)
                last = MM(dst, w[:, k % 4, q * P:(q + 1) * P], acts[:, k, :], start=(k == 0), stop=(k == KD - 1))
            return last

        def moe_tensor(pe):
            base, steps = AT["moe"], FFE_STEPS
            gate, down = swiglu_order(steps)
            with pe.Fori(0, EXPERTS) as e:
                def down_product(s):
                    unit_ready_in(pe, base, e, down[s])
                    pe.wait_ge(sem("moe_hidden"), e * (2 * steps) + (2 * s + 2))
                    if s == 0:
                        pe.wait_ge(sem("moe_added"), e + 1)
                    product_rows(base + down[s], hidT[:, 2 * (s % 2):2 * (s % 2) + 2, :], s == 0, s == steps - 1)\
                        .then_inc(sem("unit_used"), 1)

                for s in range(steps):
                    for u in range(2):
                        unit_ready_in(pe, base, e, gate[s] + u)
                    for which in range(2):
                        for j in range(2):
                            if s and not which:
                                pe.wait_ge(sem("moe_hidden"), e * (2 * steps) + (2 * s - 1 + j))
                            last = gate_up_T(base + gate[s], 2 * which + j, bank[2 * which + j][:, 0:S], xnT)
                            if which and j:
                                last.then_inc(sem("unit_used"), 2)
                            else:
                                last.then_inc(sem("moe_up" if which else "moe_gate"), 1)
                    if s:
                        down_product(s - 1)
                down_product(steps - 1)

        def moe_scalar(act):
            base, steps = AT["moe"], FFE_STEPS
            gate, _ = swiglu_order(steps)
            with act.Fori(0, EXPERTS) as e:
                for s in range(steps):
                    for j in range(2):
                        act.wait_ge(sem("moe_gate"), e * (2 * steps) + (2 * s + j + 1))
                        if s or j:
                            act.wait_ge(sem("moe_hidden"), e * (2 * steps) + max(2 * s + j - 1, 1))
                        else:
                            act.wait_ge(sem("moe_added"), e + 1)
                        ACTV(silu_g[:, j, :], bank[j][:, 0:S], ACT.Silu).then_inc(sem("moe_silu"), 1)
                ACTV(counts[:, 1:2], counts[:, 0:1], ACT.Copy).then_inc(sem("split_high"), FFE_UNITS)
            dense_done(act)
            for i in range(AHEAD):
                split_high_in(act, EXPERTS - 1, FFE_UNITS + i)

        def moe_vector(dve, ch):
            base, steps = AT["moe"], FFE_STEPS
            gate, down = swiglu_order(steps)
            with dve.Fori(0, EXPERTS) as e:
                for s in range(steps):
                    for j in range(2):
                        dve.wait_ge(sem("moe_silu"), e * (2 * steps) + (2 * s + j + 1))
                        if j == 0:
                            dve.wait_ge(sem("moe_up"), e * steps + (s + 1))
                        else:
                            dve.wait_ge(sem("unit_used"), e * FFE_UNITS + (base + gate[s] + 2))
                        if s >= 2:
                            dve.wait_ge(sem("unit_used"), e * FFE_UNITS + (base + down[s - 2] + 1))
                        V.tensor_tensor(hidT[:, 2 * (s % 2) + j, :], silu_g[:, j, :], bank[2 + j][:, 0:S], ALU.mult)\
                            .then_inc(sem("moe_hidden"), 1)
                dve.wait_ge(sem("unit_used"), e * FFE_UNITS + (base + FFE_UNITS))
                for t in range(NT):
                    for c in range(2):
                        o = slice(c * 512, (c + 1) * 512)
                        last = V.scalar_tensor_tensor(h[:, t, o], bank[4 + 2 * t + c][:, :],
                                                      gates[:, t, bass.ds(e, 1)], h[:, t, o], ALU.mult, ALU.add)
                last.then_inc(sem("moe_added"), 1)
                V.tensor_copy(counts[:, 2:3], counts[:, 0:1]).then_inc(sem("split_low"), FFE_UNITS)
            dense_done(dve)
            for i in range(AHEAD):
                split_low_in(dve, EXPERTS - 1, FFE_UNITS + i)

        def dense_done(eng):
            eng.wait_ge(sem("moe_added"), EXPERTS + 1)

        slot_of, counts = tin(NT, EXPERTS + 1), tin(EXPERTS + 1)
        s_xT = bview_r(3, KD, P), bview_r(3, KD, P, off=1024)
        s_x = bview(3, KD, P, off=1024)
        s_pick = bview(4, NT, P)
        s_gpick = bview(4, NT, P, off=256)
        s_gpickT = bview(4, NT, P, off=512)
        s_hid = bview(4, 2, 256, off=1024)
        s_silu = bview(4, 2, 256, off=1536)
        s_hidT = bview_r(5, 4, P), bview_r(5, 4, P, off=512)
        s_y = bview(5, D, off=1024)
        GU_UNITS = [swiglu_order(FFE_STEPS)[0][s] for s in range(FFE_STEPS)]
        DOWN_UNITS = swiglu_order(FFE_STEPS)[1]

        def slots_tensor(pe):
            pe.wait_ge(sem("sel_done"), 1)
            MM(bank[1][:, 0:8], const("before"), sel[:, 0, 0:8], start=True, stop=True)
            MM(bank[1][:, 8:16], const("ones"), sel[:, 0, 0:8], start=True, stop=False)
            MM(bank[1][:, 8:16], const("before"), sel[:, 1, 0:8], start=False, stop=True)
            MM(bank[1][:, 16:24], const("ones"), sel[:, 0, 0:8], start=True, stop=False)
            MM(bank[1][:, 16:24], const("ones"), sel[:, 1, 0:8], start=False, stop=True).then_inc(sem("slots"), 1)

        def slots_vector(dve, ch):
            dve.wait_ge(sem("slots"), 1)
            ch.add(V.tensor_copy(slot_of[:, :, 0:8], bank[1][:, 0:16].rearrange("p (t e) -> p t e", t=NT)))
            ch.step(V.tensor_reduce(counts[:, 0:1], bank[1][:, 16:24], AX.X, ALU.max))
            V.tensor_scalar(crowded[:, :], counts[:, 0:1], float(P), None, ALU.is_gt).then_inc(sem("crowded"), 1)

        def is_crowded(eng):
            eng.wait_ge(sem("crowded"), 1)
            return eng.value_load(crowded[0:1, 0:1], min_val=0, max_val=1)

        def pick(dst, e, weight):
            for t in range(NT):
                last = V.tensor_scalar(dst[:, t, :], const("iota"), slot_of[:, t, bass.ds(e, 1)],
                                       weight[:, t, bass.ds(e, 1)], ALU.is_equal, ALU.mult)
            return last

        def gather(pe):
            for k in range(KD):
                for t in range(NT):
                    last = MM(bank[6 + k // 4][:, (k % 4) * P:(k % 4 + 1) * P], xn[:, t, k * P:(k + 1) * P],
                              s_pick[:, t, :], start=(t == 0), stop=(t == NT - 1))
            last.then_inc(sem("sp_gathered"), 1)

        def gathered(dve, e):
            dve.wait_ge(sem("sp_gathered"), e + 1)
            hi, lo = s_xT
            for j in range(2):
                V.tensor_tensor(s_x[:, 4 * j:4 * j + 4, :], psum4(6 + j),
                                over_heads(const("gain", 8, KD)[:, 3, 4 * j:4 * j + 4], 4, P), ALU.mult)\
                    .then_inc(sem("sp_x_scaled"), 1)
            dve.wait_ge(sem("sp_x_scaled"), e * 3 + 2)
            V.tensor_copy(hi, s_x).then_inc(sem("sp_x_scaled"), 1)
            dve.wait_ge(sem("sp_x_scaled"), e * 3 + 3)
            V.tensor_tensor(lo, s_x, hi.bitcast(F32), ALU.subtract).then_inc(sem("sp_xT"), 1)

        def split_high_in(act, e, i):
            n = AT["moe"] + i
            unit_ready_in(act, AT["moe"], e, i)
            act.wait_ge(sem("unit_used"), e * FFE_UNITS + (n - HI + 1))
            ACTV(buf_r[HI_BUFS[i % HI]][:, :], ring[n % RING][:, :], ACT.Copy)\
                .then_inc(sem("split_high"), 1)

        def split_low_in(dve, e, i):
            n = AT["moe"] + i
            dve.wait_ge(sem("split_high"), e * FFE_UNITS + (SPLITS["moe"] + i + 1))
            V.tensor_tensor(ring_r[n % RING][:, :], ring[n % RING][:, :], buf_r[HI_BUFS[i % HI]][:, :].bitcast(F32),
                            ALU.subtract).then_inc(sem("split_low"), 1)

        def split_ready_in(pe, e, i):
            pe.wait_ge(sem("split_low"), e * FFE_UNITS + (SPLITS["moe"] + i + 1))

        SCATTER_STEPS = (1, 2)

        def scatter(pe, e, t):
            if t == 0:
                pe.wait_ge(sem("sp_y"), 2 * e + 2)
                pe.wait_ge(sem("sp_xT"), e + 1)
            else:
                pe.wait_ge(sem("sp_added"), 2 * e + 2)
            for c in range(2):
                last = MM(bank[6 + c][:, :], s_gpickT[:, t, :], s_y[:, c * 512:(c + 1) * 512], start=True, stop=True)
            last.then_inc(sem("sp_scattered"), 1)

        def add_scattered(dve, e, t):
            dve.wait_ge(sem("sp_scattered"), 2 * e + (t + 1))
            for c in range(2):
                o = slice(c * 512, (c + 1) * 512)
                last = V.tensor_tensor(h[:, t, o], h[:, t, o], bank[6 + c][:, :], ALU.add)
            last.then_inc(sem("sp_added"), 1)

        def sparse_tensor(pe):
            base, steps = AT["moe"], FFE_STEPS
            pe.wait_ge(sem("sp_pick"), 1)
            gather(pe)
            with pe.Fori(0, EXPERTS) as e:
                def gate_up(s, k0):
                    i = GU_UNITS[s] + k0 // 4
                    split_ready_in(pe, e, i)
                    hi, lo = high(base + i, i, 4), low(base + i, i, 4)
                    for k in range(4):
                        last = three_passes(bank[s % 2][:, :], [a[:, k0 + k, :] for a in s_xT],
                                            (hi[:, k, :], lo[:, k, :]), k0 + k == 0, k0 + k == KD - 1)
                    last.then_inc(sem("unit_used"), 1)

                def hidden_T(s):
                    pe.wait_ge(sem("sp_hid"), e * steps + (s + 2))
                    for f in range(2):
                        last = nc.tensor.transpose(bank[2][:, (2 * (s % 2) + f) * P:(2 * (s % 2) + f + 1) * P],
                                                   s_hid[:, s % 2, f * P:(f + 1) * P], ident)
                    last.then_inc(sem("sp_hidT"), 1)

                def down(s):
                    i = DOWN_UNITS[s]
                    split_ready_in(pe, e, i)
                    hi, lo = high(base + i, i, 2), low(base + i, i, 2)
                    pe.wait_ge(sem("sp_hidT_low"), e * steps + (s + 1))
                    if s == 0:
                        pe.wait_ge(sem("sp_y"), 2 * e + 2)
                    for f in range(2):
                        for c in range(2):
                            o = slice(c * 512, (c + 1) * 512)
                            last = three_passes(bank[4 + c][:, :],
                                                [a[:, 2 * (s % 2) + f, :] for a in s_hidT],
                                                (hi[:, f, o], lo[:, f, o]), s == 0 and f == 0,
                                                s == steps - 1 and f == 1)
                    last.then_inc(sem("unit_used"), 1)

                for s in range(steps):
                    if s == 0:
                        pe.wait_ge(sem("sp_xT"), e + 1)
                    gate_up(s, 0)
                    if s:
                        hidden_T(s - 1)
                    gate_up(s, 4)
                    if s:
                        down(s - 1)
                    if s in SCATTER_STEPS:
                        scatter(pe, e, s - 1)
                    if s == 4:
                        pe.wait_ge(sem("sp_gpick"), e + 1)
                        for t in range(NT):
                            last = nc.tensor.transpose(bank[3][:, t * P:(t + 1) * P], s_gpick[:, t, :], ident)
                        last.then_inc(sem("sp_gpickT"), 1)
                    if s == 9:
                        pe.wait_ge(sem("sp_pick"), e + 2)
                        pe.wait_ge(sem("sp_added"), 2 * e + 3)
                        gather(pe)
                hidden_T(steps - 1)
                down(steps - 1)
            for t in range(NT):
                scatter(pe, EXPERTS, t)

        def sparse_scalar(act):
            base, steps = AT["moe"], FFE_STEPS
            for i in range(AHEAD):
                split_high_in(act, 0, i)
            with act.Fori(0, EXPERTS) as e:
                def hidden_high(s):
                    act.wait_ge(sem("sp_hidT"), e * steps + (s + 1))
                    ACTV(s_hidT[0][:, 2 * (s % 2):2 * (s % 2) + 2, :],
                         psum4(2)[:, 2 * (s % 2):2 * (s % 2) + 2, :], ACT.Copy).then_inc(sem("sp_hidT_high"), 1)

                for s in range(steps):
                    split_high_in(act, e, GU_UNITS[s] + AHEAD)
                    if s:
                        hidden_high(s - 1)
                    split_high_in(act, e, GU_UNITS[s] + 1 + AHEAD)
                    act.wait_ge(sem("unit_used"), e * FFE_UNITS + (base + GU_UNITS[s] + 2))
                    if s >= 2:
                        act.wait_ge(sem("sp_hid"), e * steps + s)
                    ACTV(s_silu[:, s % 2, :], bank[s % 2][:, 0:256], ACT.Silu).then_inc(sem("sp_silu"), 1)
                    if s:
                        split_high_in(act, e, DOWN_UNITS[s - 1] + AHEAD)
                    if s == 6:
                        act.wait_ge(sem("sp_gpickT"), e + 1)
                        ACTV(s_gpickT, psum4(3)[:, 0:NT, :], ACT.Copy)
                hidden_high(steps - 1)
                split_high_in(act, e, DOWN_UNITS[steps - 1] + AHEAD)
                act.wait_ge(sem("unit_used"), e * FFE_UNITS + (base + FFE_UNITS))
                ACTV(s_y[:, 0:512], bank[4][:, :], ACT.Copy).then_inc(sem("sp_y"), 1)

        def sparse_vector(dve, ch):
            base, steps = AT["moe"], FFE_STEPS
            for t in range(NT):
                last = V.tensor_scalar(s_pick[:, t, :], const("iota"), slot_of[:, t, 0:1], sel[:, t, 0:1],
                                       ALU.is_equal, ALU.mult)
            last.then_inc(sem("sp_pick"), 1)
            split_low_in(dve, 0, 0)
            gathered(dve, 0)
            for i in range(1, AHEAD):
                split_low_in(dve, 0, i)
            with dve.Fori(0, EXPERTS) as e:
                def hidden_low(s):
                    dve.wait_ge(sem("sp_hidT_high"), e * steps + (s + 1))
                    o = slice(2 * (s % 2), 2 * (s % 2) + 2)
                    V.tensor_tensor(s_hidT[1][:, o, :], psum4(2)[:, o, :], s_hidT[0][:, o, :].bitcast(F32),
                                    ALU.subtract).then_inc(sem("sp_hidT_low"), 1)

                for s in range(steps):
                    split_low_in(dve, e, GU_UNITS[s] + AHEAD)
                    if s:
                        hidden_low(s - 1)
                    split_low_in(dve, e, GU_UNITS[s] + 1 + AHEAD)
                    dve.wait_ge(sem("sp_silu"), e * steps + (s + 1))
                    if s >= 2:
                        dve.wait_ge(sem("sp_hidT"), e * steps + (s - 1))
                    V.tensor_tensor(s_hid[:, s % 2, :], s_silu[:, s % 2, :], bank[s % 2][:, 256:512], ALU.mult)\
                        .then_inc(sem("sp_hid"), 1)
                    if s == steps - 1:
                        gathered(dve, e + 1)
                        hidden_low(s)
                    if s:
                        split_low_in(dve, e, DOWN_UNITS[s - 1] + AHEAD)
                    if s in SCATTER_STEPS:
                        add_scattered(dve, e, s - 1)
                    if s == 3:
                        pick(s_gpick, e, gates).then_inc(sem("sp_gpick"), 1)
                    if s == 6:
                        pick(s_pick, e + 1, sel).then_inc(sem("sp_pick"), 1)
                split_low_in(dve, e, DOWN_UNITS[steps - 1] + AHEAD)
                dve.wait_ge(sem("unit_used"), e * FFE_UNITS + (base + FFE_UNITS))
                V.tensor_copy(s_y[:, 512:1024], bank[5][:, :]).then_inc(sem("sp_y"), 1)
            for t in range(NT):
                add_scattered(dve, EXPERTS, t)

        def experts_tensor(pe):
            slots_tensor(pe)
            with pe.If(is_crowded(pe)):
                moe_tensor(pe)
            with pe.Else():
                sparse_tensor(pe)

        def experts_scalar(act):
            with act.If(is_crowded(act)):
                moe_scalar(act)
            with act.Else():
                sparse_scalar(act)

        def experts_vector(dve, ch):
            slots_vector(dve, ch)
            for i, name in enumerate(("sp_hid", "sp_added", "moe_added")):
                V.memset(counts[:, i + 1:i + 2], 0.0).then_inc(sem(name), 1)
            for room in (s_y, s_gpickT):
                V.memset(room, 0.0).then_inc(sem("sp_y"), 1)
            V.memset(slot_of[:, :, 8:9], 0.0).then_inc(sem("pads_set"), 1)
            dve.wait_ge(sem("pads_set"), 2)
            dve.wait_ge(sem("moe_added"), 1)
            with dve.If(is_crowded(dve)):
                moe_vector(dve, ch)
                V.tensor_copy(n_gt[:, :, 2:3], n_gt[:, :, 1:2]).then_inc(sem("h_done"), NT)
            with dve.Else():
                sparse_vector(dve, ch)
                dve.wait_ge(sem("sp_added"), 2 * EXPERTS + 3)
                V.tensor_copy(n_gt[:, :, 2:3], n_gt[:, :, 1:2]).then_inc(sem("h_done"), NT)

        mem_rows = bview(8, NT, D)
        memT = bview(7, KD, S)
        mem_kT = bview(3, MH, S)
        mem_v = bview(3, NT, 512, off=1024)
        hg_q, hg_k = bview(0, MH, S), bview(0, MH, S, off=1024)
        hg_qs, hg_b = bview(1, MH, S), bview(1, MH, S, off=1024)
        hg_ks, hg_kl = bview(2, MH, S), bview(2, MH, S, off=1024)
        hg_kl_rows, hg_scores = bview(4, 8, P), bview(4, 8, P, off=1024)
        hg_v, hg_gate = bview(5, NT, 512), bview(5, NT, 512, off=1024)
        hg_sq, hg_y = bview(2, 8, P), bview(2, 8, P, off=1024)
        hg_S = [buf[11][:, i * 512:(i + 1) * 512].rearrange("p (a b) -> p a b", b=P) for i in range(3)]
        xn_a = xn[:, 0, :].rearrange("p (a b) -> p a b", b=S)
        xn_b = xn[:, 1, :].rearrange("p (a b) -> p a b", b=S)
        dil_q = [bview(6, MH, S), bview(7, MH, S, off=1024), xn_a]
        dil_k = [bview(6, MH, S, off=1024), bview(8, MH, S), xn_b]
        dil_v = [bview(7, NT, 512), bview(8, NT, 512, off=1024), bview(10, NT, 512)]
        mem_q = bview(10, MH, S, off=1024)
        y_hgT, y_dilT, y_memT = bview(0, MH, S, off=1024), bview(4, MH, S), bview(5, MH, S)
        gl = [bview(6 + i, KD, S) for i in range(3)]
        mixed = bview(10, KD, S)
        mix_t = bview(11, 2, S)
        lb, one_lb, lg_d, lg_e = tin(MH), tin(MH), tin(2 * MH), tin(2 * MH)
        hg_ssq, hg_rstd = tin(8), tin(8)

        def product_any(n, kind, j, dst, acts):
            return product_T(n, j, dst, acts) if kind == "T" else product(n, j, dst, acts)

        def in_jobs(base, parts):
            jobs = []
            for kind, units in parts:
                for u in range(units):
                    for j in range(2):
                        jobs.append((base, kind, j))
                    base += 1
            return jobs

        def jobs_tensor(pe, past, jobs, acts, banks):
            for i, (n, kind, j) in enumerate(jobs):
                unit_ready(pe, n)
                if i >= len(banks):
                    pe.wait_ge(sem("job_read"), past + i - len(banks) + 1)
                last = product_any(n, kind, j, bank[banks[i % len(banks)]][:, 0:S], acts)
                last.then_inc(sem("unit_used" if j else "half_done"), 1)

        def jobs_scalar(act, past, jobs, banks, first, outs):
            for i, (dst, func, scale, bias) in enumerate(outs, first):
                n, _, j = jobs[i]
                if j:
                    act.wait_ge(sem("unit_used"), n + 1)
                else:
                    half_done(act, n)
                src = bank[banks[i % len(banks)]][:, 0:S]
                if bias is None:
                    ins = ACTV(dst, src, func, scale=scale)
                else:
                    ins = ACTV(dst, src, func, scale=scale, bias=bias)
                ins.then_inc(sem("job_read"), 1)

        def outs_T(dst, func=ACT.Copy, scale=1.0):
            return [(dst[:, c, :], func, scale, None) for c in range(MH)]

        def outs_rows(dst, func=ACT.Copy):
            return [(dst[:, t, u * 256:(u + 1) * 256], func, 1.0, None) for u in range(2) for t in range(NT)]

        kv_jobs = in_jobs(AT["mem_kv"], [("T", 2), ("rows", 2)])
        kv_outs = outs_T(mem_kT) + outs_rows(mem_v)
        hg_jobs = in_jobs(AT["hg_in"], [("T", 4), ("rows", 4)] + [("T", 4), ("rows", 2)] * DIL + [("T", 2)])
        hg_outs = outs_T(hg_q, ACT.Silu) + outs_T(hg_k, ACT.Sigmoid) + outs_rows(hg_v) + outs_rows(hg_gate, ACT.Sigmoid)
        dil_outs = []
        for g in range(DIL):
            dil_outs += outs_T(dil_q[g], scale=P ** -0.5) + outs_T(dil_k[g]) + outs_rows(dil_v[g])
        dil_outs += outs_T(mem_q, scale=P ** -0.5)
        gl_jobs = in_jobs(AT["gl_in"], [("T", 12)])
        gl_outs = [(gl[i // KD][:, i % KD, :], ACT.Sigmoid, 1.0, const("b_gate")[:, i:i + 1]) for i in range(24)]
        FOUR = (0, 1, 2, 3)
        JOBS_KV, JOBS_HG, JOBS_GL = 0, len(kv_jobs), len(kv_jobs) + len(hg_jobs)

        def chunks(a):
            return flat(a).rearrange("p (a b) -> p a b", b=CHUNK)

        def hg_prepare(dve, ch):
            l = const("hg_logits")
            ch.step(V.tensor_tensor(lb, l[:, 0:MH], l[:, MH:2 * MH], ALU.max))
            ch.step(V.tensor_tensor(lg_d[:, 0:MH], l[:, 0:MH], lb, ALU.subtract))
            V.tensor_tensor(lg_d[:, MH:2 * MH], l[:, MH:2 * MH], lb, ALU.subtract).then_inc(sem("lb_arg"), 1)
            dve.wait_ge(sem("lb_exp"), 1)
            ch.step(V.tensor_tensor(one_lb, lg_e[:, 0:MH], lg_e[:, MH:2 * MH], ALU.add))
            ch.step(V.reciprocal(one_lb, one_lb))
            ch.step(V.tensor_tensor(lb, lg_e[:, 0:MH], one_lb, ALU.mult))
            ch.step(V.tensor_scalar(one_lb, lb, -1.0, 1.0, ALU.mult, ALU.add))

        def hg_prepare_scalar(act):
            act.wait_ge(sem("lb_arg"), 1)
            ACTV(lg_e, lg_d, ACT.Exp).then_inc(sem("lb_exp"), 1)

        def hg_decay_scalar(act):
            act.wait_ge(sem("hg_f"), 1)
            ACTV(flat(hg_qs), flat(hg_k), ACT.Ln).then_inc(sem("hg_ln"), 1)
            act.wait_ge(sem("hg_sums"), 1)
            ACTV(flat(hg_ks), flat(hg_qs), ACT.Exp, scale=-1.0).then_inc(sem("hg_exp"), 1)
            ACTV(flat(hg_kl), flat(hg_kl), ACT.Exp).then_inc(sem("hg_exp"), 1)
            act.wait_ge(sem("hg_exp"), 1)
            ACTV(flat(hg_qs), flat(hg_qs), ACT.Exp).then_inc(sem("hg_exp"), 1)
            ACTV(flat(hg_b), flat(hg_b), ACT.Exp).then_inc(sem("hg_exp"), 1)

        def hg_decay_vector(dve, ch):
            dve.wait_ge(sem("job_read"), JOBS_HG + 16)
            ch.add(V.memset(flat(hg_scores), 0.0))
            for c in range(MH):
                last = V.tensor_scalar(hg_k[:, c, :], hg_k[:, c, :], one_lb[:, c:c + 1], lb[:, c:c + 1],
                                       ALU.mult, ALU.add)
            last.then_inc(sem("hg_f"), 1)
            dve.wait_ge(sem("hg_ln"), 1)
            ch.add(V.tensor_scalar(flat(hg_k), flat(hg_k), -1.0, 1.0, ALU.mult, ALU.add))
            for c in range(MH):
                ch.add(V.tensor_tensor_scan(hg_b[:, c, :], const("reset"), hg_qs[:, c, :], 0.0, ALU.mult, ALU.add))
            ch.sync()
            b = chunks(hg_b)
            mid = b[:, :, CHUNK // 2 - 1:CHUNK // 2].broadcast_to([P, 16, CHUNK])
            end = b[:, :, CHUNK - 1:CHUNK].broadcast_to([P, 16, CHUNK])
            V.tensor_tensor(chunks(hg_qs), b, mid, ALU.subtract)
            V.tensor_tensor(chunks(hg_kl), end, b, ALU.subtract).then_inc(sem("hg_sums"), 1)
            dve.wait_ge(sem("hg_exp"), 1)
            ch.add(V.tensor_tensor(flat(hg_ks), flat(hg_ks), flat(hg_k), ALU.mult))
            dve.wait_ge(sem("hg_exp"), 2)
            ch.add(V.tensor_tensor(flat(hg_kl), flat(hg_kl), flat(hg_k), ALU.mult))
            dve.wait_ge(sem("hg_exp"), 3)
            ch.add(V.tensor_tensor(flat(hg_qs), flat(hg_qs), flat(hg_q), ALU.mult))
            dve.wait_ge(sem("hg_exp"), 4)
            ch.sync()
            V.tensor_tensor(flat(hg_q), flat(hg_q), flat(hg_b), ALU.mult).then_inc(sem("hg_factors"), 1)

        def hg_tensor(pe):
            pe.wait_ge(sem("hg_factors"), 1)
            pe.wait_ge(sem("job_read"), JOBS_HG + len(hg_jobs))
            for i in range(8):
                t, e = i // MH, i % MH
                last = nc.tensor.transpose(bank[i // 4][:, e * P:(e + 1) * P], hg_kl[:, e, t * P:(t + 1) * P], ident)
            last.then_inc(sem("hg_klT"), 1)
            for i in range(8):
                t, e = i // MH, i % MH
                last = MM(bank[2 + i // 4][:, e * P:(e + 1) * P], hg_ks[:, e, t * P:(t + 1) * P],
                          hg_qs[:, e, t * P:(t + 1) * P], start=True, stop=True)
            last.then_inc(sem("hg_ST"), 1)
            pe.wait_ge(sem("hg_kl_rows"), 1)
            for c in range(3):
                t, r = c // 2, slice(CHUNK * (c % 2), CHUNK * (c % 2) + CHUNK)
                for e in range(MH):
                    last = MM(bank[4 + c][:, e * P:(e + 1) * P], hg_kl_rows[r, MH * t + e, :],
                              hg_v[r, t, e * P:(e + 1) * P], start=True, stop=True)
            last.then_inc(sem("hg_kv"), 1)
            pe.wait_ge(sem("hg_masked"), 1)
            pe.wait_ge(sem("hg_states"), 1)
            for i in range(8):
                t, e = i // MH, i % MH
                dst = bank[t][:, e * P:(e + 1) * P]
                MM(dst, hg_scores[:, i, :], hg_v[:, t, e * P:(e + 1) * P], start=True, stop=True)
                for c in (2 * t, 2 * t + 1):
                    if c:
                        r = slice(CHUNK * (c % 2), CHUNK * (c % 2) + CHUNK)
                        last = MM(bank[t][r, e * P:(e + 1) * P],
                                  hg_q[:, e, c * CHUNK:(c + 1) * CHUNK], hg_S[c - 1][:, e, :],
                                  start=False, stop=True, skip_group_check=True)
            last.then_inc(sem("hg_o"), 1)
            pe.wait_ge(sem("hg_y"), 1)
            for i in range(8):
                t, e = i // MH, i % MH
                last = nc.tensor.transpose(bank[2 + e // 2][:, (e % 2) * S + t * P:(e % 2) * S + (t + 1) * P],
                                           hg_y[:, i, :], ident)
            last.then_inc(sem("hg_yT"), 1)

        def hg_scalar(act):
            act.wait_ge(sem("hg_o"), 1)
            for t in range(NT):
                last = ACTV(hg_sq[:, MH * t:MH * t + MH, :], psum4(t), ACT.Square)
            last.then_inc(sem("hg_osq"), 1)

        def hg_vector(dve, ch):
            dve.wait_ge(sem("hg_klT"), 1)
            for j in range(2):
                last = V.tensor_copy(hg_kl_rows[:, 4 * j:4 * j + 4, :], psum4(j))
            last.then_inc(sem("hg_kl_rows"), 1)
            dve.wait_ge(sem("hg_ST"), 1)
            mask = per_head(const("cum").bitcast(U32), 4, P)
            for j in range(2):
                last = V.copy_predicated(hg_scores[:, 4 * j:4 * j + 4, :], mask, psum4(2 + j))
            last.then_inc(sem("hg_masked"), 1)
            dve.wait_ge(sem("hg_kv"), 1)
            ch.step(V.tensor_copy(hg_S[0], psum4(4)))
            for c in (1, 2):
                for e in range(MH):
                    end = (c + 1) * CHUNK - 1
                    last = V.scalar_tensor_tensor(hg_S[c][:, e, :], hg_S[c - 1][:, e, :], hg_b[:, e, end:end + 1],
                                                  psum4(4 + c)[:, e, :], ALU.mult, ALU.add)
                    if c == 1:
                        ch.add(last)
                ch.sync()
            last.then_inc(sem("hg_states"), 1)
            dve.wait_ge(sem("hg_osq"), 1)
            ch.step(V.tensor_reduce(hg_ssq, hg_sq, AX.X, ALU.add))
            V.tensor_scalar(hg_ssq, hg_ssq, 1.0 / P, EPS, ALU.mult, ALU.add).then_inc(sem("head_var"), 1)
            dve.wait_ge(sem("head_rstd"), NT + 2)
            for t in range(NT):
                ch.add(V.tensor_tensor(hg_y[:, MH * t:MH * t + MH, :], psum4(t),
                                       over_heads(hg_rstd[:, MH * t:MH * t + MH], MH, P), ALU.mult))
            ch.sync()
            ch.step(V.tensor_tensor(hg_y, hg_y, per_head(const("hg_norm"), 8, P), ALU.mult))
            V.tensor_tensor(hg_y, hg_y, flat(hg_gate).rearrange("p (a b) -> p a b", b=P), ALU.mult)\
                .then_inc(sem("hg_y"), 1)
            dve.wait_ge(sem("hg_yT"), 1)
            for j in range(2):
                V.tensor_copy(y_hgT[:, 2 * j:2 * j + 2, :], bank[2 + j][:, :].rearrange("p (a b) -> p a b", b=S))\
                    .then_inc(sem("hg_out"), 1)

        def hg_pool(pool):
            pool.wait_ge(sem("head_var"), NT + 2)
            G.tensor_tensor(hg_rstd, hg_ssq, minus_half, ALU.pow).then_inc(sem("head_rstd"), 1)

        def att2_units():
            units = []
            for t in range(NT):
                w = (t + 1) * P
                q = slice(t * P, (t + 1) * P)
                for e in range(MH):
                    units.append(dict(
                        score=[(g * w, w, dil_q[g][:, e, q], dil_k[g][:, e, 0:w]) for g in range(DIL)],
                        mask=[(g * w, w, const("dist", DIL, 2 * P)[:, g, 2 * P - w:2 * P], SLOPES[MH * g + e])
                              for g in range(DIL)],
                        spans=[(0, DIL * w)], block=lambda b: b * P, sink=None,
                        values=[dil_v[g][:, b, e * P:(e + 1) * P] for g in range(DIL) for b in range(t + 1)],
                        rows=(0, P), out=y_dilT[:, e, q]))
                    units.append(dict(
                        score=[(0, S, mem_q[:, e, q], mem_kT[:, e, :])], mask=[(0, S, None, None)],
                        spans=[(0, S)], block=lambda b: b * P, sink=None,
                        values=[mem_v[:, b, e * P:(e + 1) * P] for b in range(2)],
                        rows=(0, P), out=y_memT[:, e, q]))
            return units

        att2 = att2_units()

        def att2_before(pe):
            pe.wait_ge(sem("hg_out"), 2)

        def branch_tensor(pe):
            pe.wait_ge(sem("att_out"), len(att0) + len(att2))
            for i in range(24):
                b, d = i // KD, i % KD
                n = AT["branch"] + i // 4
                unit_ready(pe, n)
                w = ring[n % RING][:, :].rearrange("p (k c) -> p k c", k=4)
                if i >= 4:
                    pe.wait_ge(sem("branch_read"), i - 3)
                else:
                    pe.wait_ge(sem("job_read"), JOBS_GL + 24)
                acts = (y_hgT, y_dilT, y_memT)[b]
                for k in range(4):
                    last = MM(bank[i % 4][:, 0:S], w[:, k, (i % 4) * P:(i % 4 + 1) * P], acts[:, k, :],
                              start=(k == 0), stop=(k == 3))
                last.then_inc(sem("unit_used" if i % 4 == 3 else "branch_done"), 1)

        def branch_vector(dve, ch):
            dve.wait_ge(sem("job_read"), JOBS_GL + 24)
            for i in range(24):
                b, d = i // KD, i % KD
                if i % 4 == 3:
                    dve.wait_ge(sem("unit_used"), AT["branch"] + i // 4 + 1)
                else:
                    dve.wait_ge(sem("branch_done"), 3 * (i // 4) + i % 4 + 1)
                if b == 0:
                    V.tensor_tensor(mixed[:, d, :], gl[b][:, d, :], bank[i % 4][:, 0:S], ALU.mult)\
                        .then_inc(sem("branch_read"), 1)
                else:
                    ins = V.tensor_tensor(mix_t[:, i % 2, :], gl[b][:, d, :], bank[i % 4][:, 0:S], ALU.mult)
                    ins.then_inc(sem("branch_read"), 1)
                    dve.wait_ge(sem("branch_read"), i + 1)
                    ins = V.tensor_tensor(mixed[:, d, :], mixed[:, d, :], mix_t[:, i % 2, :], ALU.add)
                    if b == 2:
                        ins.then_inc(sem("mixed_done"), 1)
                    else:
                        ch.add(ins)
                if i % KD == KD - 1:
                    ch.sync()

        def load_post(act, i):
            act.dma_start(post_gain, post_d[i, :, :]).then_inc(sem("post_in"), 16)

        block = ctx.enter_context(nc.Block())

        @block.sync
        def _(sp):
            sp.dma_start(small[:, :], small_d).then_inc(sem("small_in"), 16)
            sp.dma_start(h[:, :, :], x_d.rearrange("(t p) d -> p t d", p=P)).then_inc(sem("x_in"), 16)
            for s in range(RING):
                sp.dma_start(ring[s][:, :], w_d[s, :, :]).then_inc(sem(f"unit_in{s}"), 16)
            last_unit = {1: AT["ffn0"], 2: AT["gdn_in"], 3: AT["moe"], 4: AT["ffn1"], 5: AT["mem_kv"], 6: AT["ffn2"]}.get(upto, UNITS)
            whole = max(last_unit // RING, 2)
            with sp.Fori(1, whole) as g:
                for s in range(RING):
                    sp.wait_ge(sem("unit_used"), g * RING + (s + 1 - RING))
                    sp.dma_start(ring[s][:, :], w_d[g * RING + s, :, :]).then_inc(sem(f"unit_in{s}"), 16)
            for n in range(whole * RING, last_unit):
                sp.wait_ge(sem("unit_used"), n - RING + 1)
                sp.dma_start(ring[n % RING][:, :], w_d[n, :, :]).then_inc(sem(f"unit_in{n % RING}"), 16)
            h_ready(sp, min(upto, 7))
            sp.dma_start(out_d.rearrange("(t p) d -> p t d", p=P), h[:, :, :]).then_inc(sem("out_written"), 16)
            sp.wait_ge(sem("out_written"), 16)

        @block.tensor
        def _(pe):
            pe.wait_ge(sem("small_in"), 16)
            norm_transpose(pe, 0)
            mix0_tensor(pe)
            att_tensor(pe, 0, att0, att0_before)

            def mix0_ready(pe):
                pe.wait_ge(sem("att_out"), len(att0))
                pe.wait_ge(sem("lru_y"), 1)
            out_tensor(pe, AT["mix0_out"], mix0_ready, mixT)
            if upto > 1:
                norm_transpose(pe, 1)
                norm_ready(pe, 1)
                ffn_tensor(pe, PAST["ffn0"], "ffn0", (xnT_r, x_lo))
            if upto > 2:
                norm_transpose(pe, 2)
                gdn_in_tensor(pe)
                gdn_core_tensor(pe)
                out_tensor(pe, AT["gdn_out"], lambda pe: pe.wait_ge(sem("gdn_mixT"), 4), mixT)
            if upto > 3:
                norm_transpose(pe, 3)
                router_tensor(pe)
                experts_tensor(pe)
            if upto > 4:
                norm_transpose(pe, 4)
                norm_transpose(pe, 5)
                norm_ready(pe, 5)
                ffn_tensor(pe, PAST["ffn1"], "ffn1", (xnT_r, x_lo))
            if upto > 5:
                jobs_tensor(pe, JOBS_KV, kv_jobs, memT, FOUR)
                norm_transpose(pe, 6)
                norm_ready(pe, 6)
                jobs_tensor(pe, JOBS_HG, hg_jobs, xnT, FOUR)
                hg_tensor(pe)
                att_tensor(pe, len(att0), att2, att2_before)
                pe.wait_ge(sem("att_out"), len(att0) + len(att2))
                jobs_tensor(pe, JOBS_GL, gl_jobs, xnT, FOUR)
                branch_tensor(pe)
                out_tensor(pe, AT["mix2_out"], lambda pe: pe.wait_ge(sem("mixed_done"), KD), mixed)
            if upto > 6:
                norm_transpose(pe, 7)
                norm_ready(pe, 7)
                ffn_tensor(pe, PAST["ffn2"], "ffn2", (xnT_r, x_lo))

        @block.scalar
        def _(act):
            act.wait_ge(sem("small_in"), 16)
            softplus_scalar(act, 1, lam_b)
            h_ready(act, 0)
            norm_square(act, 0, h, 0, xnT)
            norm_out_act(act, 0, 0, xnT)
            mix0_scalar(act)
            att_scalar(act, 0, att0)
            if upto > 1:
                act.wait_ge(sem("att_out"), len(att0))
                for i in range(AHEAD):
                    split_high(act, "ffn0", i)
                h_ready(act, 1)
                norm_square(act, 1, h, 1, xnT)
                for i in range(AHEAD, FIRST_SPLITS):
                    split_high(act, "ffn0", i)
                norm_high(act, 1, 1)
                ffn_scalar(act, PAST["ffn0"], "ffn0")
            if upto > 2:
                h_ready(act, 2)
                norm_square(act, 2, h, 2, xnT)
                norm_out_act(act, 2, 2, xnT)
                gdn_in_scalar(act)
                gdn_core_scalar(act)
            if upto > 3:
                h_ready(act, 3)
                act.dma_start(mem_rows, mem_d.rearrange("(t p) d -> p t d", p=P)).then_inc(sem("mem_in"), 16)
                load_post(act, 0)
                norm_square(act, 3, h, 3, xnT)
                norm_out_act(act, 3, 3, xnT)
                router_scalar(act)
                experts_scalar(act)
            if upto > 4:
                h_ready(act, 4)
                act.wait_ge(sem("mem_in"), 16)
                norm_square(act, 4, mem_rows, 7, memT)
                norm_out_act(act, 4, 7, memT)
                norm_square(act, 5, h, 4, xnT)
                for i in range(AHEAD, FIRST_SPLITS):
                    split_high(act, "ffn1", i)
                norm_high(act, 5, 4)
                ffn_scalar(act, PAST["ffn1"], "ffn1")
                post_square(act, 0, AT["mem_kv"])
            if upto > 5:
                hg_prepare_scalar(act)
                jobs_scalar(act, JOBS_KV, kv_jobs, FOUR, 0, kv_outs)
                h_ready(act, 5)
                load_post(act, 1)
                norm_square(act, 6, h, 5, xnT)
                norm_out_act(act, 6, 5, xnT)
                jobs_scalar(act, JOBS_HG, hg_jobs, FOUR, 0, hg_outs)
                hg_decay_scalar(act)
                jobs_scalar(act, JOBS_HG, hg_jobs, FOUR, len(hg_outs), dil_outs)
                hg_scalar(act)
                att_scalar(act, len(att0), att2)
                act.wait_ge(sem("att_out"), len(att0) + len(att2))
                jobs_scalar(act, JOBS_GL, gl_jobs, FOUR, 0, gl_outs)
                if upto > 6:
                    act.wait_ge(sem("mixed_done"), KD)
                    for i in range(AHEAD):
                        split_high(act, "ffn2", i)
                post_square(act, 1, AT["ffn2"])
            if upto > 6:
                h_ready(act, 6)
                load_post(act, 2)
                norm_square(act, 7, h, 6, xnT)
                for i in range(AHEAD, FIRST_SPLITS):
                    split_high(act, "ffn2", i)
                norm_high(act, 7, 6)
                ffn_scalar(act, PAST["ffn2"], "ffn2")
                post_square(act, 2, AT["end"])

        @block.vector
        def _(dve):
            ch = Chain(dve, "dve_step")
            V.memset(eps_col, EPS)
            V.memset(minus_half, -0.5).then_inc(sem("half_set"), 1)
            dve.wait_ge(sem("small_in"), 16)
            softplus_vector_a(ch, const("lam"), lam_b)
            dve.wait_ge(sem("softplus_z"), 1)
            neg_lam = lam_b[0]
            ch.step(V.tensor_scalar(neg_lam, const("lam"), -1.0, None, ALU.mult))
            softplus_vector_b(dve, ch, 1, neg_lam, lam_b, lam_s)
            ch.step(V.tensor_scalar(neg_s, lam_s, -8.0, None, ALU.mult))
            V.tensor_scalar(pos_s, lam_s, 8.0, None, ALU.mult).then_inc(sem("lam_done"), 1)
            dve.wait_ge(sem("x_in"), 16)
            norm_scale(dve, 0, h)
            norm_out_dve(dve, 0, 0, xnT)
            mix0_vector(dve, ch)
            mix0_vector_lru(dve, ch)
            att_vector(dve, ch, 0, att0)
            if upto > 1:
                for i in range(AHEAD):
                    split_low(dve, "ffn0", i)
            add_product(dve, AT["mix0_out"] + 4)
            if upto > 1:
                dve.wait_ge(sem("h_done"), NT)
                norm_scale(dve, 1, h)
                norm_low(dve, 1, 1)
                for i in range(AHEAD, FIRST_SPLITS):
                    split_low(dve, "ffn0", i)
                ffn_vector(dve, ch, PAST["ffn0"], "ffn0")
                add_product(dve, AT["gdn_in"])
            if upto > 2:
                dve.wait_ge(sem("h_done"), 2 * NT)
                norm_scale(dve, 2, h)
                norm_out_dve(dve, 2, 2, xnT)
                gdn_in_vector(dve, ch)
                gdn_core_vector(dve, ch)
                add_product(dve, AT["moe"])
            if upto > 3:
                dve.wait_ge(sem("h_done"), 3 * NT)
                norm_scale(dve, 3, h)
                norm_out_dve(dve, 3, 3, xnT)
                router_vector(dve, ch)
                experts_vector(dve, ch)
            if upto > 4:
                dve.wait_ge(sem("mem_in"), 16)
                norm_scale(dve, 4, mem_rows)
                norm_out_dve(dve, 4, 7, memT)
                dve.wait_ge(sem("h_done"), 4 * NT)
                norm_scale(dve, 5, h)
                norm_low(dve, 5, 4)
                for i in range(AHEAD, FIRST_SPLITS):
                    split_low(dve, "ffn1", i)
                ffn_vector(dve, ch, PAST["ffn1"], "ffn1")
                post_add(dve, ch, 0, 0.5)
            if upto > 5:
                hg_prepare(dve, ch)
                dve.wait_ge(sem("h_done"), 5 * NT)
                norm_scale(dve, 6, h)
                norm_out_dve(dve, 6, 5, xnT)
                hg_decay_vector(dve, ch)
                hg_vector(dve, ch)
                att_vector(dve, ch, len(att0), att2)
                branch_vector(dve, ch)
                if upto > 6:
                    for i in range(AHEAD):
                        split_low(dve, "ffn2", i)
                post_add(dve, ch, 1, 1.0)
            if upto > 6:
                dve.wait_ge(sem("h_done"), 6 * NT)
                norm_scale(dve, 7, h)
                norm_low(dve, 7, 6)
                for i in range(AHEAD, FIRST_SPLITS):
                    split_low(dve, "ffn2", i)
                ffn_vector(dve, ch, PAST["ffn2"], "ffn2")
                post_add(dve, ch, 2, 0.5)

        @block.gpsimd
        def _(pool):
            pool.wait_ge(sem("half_set"), 1)
            norm_pow(pool, 0)
            pool.wait_ge(sem("head_var"), 1)
            G.tensor_tensor(qk_rstd, qk_var, minus_half[:, 0:1].broadcast_to([P, 20]), ALU.pow)\
                .then_inc(sem("head_rstd"), 1)
            if upto > 1:
                norm_pow(pool, 1)
            if upto > 2:
                norm_pow(pool, 2)
                gdn_square(pool)
                gdn_core_pool(pool)
            if upto > 3:
                norm_pow(pool, 3)
            if upto > 4:
                norm_pow(pool, 4)
                norm_pow(pool, 5)
                post_pow(pool, 0)
            if upto > 5:
                norm_pow(pool, 6)
                hg_pool(pool)
                post_pow(pool, 1)
            if upto > 6:
                norm_pow(pool, 7)
                post_pow(pool, 2)


def col(v):
    return v.reshape(-1, P).T


def row(v):
    return np.broadcast_to(v.reshape(1, -1), (P, v.size))


def rows_of(w):
    k, n = w.shape
    return w.reshape(k // P, P, n).transpose(1, 0, 2).reshape(P, -1)


def block_diagonal(w):
    out = np.zeros((4, P, P), w.dtype)
    out[:, 0:64, 0:64] = w[0::2]
    out[:, 64:128, 64:128] = w[1::2]
    return out.transpose(1, 0, 2).reshape(P, -1)


def shape_constants():
    f = np.float32
    i = np.arange(P)
    p, c = i[:, None], i[None, :]
    same = (p // CHUNK) == (c // CHUNK)
    level = [(((p >> k) & 1) == 1) & ((p >> k) == (c >> k) + 1) for k in range(6)]
    q2, k2 = P + p, np.arange(2 * P)[None, :]
    dist = q2 - k2
    steps = [(dist >= 0) & (dist <= 128), (dist >= 0) & (dist % 4 == 0), (dist >= 0) & (dist % 16 == 0)]
    inv = (f(10000.0) ** (-np.arange(32, dtype=f) / f(32))).astype(f)
    ang = np.arange(S, dtype=f)[:, None] * inv[None, :]
    return {
        "ident": np.eye(P), "cum": same & (p <= c), "same": same, "ones": np.ones((P, P)),
        "before": p < c, "iota": row(np.arange(P)),
        "low": np.where(same & (p >= c), 0, BIG), "up": np.where(same & (p <= c), 0, -BIG),
        "level": np.concatenate(level, 1), "band": np.where((dist >= 0) & (dist < P), 0, -BIG),
        "dist": np.concatenate([np.where(m, -dist, -BIG) for m in steps], 1),
        "cos": rows_of(np.cos(ang)), "sin": rows_of(np.sin(ang)), "reset": row((np.arange(S) % CHUNK != 0) * 1.0),
    }


def pack_small(a):
    heads = [h for c in range(4) for h in (c, c + 4)]
    tiles = dict(shape_constants())
    tiles["gain"] = np.concatenate([col(v) for v in (
        a["ln_mix"][0], a["ln_ffn"][0], a["ln_mix"][1], a["ln_ffn"][1], a["ffn1_pre_w_2"][0], a["mix_pre_w_2"][0],
        a["ffn2_pre_w_2"][0], a["mem_norm_w_2"][0])], 1)
    tiles["lru_w"] = rows_of(np.ascontiguousarray(a["e_lru_conv_w"][0].T))
    tiles["lru_b"] = col(a["e_lru_conv_b"][0])
    tiles["lru_wa"] = block_diagonal(a["e_lru_w_a"][0])
    tiles["lru_wi"] = block_diagonal(a["e_lru_w_i"][0])
    tiles["lru_ba"], tiles["lru_bi"] = col(a["e_lru_b_a"][0]), col(a["e_lru_b_i"][0])
    tiles["lam"] = col(a["e_lru_lambda"][0])
    tiles["q_norm"], tiles["k_norm"] = row(a["e_q_norm"][0]), row(a["e_k_norm"][0])
    tiles["sinks"] = row(a["e_sinks"][0][heads])
    tiles["gdn_conv"] = rows_of(np.ascontiguousarray(a["o_conv_w"][0].T))
    tiles["w_ab"] = rows_of(a["o_w_in"][0][:, 4096:])
    tiles["a_log"], tiles["dt_bias"] = row(a["o_a_log"][0]), row(a["o_dt_bias"][0])
    tiles["out_norm"] = row(a["o_out_norm"][0])
    tiles["router"] = rows_of(a["o_router"][0])
    tiles["b_gate"] = col(a["b_gate_2"][0])
    tiles["hg_logits"] = np.concatenate([col(a["hg_lb_logits_2"][0]), col(a["hg_lb_logits_2"][1])], 1)
    tiles["hg_norm"] = row(a["hg_norm_w_2"][0])
    out = np.empty((P, SMALL), np.float32)
    for name, (o, width) in COLS.items():
        assert tiles[name].shape == (P, width), (name, tiles[name].shape, width)
        out[:, o:o + width] = tiles[name]
    return out


def pack_post(a):
    return np.stack([row(a[k][0]) for k in ("ffn1_post_w_2", "mix_post_w_2", "ffn2_post_w_2")])


def pack_weights(a):
    out = np.empty((UNITS, P, UNIT), np.float32)
    at = [0]

    def cols(w, perm=None):
        k, n = w.shape
        m = n // 256
        out[at[0]:at[0] + m].reshape(m, P, k // P, 256)[:] = w.reshape(k // P, P, m, 256).transpose(2, 1, 0, 3)
        at[0] += m

    def rows(w):
        k, n = w.shape
        m = k // 256
        out[at[0]:at[0] + m].reshape(m, P, 2, n)[:] = w.reshape(m, 2, P, n).transpose(0, 2, 1, 3)
        at[0] += m

    def half_cols(w):
        out[at[0]:at[0] + 2].reshape(2, P, 4, 512)[:] = w.reshape(4, P, 2, 512).transpose(2, 1, 0, 3)
        at[0] += 2

    def swiglu(gate, up, down):
        steps = down.shape[0] // 256
        for s in range(steps):
            for i, w in enumerate((gate, up)):
                out[at[0]:at[0] + 2].reshape(2, P, 4, 2, 256)[:, :, :, i] = \
                    w[:, s * 256:(s + 1) * 256].reshape(2, 4, P, 256).transpose(0, 2, 1, 3)
            at[0] += 2
            if s:
                rows(down[(s - 1) * 256:s * 256])
        rows(down[(steps - 1) * 256:])

    heads = [h for c in range(4) for h in (c, c + 4)]
    w = a["e_w_in"][0]
    q = w[:, 1024:1536].reshape(D, 8, 64)[:, heads].reshape(D, 512)
    cols(w[:, 0:1024])
    cols(q)
    cols(w[:, 1536:])
    w = a["e_w_out"][0]
    rows(w[0:512])
    rows(w[512:].reshape(8, 64, D)[heads].reshape(512, D))
    swiglu(a["e_ffn_w_gate"][0], a["e_ffn_w_up"][0], a["e_ffn_w_down"][0])
    assert at[0] == AT["gdn_in"]
    cols(a["o_w_in"][0][:, 0:4096])
    rows(a["o_w_out"][0])
    for e in range(EXPERTS):
        swiglu(a["o_moe_w_gate"][0, e], a["o_moe_w_up"][0, e], a["o_moe_w_down"][0, e])
    assert at[0] == AT["ffn1"]
    swiglu(a["ffn1_w_gu_2"][0][:, :FF], a["ffn1_w_gu_2"][0][:, FF:], a["ffn1_w_down_2"][0])
    cols(a["w_mem_kv_2"][0])
    cols(a["w_in_2"][0])
    assert at[0] == AT["branch"]
    for name in ("w_br_hg_2", "w_br_dil_2", "w_br_mem_2"):
        half_cols(a[name][0])
    rows(a["w_out_2"][0])
    swiglu(a["ffn2_w_gu_2"][0][:, :FF], a["ffn2_w_gu_2"][0][:, FF:], a["ffn2_w_down_2"][0])
    assert at[0] == UNITS
    return out


def kernel(**inputs):
    import concourse.bacc as bacc
    from concourse.bass_utils import run_bass_kernel_spmd

    a = {k: np.asarray(v) for k, v in inputs.items()}
    arrays = {"small": pack_small(a), "post": pack_post(a), "weights": pack_weights(a), "x": a["x"][0], "mem": a["mem_2"][0]}
    nc = bacc.Bacc("TRN2", target_bir_lowering=False, num_devices=1)
    args = [nc.dram_tensor(n, v.shape, F32, kind="ExternalInput").ap() for n, v in arrays.items()]
    out = nc.dram_tensor("out", (S, D), F32, kind="ExternalOutput").ap()
    build(nc, *args, out)
    r = run_bass_kernel_spmd(nc, [arrays], core_ids=[0])
    return r.results[0]["out"].reshape(1, S, D)
```

```python
import numpy as np
import concourse.bass as bass
from concourse import mybir
from contextlib import ExitStack

F32 = mybir.dt.float32
F32R = mybir.dt.float32r
U32 = mybir.dt.uint32
ALU = mybir.AluOpType
ACT = mybir.ActivationFunctionType
AX = mybir.AxisListType

P = 128
S = 256
NT = S // P
D = 1024
KD = D // P
EPS = 1e-6
CONV = 4
SUBLAYERS = 7
CHUNK = 64
BIG = 1e30
FF = 2816
FFE = 3584
EXPERTS = 8
GH = 8
ATT_SLOTS = 8
DIL = 3
MH = 4

UNIT = 2048
RING = 7
FF_STEPS = FF // 256
FFE_STEPS = FFE // 256
FF_UNITS = 3 * FF_STEPS
FFE_UNITS = 3 * FFE_STEPS
assert FFE_UNITS % RING == 0


def units_before():
    at, n = {}, 0
    for name, count in (("mix0_in", 7), ("mix0_out", 4), ("ffn0", FF_UNITS), ("gdn_in", 16), ("gdn_out", 4),
                        ("moe", EXPERTS * FFE_UNITS), ("ffn1", FF_UNITS), ("mem_kv", 4), ("hg_in", 8),
                        ("dil_in", 18), ("mq_in", 2), ("gl_in", 12), ("branch", 6), ("mix2_out", 4),
                        ("ffn2", FF_UNITS)):
        at[name] = n
        n += count
    at["end"] = n
    return at


AT = units_before()
PAST = {"ffn0": 0, "ffn1": FF_STEPS, "ffn2": 2 * FF_STEPS}
UNITS = AT["end"]
SPLIT_STAGES = {
    "mix0_in": (7, (5, 6, 7, 8, 9, 10, 11)), "ffn0": (FF_UNITS, (2, 6, 9, 10, 11, 1)),
    "gdn_in": (16, (5, 7, 6, 10, 11)), "moe": (EXPERTS * FFE_UNITS, (2, 6, 9, 10, 11, 1)),
    "ffn1": (FF_UNITS, (2, 6, 9, 10, 11, 1)), "hg_in": (28, (9, 11, 4)), "gl_in": (12, (1, 2, 9, 3)),
    "ffn2": (FF_UNITS, (2, 6, 9, 10, 11, 1))}
HI = {stage: bufs for stage, (_, bufs) in SPLIT_STAGES.items()}
SPLITS = {stage: sum(n for n, _ in list(SPLIT_STAGES.values())[:i]) for i, stage in enumerate(SPLIT_STAGES)}
AHEAD = 3
assert FFE_UNITS % len(HI["moe"]) == 0 and HI["moe"] == HI["ffn1"]


def small_layout():
    cols, n = {}, 0
    for name, width in (
            ("ident", P), ("gain", 8 * KD), ("lam", 4), ("cum", P), ("same", P), ("ones", P), ("before", P),
            ("iota", P), ("low", P), ("up", P),
            ("band", 2 * P), ("cos", NT * 32), ("sin", NT * 32), ("reset", S),
            ("lru_w", 4 * CONV), ("lru_b", 4), ("lru_wa", 4 * P), ("lru_wi", 4 * P),
            ("lru_ba", 4), ("lru_bi", 4), ("q_norm", 64), ("k_norm", 64), ("sinks", ATT_SLOTS),
            ("gdn_conv", 24 * CONV), ("w_ab", KD * 16), ("a_log", GH), ("dt_bias", GH), ("out_norm", P),
            ("router", KD * EXPERTS), ("b_gate", 24), ("hg_logits", 2 * MH), ("hg_norm", P)):
        cols[name] = (n, width)
        n += width
    return cols, n


COLS, SMALL = small_layout()
FIRST = COLS["cum"][0]
SLOPES = [2.0 ** (-8.0 * (i + 1) / (DIL * MH)) for i in range(DIL * MH)]


def build(nc, small_d, post_d, w_d, x_d, mem_d, out_d):
    ctx = ExitStack()
    with ctx:
        def sb(name, *shape):
            return ctx.enter_context(nc.sbuf_tensor(name, [P, *shape], F32))

        sems = {}

        def sem(name):
            if name not in sems:
                sems[name] = ctx.enter_context(nc.semaphore(name))
            return sems[name]

        def sb_twice(name, *shape):
            a = sb(name, *shape)
            at = nc.sbuf_base - 4 * int(np.prod(shape))
            return a, nc.alloc_sbuf_tensor_at(name + "_r", [P, *shape], F32R, offset=at)

        small = sb("small_sb", SMALL)
        ring, ring_r = zip(*[sb_twice(f"ring{i}", UNIT) for i in range(RING)])
        h = sb("h", NT, D)
        xnT, xnT_r = sb_twice("xnT", KD, S)
        x_lo = ctx.enter_context(nc.sbuf_tensor("x_lo", [P, KD, S], F32R))
        xn = sb("xn", NT, D)
        buf, buf_r = zip(*[sb_twice(f"buf{i}", 2048) for i in range(12)])
        bank = [ctx.enter_context(nc.psum_tensor(f"bank{i}", [P, 512], F32)) for i in range(8)]
        tiny = sb("tiny", 1024)
        small_conv = sb("small_conv", 4 * S)
        crowded = ctx.enter_context(nc.sbuf_tensor("crowded", [P, 1], mybir.dt.int32))

        tiny_at = [0]

        def tin(*shape):
            n = int(np.prod(shape))
            a = tiny[:, tiny_at[0]:tiny_at[0] + n]
            tiny_at[0] += n
            assert tiny_at[0] <= 1024
            if len(shape) == 2:
                return a.rearrange("p (a b) -> p a b", b=shape[1])
            return a

        def const(name, *shape):
            o, width = COLS[name]
            a = small[:, o:o + width]
            if len(shape) == 2:
                return a.rearrange("p (a b) -> p a b", b=shape[1])
            return a

        def later(width):
            return small[:, COLS["lru_wa"][0]:COLS["lru_wa"][0] + width * P].rearrange("p (a b) -> p a b", b=P)

        level, dist = later(6), later(6).rearrange("p (g k) q -> p g (k q)", k=2)

        def bview(i, *shape, off=0, of=buf):
            n = int(np.prod(shape))
            a = of[i][:, off:off + n]
            if len(shape) == 1:
                return a
            if len(shape) == 2:
                return a.rearrange("p (a b) -> p a b", b=shape[1])
            return a.rearrange("p (a b c) -> p a b c", b=shape[1], c=shape[2])

        def bview_r(i, *shape, off=0):
            return bview(i, *shape, off=off, of=buf_r)

        def over_heads(a, n, width):
            return a.unsqueeze(2).broadcast_to([P, n, width])

        def per_head(a, n, width):
            return a.unsqueeze(1).broadcast_to([P, n, width])

        ident = const("ident")
        minus_half = tin(8)

        ACTV = nc.scalar.activation
        V = nc.vector
        G = nc.gpsimd
        MM = nc.tensor.matmul

        class Chain:

            def __init__(self, eng, name):
                self.eng, self.name, self.n = eng, name, 0

            def add(self, ins):
                self.n += 1
                ins.then_inc(sem(self.name), 1)
                return ins

            def sync(self):
                self.eng.wait_ge(sem(self.name), self.n)

            def step(self, ins):
                self.add(ins)
                self.sync()

        def unit_ready(pe, n):
            pe.wait_ge(sem(f"unit_in{n % RING}"), 16 * (n // RING + 1))

        def w_cols(n):
            return ring[n % RING][:, :].rearrange("p (k c) -> p k c", k=KD)

        def w_rows(n):
            return ring[n % RING][:, :].rearrange("p (k c) -> p k c", k=2)

        def product_T(n, j, dst, acts):
            for k in range(KD):
                last = MM(dst, w_cols(n)[:, k, j * P:(j + 1) * P], acts[:, k, :], start=(k == 0), stop=(k == KD - 1))
            return last

        def product(n, t, dst, acts):
            for k in range(KD):
                last = MM(dst, acts[:, k, t * P:(t + 1) * P], w_cols(n)[:, k, :], start=(k == 0), stop=(k == KD - 1))
            return last

        def product_rows(n, lhsT, first, final):
            for kk in range(2):
                for t in range(NT):
                    for c in range(2):
                        last = MM(bank[4 + 2 * t + c][:, :], lhsT[:, kk, t * P:(t + 1) * P],
                                  w_rows(n)[:, kk, c * 512:(c + 1) * 512],
                                  start=first and kk == 0, stop=final and kk == 1)
            return last

        HALVES = [n for a, b in (("mix0_in", "mix0_out"), ("gdn_in", "gdn_out"), ("mem_kv", "branch"))
                  for n in range(AT[a], AT[b])]

        def half_done(eng, n):
            eng.wait_ge(sem("half_done"), HALVES.index(n) + 1)

        ssq = tin(8, NT)
        rstd = tin(8, NT)

        def norm_square(act, k, src, sublayers=None):
            for t in range(NT):
                if sublayers:
                    act.wait_ge(sem("h_done"), NT * (sublayers - 1) + t + 1)
                ACTV(xn[:, t, :], src[:, t, :], ACT.Square, accum_out=ssq[:, k, t:t + 1]).then_inc(sem("norm_ssq"), 1)
            act.wait_ge(sem("norm_rstd"), NT * (k + 1))
            ACTV(xn[:, 1, :], src[:, 1, :], ACT.Copy, scale=rstd[:, k, 1:2]).then_inc(sem("norm_xn_1"), 1)

        def norm_pow(pool, k):
            for t in range(NT):
                pool.wait_ge(sem("norm_var"), NT * k + t + 1)
                G.tensor_tensor(rstd[:, k, t:t + 1], ssq[:, k, t:t + 1], minus_half[:, 0:1], ALU.pow)\
                    .then_inc(sem("norm_rstd"), 1)

        def norm_scale(dve, k, src):
            for t in range(NT):
                dve.wait_ge(sem("norm_ssq"), NT * k + t + 1)
                V.tensor_scalar(ssq[:, k, t:t + 1], ssq[:, k, t:t + 1], 1.0 / D, EPS, ALU.mult, ALU.add)\
                    .then_inc(sem("norm_var"), 1)
            dve.wait_ge(sem("norm_rstd"), NT * k + 1)
            V.tensor_scalar(xn[:, 0, :], src[:, 0, :], rstd[:, k, 0:1], None, ALU.mult).then_inc(sem("norm_xn_0"), 1)

        def norm_transpose(pe, k):
            for t in range(NT):
                pe.wait_ge(sem("norm_xn_1" if t else "norm_xn_0"), k + 1)
                for c in range(KD):
                    last = nc.tensor.transpose(bank[c // 2][:, (c % 2) * S + t * P:(c % 2) * S + (t + 1) * P],
                                               xn[:, t, c * P:(c + 1) * P], ident)
            last.then_inc(sem("norm_T"), 1)

        def norm_out_act(act, k, row, dstT):
            act.wait_ge(sem("norm_T"), k + 1)
            for c in (0, 1, 4, 5):
                ACTV(dstT[:, c, :], bank[c // 2][:, (c % 2) * S:(c % 2 + 1) * S], ACT.Copy,
                     scale=const("gain", 8, KD)[:, row, c:c + 1]).then_inc(sem("norm_done"), 1)

        def norm_out_dve(dve, k, row, dstT):
            dve.wait_ge(sem("norm_T"), k + 1)
            for c in (2, 3, 6, 7):
                V.tensor_scalar(dstT[:, c, :], bank[c // 2][:, (c % 2) * S:(c % 2 + 1) * S],
                                const("gain", 8, KD)[:, row, c:c + 1], None, ALU.mult).then_inc(sem("norm_done"), 1)

        SPLIT_NORMS = (0, 1, 2, 4, 6, 7)

        def norm_high(act, k, row):
            act.wait_ge(sem("norm_T"), k + 1)
            for c in range(KD):
                ACTV(xnT_r[:, c, :], bank[c // 2][:, (c % 2) * S:(c % 2 + 1) * S], ACT.Copy,
                     scale=const("gain", 8, KD)[:, row, c:c + 1]).then_inc(sem("norm_high"), 1)

        def norm_low(dve, k, row):
            for c in range(KD):
                dve.wait_ge(sem("norm_high"), KD * SPLIT_NORMS.index(k) + c + 2 - c % 2)
                V.scalar_tensor_tensor(x_lo[:, c, :], bank[c // 2][:, (c % 2) * S:(c % 2 + 1) * S],
                                       const("gain", 8, KD)[:, row, c:c + 1], xnT_r[:, c, :].bitcast(F32),
                                       ALU.mult, ALU.subtract).then_inc(sem("norm_done"), 1)

        def norm_ready(eng, k):
            eng.wait_ge(sem("norm_done"), KD * (k + 1))

        def h_ready(eng, sublayers):
            if sublayers:
                eng.wait_ge(sem("h_done"), NT * sublayers)
            else:
                eng.wait_ge(sem("x_in"), 16)

        pssq = tin(3, 4)
        pvar = tin(3, NT)
        prstd = tin(3, NT)

        post_gain = small_conv[:, :]

        def post_square(act, i, units):
            act.wait_ge(sem("unit_used"), units)
            for j in range(4):
                ACTV(xn[:, j // 2, (j % 2) * 512:(j % 2 + 1) * 512], bank[4 + j][:, :], ACT.Square,
                     accum_out=pssq[:, i, j:j + 1]).then_inc(sem("post_ssq"), 1)

        def post_pow(pool, i):
            pool.wait_ge(sem("post_var"), i + 1)
            G.tensor_tensor(prstd[:, i, :], pvar[:, i, :], minus_half[:, 0:NT], ALU.pow).then_inc(sem("post_rstd"), 1)

        def post_add(dve, ch, i, scale):
            dve.wait_ge(sem("post_ssq"), 4 * (i + 1))
            ch.step(V.tensor_tensor(pvar[:, i, :], pssq[:, i, 0:4:2], pssq[:, i, 1:4:2], ALU.add))
            V.tensor_scalar(pvar[:, i, :], pvar[:, i, :], 1.0 / D, EPS, ALU.mult, ALU.add)\
                .then_inc(sem("post_var"), 1)
            dve.wait_ge(sem("post_rstd"), i + 1)
            dve.wait_ge(sem("post_in"), 16 * (i + 1))
            if scale != 1.0:
                ch.step(V.tensor_scalar(prstd[:, i, :], prstd[:, i, :], scale, None, ALU.mult))
            for t in range(NT):
                halves = [slice(0, 512), slice(512, 1024)]
                for j, c in enumerate(halves):
                    ch.add(V.scalar_tensor_tensor(xn[:, t, c], bank[4 + 2 * t + j][:, :], prstd[:, i, t:t + 1],
                                                  post_gain[:, c], ALU.mult, ALU.mult))
                ch.sync()
                V.tensor_tensor(h[:, t, :], h[:, t, :], xn[:, t, :], ALU.add).then_inc(sem("h_done"), 1)

        def high_room(stage, i):
            return buf_r[HI[stage][i % len(HI[stage])]][:, :]

        def high(stage, i, k):
            return high_room(stage, i).rearrange("p (k c) -> p k c", k=k)

        def low(stage, i, k):
            return ring_r[(AT[stage] + i) % RING][:, :].rearrange("p (k c) -> p k c", k=k)

        def split_high(act, stage, i):
            n = AT[stage] + i
            unit_ready(act, n)
            if i >= len(HI[stage]):
                act.wait_ge(sem("unit_used"), n - len(HI[stage]) + 1)
            ACTV(high_room(stage, i), ring[n % RING][:, :], ACT.Copy).then_inc(sem("split_high"), 1)

        def split_low(eng, stage, i, engine=V):
            n = AT[stage] + i
            eng.wait_ge(sem("split_high"), SPLITS[stage] + i + 1)
            engine.tensor_tensor(ring_r[n % RING][:, :], ring[n % RING][:, :], high_room(stage, i).bitcast(F32),
                                 ALU.subtract).then_inc(sem("split_low"), 1)

        def split_ready(pe, stage, i):
            pe.wait_ge(sem("split_low"), SPLITS[stage] + i + 1)

        def three_passes(dst, stationary, moving, start, stop):
            MM(dst, stationary[0], moving[0], start=start, stop=False)
            MM(dst, stationary[0], moving[1], start=False, stop=False)
            return MM(dst, stationary[1], moving[0], start=False, stop=stop)

        def split_product_T(stage, i, j, dst):
            for k in range(KD):
                o = slice(j * P, (j + 1) * P)
                last = three_passes(dst, (high(stage, i, KD)[:, k, o], low(stage, i, KD)[:, k, o]),
                                    (xnT_r[:, k, :], x_lo[:, k, :]), k == 0, k == KD - 1)
            return last

        def split_product(stage, i, t, dst):
            for k in range(KD):
                o = slice(t * P, (t + 1) * P)
                last = three_passes(dst, (xnT_r[:, k, o], x_lo[:, k, o]),
                                    (high(stage, i, KD)[:, k, :], low(stage, i, KD)[:, k, :]), k == 0, k == KD - 1)
            return last

        ffn_hid = bview_r(0, 4, S), bview_r(0, 4, S, off=1024)
        ffn_silu = bview(4, 2, S)
        ffn_prod = bview(4, 2, S, off=512)

        def swiglu_order(steps):
            gate = [max(3 * s - 1, 0) for s in range(steps)]
            down = [3 * s + 4 if s < steps - 1 else 3 * steps - 1 for s in range(steps)]
            return gate, down

        def parts(pair, *index):
            return [a[index] for a in pair]

        def ffn_tensor(pe, past, stage, acts):
            steps, base = FF_STEPS, AT[stage]
            gate, down = swiglu_order(steps)
            every = slice(None)

            def down_product(s):
                i = down[s]
                split_ready(pe, stage, i)
                pe.wait_ge(sem("ffn_hidden"), 2 * (past + s) + 2)
                hi, lo = high(stage, i, 2), low(stage, i, 2)
                for kk in range(2):
                    for t in range(NT):
                        hid = parts(ffn_hid, every, 2 * (s % 2) + kk, slice(t * P, (t + 1) * P))
                        for c in range(2):
                            o = slice(c * 512, (c + 1) * 512)
                            last = three_passes(bank[4 + 2 * t + c][:, :], hid, (hi[:, kk, o], lo[:, kk, o]),
                                                s == 0 and kk == 0, s == steps - 1 and kk == 1)
                last.then_inc(sem("unit_used"), 1)

            for s in range(steps):
                for q in range(4):
                    if s and q < 2:
                        pe.wait_ge(sem("ffn_hidden"), 2 * (past + s) - 1 + q)
                    for k in range(KD):
                        i = gate[s] + k // 4
                        if q == 0 and k % 4 == 0:
                            split_ready(pe, stage, i)
                        o = slice(q * P, (q + 1) * P)
                        last = three_passes(bank[q][:, 0:S], (high(stage, i, 4)[:, k % 4, o],
                                                              low(stage, i, 4)[:, k % 4, o]),
                                            parts(acts, every, k, every), k == 0, k == KD - 1)
                    if q == 3:
                        last.then_inc(sem("unit_used"), 2)
                    else:
                        last.then_inc(sem("ffn_up" if q == 2 else "ffn_gate"), 1)
                if s:
                    down_product(s - 1)
            down_product(steps - 1)

        FIRST_SPLITS = 5

        def ffn_splits(s):
            return range(FIRST_SPLITS + 3 * s, min(FIRST_SPLITS + 3 * s + 3, FF_UNITS))

        def ffn_scalar(act, past, stage):
            for s in range(FF_STEPS):
                for j in range(2):
                    act.wait_ge(sem("ffn_gate"), 2 * (past + s) + j + 1)
                    if s:
                        act.wait_ge(sem("ffn_hidden"), 2 * (past + s) + j - 1)
                    ACTV(ffn_silu[:, j, :], bank[j][:, 0:S], ACT.Silu).then_inc(sem("ffn_silu"), 1)
                for i in ffn_splits(s):
                    split_high(act, stage, i)

        def ffn_vector(dve, ch, past, stage):
            base = AT[stage]
            gate, down = swiglu_order(FF_STEPS)
            for s in range(FF_STEPS):
                for j in range(2):
                    dve.wait_ge(sem("ffn_silu"), 2 * (past + s) + j + 1)
                    if j == 0:
                        dve.wait_ge(sem("ffn_up"), past + s + 1)
                    else:
                        dve.wait_ge(sem("unit_used"), base + gate[s] + 2)
                    if s >= 2:
                        dve.wait_ge(sem("unit_used"), base + down[s - 2] + 1)
                    hi, lo = (a[:, 2 * (s % 2) + j, :] for a in ffn_hid)
                    ch.step(V.tensor_tensor(ffn_prod[:, j, :], ffn_silu[:, j, :], bank[2 + j][:, 0:S], ALU.mult))
                    ch.step(V.tensor_copy(hi, ffn_prod[:, j, :]))
                    V.tensor_tensor(lo, ffn_prod[:, j, :], hi.bitcast(F32), ALU.subtract)\
                        .then_inc(sem("ffn_hidden"), 1)
                for i in ffn_splits(s):
                    split_low(dve, stage, i)

        sc_sb = bview(9, 2, 1024)
        pr_sb = sc_sb
        pT_sb = bview(11, 2, 1024)
        mxs, nmx, esum, sink_e, rden = tin(2), tin(2), tin(2), tin(2), tin(2)

        def att_tensor(pe, past, units, before):
            before(pe)

            def scores(u):
                if u >= 2:
                    pe.wait_ge(sem("att_masked"), past + u - 1)
                for off, w, lhsT, rhs in units[u]["score"]:
                    last = MM(bank[2 * (u % 2) + off // 512][:, off % 512:off % 512 + w], lhsT, rhs,
                              start=True, stop=True)
                last.then_inc(sem("att_scores"), 1)

            def values(u):
                pe.wait_ge(sem("att_copied"), past + u + 1)
                if u >= 2:
                    pe.wait_ge(sem("att_out"), past + u - 1)
                unit, n = units[u], len(units[u]["values"])
                lo, size = unit["rows"]
                for b, v in enumerate(unit["values"]):
                    last = MM(bank[6 + u % 2][lo:lo + size, 0:P], v, pT_sb[:, u % 2, b * P:(b + 1) * P],
                              start=(b == 0), stop=(b == n - 1))
                last.then_inc(sem("att_values"), 1)

            scores(0)
            scores(1)
            for u, unit in enumerate(units):
                if u + 2 < len(units):
                    scores(u + 2)
                pe.wait_ge(sem("att_probs"), past + u + 1)
                if u:
                    pe.wait_ge(sem("att_copied"), past + u)
                for b in range(len(unit["values"])):
                    last = nc.tensor.transpose(bank[4 + b // 4][:, (b % 4) * P:(b % 4 + 1) * P],
                                               pr_sb[:, u % 2, unit["block"](b):unit["block"](b) + P], ident)
                last.then_inc(sem("att_T"), 1)
                if u:
                    values(u - 1)
            values(len(units) - 1)

        def att_scalar(act, past, units):
            def exponential(u):
                i, unit = u % 2, units[u]
                act.wait_ge(sem("att_max"), past + u + 1)
                for off, w in unit["spans"]:
                    last = ACTV(pr_sb[:, i, off:off + w], sc_sb[:, i, off:off + w], ACT.Exp, bias=nmx[:, i:i + 1],
                                accum_out=esum[:, i:i + 1])
                if unit["sink"] is not None:
                    last = ACTV(sink_e[:, i:i + 1], unit["sink"], ACT.Exp, bias=nmx[:, i:i + 1])
                last.then_inc(sem("att_exp"), 1)

            exponential(0)
            for u, unit in enumerate(units):
                if u + 1 < len(units):
                    exponential(u + 1)
                i = u % 2
                act.wait_ge(sem("att_T"), past + u + 1)
                if u >= 2:
                    act.wait_ge(sem("att_values"), past + u - 1)
                nb = len(unit["values"])
                for b in range(0, nb, 4):
                    w = min(4, nb - b) * P
                    last = ACTV(pT_sb[:, i, b * P:b * P + w], bank[4 + b // 4][:, 0:w], ACT.Copy)
                last.then_inc(sem("att_copied"), 1)

        def att_vector(dve, ch, past, units):
            def maximum(u):
                i, unit = u % 2, units[u]
                dve.wait_ge(sem("att_scores"), past + u + 1)
                if u >= 2:
                    dve.wait_ge(sem("att_T"), past + u - 1)
                for off, w, mask, slope in unit["mask"]:
                    src = bank[2 * (u % 2) + off // 512][:, off % 512:off % 512 + w]
                    if mask is None:
                        last = V.tensor_copy(sc_sb[:, i, off:off + w], src)
                    else:
                        last = V.scalar_tensor_tensor(sc_sb[:, i, off:off + w], mask, slope, src, ALU.mult, ALU.add)
                last.then_inc(sem("att_masked"), 1)
                dve.wait_ge(sem("att_masked"), past + u + 1)
                (off, w), = unit["spans"]
                if unit["sink"] is None:
                    V.tensor_reduce(nmx[:, i:i + 1], sc_sb[:, i, off:off + w], AX.X, ALU.max, negate=True)\
                        .then_inc(sem("att_max"), 1)
                else:
                    ch.step(V.tensor_reduce(mxs[:, i:i + 1], sc_sb[:, i, off:off + w], AX.X, ALU.max))
                    V.tensor_scalar(nmx[:, i:i + 1], mxs[:, i:i + 1], unit["sink"], -1.0, ALU.max, ALU.mult)\
                        .then_inc(sem("att_max"), 1)

            def result(u):
                dve.wait_ge(sem("att_values"), past + u + 1)
                lo, n = units[u]["rows"]
                V.tensor_copy(units[u]["out"], bank[6 + u % 2][lo:lo + n, 0:P]).then_inc(sem("att_out"), 1)

            maximum(0)
            for u, unit in enumerate(units):
                if u + 1 < len(units):
                    maximum(u + 1)
                if u >= 2:
                    result(u - 2)
                i = u % 2
                dve.wait_ge(sem("att_exp"), past + u + 1)
                den = esum[:, i:i + 1]
                if unit["sink"] is not None:
                    ch.step(V.tensor_tensor(esum[:, i:i + 1], esum[:, i:i + 1], sink_e[:, i:i + 1], ALU.add))
                ch.step(V.reciprocal(rden[:, i:i + 1], den))
                (off, w), = unit["spans"]
                V.tensor_scalar(pr_sb[:, i, off:off + w], pr_sb[:, i, off:off + w], rden[:, i:i + 1], None, ALU.mult)\
                    .then_inc(sem("att_probs"), 1)
            for u in (len(units) - 2, len(units) - 1):
                result(u)

        def softplus_buffers(n):
            return [tin(n) for _ in range(5)]

        def softplus_vector_a(ch, x, b):
            V.scalar_tensor_tensor(b[0], x, -1.0, x, ALU.mult, ALU.min).then_inc(sem("softplus_arg"), 1)

        def softplus_scalar(act, use, b):
            act.wait_ge(sem("softplus_arg"), use)
            ACTV(b[1], b[0], ACT.Exp).then_inc(sem("softplus_z"), 1)
            act.wait_ge(sem("softplus_w"), use)
            ACTV(b[3], b[2], ACT.Ln).then_inc(sem("softplus_ln"), 1)

        def softplus_vector_b(dve, ch, use, x, b, out):
            dve.wait_ge(sem("softplus_z"), use)
            V.tensor_scalar(b[2], b[1], 1.0, None, ALU.add).then_inc(sem("softplus_w"), 1)
            dve.wait_ge(sem("softplus_w"), use)
            dve.wait_ge(sem("softplus_ln"), use)
            ch.step(V.tensor_tensor(b[3], b[3], b[1], ALU.mult))
            ch.step(V.tensor_scalar(b[4], b[2], -1.0, None, ALU.add))
            ch.step(V.tensor_scalar(b[2], b[4], 0.0, None, ALU.is_equal))
            ch.step(V.tensor_tensor(b[4], b[4], b[2], ALU.add))
            ch.step(V.reciprocal(b[4], b[4]))
            ch.step(V.tensor_tensor(b[3], b[3], b[4], ALU.mult))
            ch.step(V.tensor_tensor(b[2], b[2], b[1], ALU.mult))
            ch.step(V.tensor_tensor(b[3], b[3], b[2], ALU.add))
            ch.step(V.scalar_tensor_tensor(out, x, 0.0, b[3], ALU.max, ALU.add))

        xcT = bview(0, 4, S)
        gelT = bview(0, 4, S, off=1024)
        lru_r = bview(1, 4, S)
        lru_i = bview(1, 4, S, off=1024)
        lru_a = bview(2, 4, S)
        lru_t = bview(2, 4, S, off=1024)
        qkv = bview(3, NT, 768)
        qT0 = bview(4, 4, S)
        kT0 = bview(4, S, off=1024)
        rope_a = bview(5, NT, 640)
        rope_b = bview(6, NT, 640)
        mixT = bview(7, KD, S)
        lam_s = tin(4)
        lam_b = softplus_buffers(4)
        neg_s, pos_s = tin(4), tin(4)
        qk_ssq, qk_var, qk_rstd = tin(20), tin(20), tin(20)

        def flat(a):
            return a.rearrange("p a b -> p (a b)")

        def mix0_tensor(pe):
            base = AT["mix0_in"]
            norm_ready(pe, 0)
            for i in range(8):
                n = base + i // 2
                split_ready(pe, "mix0_in", i // 2)
                if i >= 4:
                    pe.wait_ge(sem("conv0_done"), i - 3)
                last = split_product_T("mix0_in", i // 2, i % 2, bank[i % 4][:, 0:S])
                if i % 2:
                    last.then_inc(sem("unit_used"), 1)
                else:
                    last.then_inc(sem("half_done"), 1)
            for i in range(6):
                n = base + 4 + i // 2
                split_ready(pe, "mix0_in", 4 + i // 2)
                if i >= 4:
                    pe.wait_ge(sem("qkv_copied"), i - 3)
                last = split_product("mix0_in", 4 + i // 2, i % 2, bank[4 + i % 4][:, 0:256])
                if i % 2:
                    last.then_inc(sem("unit_used"), 1)
                else:
                    last.then_inc(sem("half_done"), 1)
            pe.wait_ge(sem("conv0_done"), 4)
            pe.wait_ge(sem("rest_in"), 16)
            for c in range(4):
                pe.wait_ge(sem("gelu_done"), c + 1)
                MM(bank[c][:, 0:S], const("lru_wa", 4, P)[:, c, :], xcT[:, c, :], start=True, stop=True)
                MM(bank[c][:, S:2 * S], const("lru_wi", 4, P)[:, c, :], xcT[:, c, :], start=True, stop=True)\
                    .then_inc(sem("lru_gates"), 1)
            for t in range(NT):
                pe.wait_ge(sem("rope_done"), t + 1)
                pe.wait_ge(sem("qkv_copied"), 6)
                for c in range(4):
                    nc.tensor.transpose(bank[4 + t][:, c * P:(c + 1) * P], qkv[:, t, c * P:(c + 1) * P], ident)
            for t in range(NT):
                pe.wait_ge(sem("rope_done"), NT + t + 1)
                last = nc.tensor.transpose(bank[6][:, t * P:(t + 1) * P], qkv[:, t, 512:640], ident)
            last.then_inc(sem("qk_T"), 1)

        def att0_units():
            units = []
            for t in range(NT):
                for s in range(ATT_SLOTS):
                    c, lo = s // 2, (s % 2) * 64
                    w = (t + 1) * P
                    units.append(dict(
                        score=[(0, w, qT0[lo:lo + 64, c, t * P:(t + 1) * P], kT0[lo:lo + 64, 0:w])],
                        mask=[(0, w, const("band")[:, 2 * P - w:2 * P], 1.0)], spans=[(0, w)],
                        block=lambda b: b * P, sink=const("sinks")[:, s:s + 1],
                        values=[qkv[:, b, 640 + lo:640 + lo + 64] for b in range(t + 1)],
                        rows=(lo, 64), out=mixT[lo:lo + 64, 4 + c, t * P:(t + 1) * P]))
            return units

        att0 = att0_units()

        def att0_before(pe):
            pe.wait_ge(sem("qT0_done"), 1)
            pe.wait_ge(sem("lru_gates_read"), 8)

        def mix0_scalar(act):
            base = AT["mix0_in"]
            for c in range(4):
                if c % 2:
                    act.wait_ge(sem("unit_used"), base + 2 + c // 2 + 1)
                else:
                    half_done(act, base + 2 + c // 2)
                ACTV(gelT[:, c, :], bank[c][:, 0:S], ACT.Gelu_apprx_tanh).then_inc(sem("gelu_done"), 1)
            for i in range(6):
                if i % 2:
                    act.wait_ge(sem("unit_used"), base + 4 + i // 2 + 1)
                else:
                    half_done(act, base + 4 + i // 2)
                ACTV(qkv[:, i % 2, (i // 2) * 256:(i // 2 + 1) * 256], bank[4 + i % 4][:, 0:256], ACT.Copy)\
                    .then_inc(sem("qkv_copied"), 1)
            for c in range(4):
                act.wait_ge(sem("lru_gates"), c + 1)
                ACTV(lru_r[:, c, :], bank[c][:, 0:S], ACT.Sigmoid, bias=const("lru_ba")[:, c:c + 1])\
                    .then_inc(sem("lru_gates_read"), 1)
                ACTV(lru_i[:, c, :], bank[c][:, S:2 * S], ACT.Sigmoid, bias=const("lru_bi")[:, c:c + 1])\
                    .then_inc(sem("lru_gates_read"), 1)
            act.wait_ge(sem("lru_gates_read"), 8)
            act.wait_ge(sem("lam_done"), 1)
            for c in range(4):
                ACTV(lru_a[:, c, :], lru_r[:, c, :], ACT.Exp, scale=neg_s[:, c:c + 1])
                ACTV(lru_t[:, c, :], lru_r[:, c, :], ACT.Tanh, scale=pos_s[:, c:c + 1]).then_inc(sem("lru_at"), 1)
            act.wait_ge(sem("qk_T"), 1)
            ACTV(flat(qT0)[:, :].rearrange("p (c t q) -> p c t q", c=4, t=NT)[:, :, 0, :],
                 bank[4][:, :].rearrange("p (c q) -> p c q", c=4), ACT.Copy, scale=64 ** -0.5)
            ACTV(flat(qT0)[:, :].rearrange("p (c t q) -> p c t q", c=4, t=NT)[:, :, 1, :],
                 bank[5][:, :].rearrange("p (c q) -> p c q", c=4), ACT.Copy, scale=64 ** -0.5)
            ACTV(kT0, bank[6][:, 0:S], ACT.Copy).then_inc(sem("qT0_done"), 1)
            act.wait_ge(sem("lru_m"), 1)
            ACTV(flat(lru_t), flat(lru_t), ACT.Sqrt).then_inc(sem("lru_root"), 1)

        def conv(dve, ch, dst, src, taps, bias, width=S):
            if bias is None:
                ch.step(V.tensor_scalar(dst, src, taps[:, 3:4], None, ALU.mult))
            else:
                ch.step(V.tensor_scalar(dst, src, taps[:, 3:4], bias, ALU.mult, ALU.add))
            for j in (2, 1, 0):
                d = 3 - j
                ins = V.scalar_tensor_tensor(dst[:, d:width], src[:, 0:width - d], taps[:, j:j + 1],
                                             dst[:, d:width], ALU.mult, ALU.add)
                if j:
                    ch.step(ins)
            return ins

        def mix0_vector(dve, ch):
            base = AT["mix0_in"]
            for c in range(4):
                if c % 2:
                    dve.wait_ge(sem("unit_used"), base + c // 2 + 1)
                else:
                    half_done(dve, base + c // 2)
                conv(dve, ch, xcT[:, c, :], bank[c][:, 0:S], const("lru_w", 4, CONV)[:, c, :],
                     const("lru_b")[:, c:c + 1]).then_inc(sem("conv0_done"), 1)
                split_low(dve, "mix0_in", 3 + c)
            for part, (lo, hi, copied) in enumerate(((0, 8, 4), (8, 10, 6))):
                dve.wait_ge(sem("qkv_copied"), copied)
                n = hi - lo
                qk = qkv[:, :, 64 * lo:64 * hi]
                sq = rope_a[:, :, 64 * lo:64 * hi]
                ssq_h, var_h = qk_ssq[:, 2 * lo:2 * hi], qk_var[:, 2 * lo:2 * hi]
                ch.step(V.tensor_tensor(sq, qk, qk, ALU.mult))
                for t in range(NT):
                    ch.add(V.tensor_reduce(ssq_h[:, n * t:n * t + n], sq[:, t, :].rearrange("p (h d) -> p h d", d=64),
                                           AX.X, ALU.add))
                ch.sync()
                V.tensor_scalar(var_h, ssq_h, 1.0 / 64, EPS, ALU.mult, ALU.add).then_inc(sem("head_var"), 1)
                dve.wait_ge(sem("head_rstd"), part + 1)
                rstd_h = qk_rstd[:, 2 * lo:2 * hi]
                gain_h = const("k_norm" if part else "q_norm")
                heads = [qkv[:, t, 64 * lo:64 * hi].rearrange("p (h d) -> p h d", d=64) for t in range(NT)]
                for t in range(NT):
                    ch.add(V.tensor_tensor(heads[t], heads[t], over_heads(rstd_h[:, n * t:n * t + n], n, 64), ALU.mult))
                ch.sync()
                for t in range(NT):
                    ch.add(V.tensor_tensor(heads[t], heads[t], per_head(gain_h, n, 64), ALU.mult))
                ch.sync()
                for t in range(NT):
                    x1, x2 = heads[t][:, :, 0:32], heads[t][:, :, 32:64]
                    ta = rope_a[:, t, 64 * lo:64 * hi].rearrange("p (h d) -> p h d", d=64)
                    tb = rope_b[:, t, 64 * lo:64 * hi].rearrange("p (h d) -> p h d", d=64)
                    cos = per_head(const("cos", NT, 32)[:, t, :], n, 32)
                    sin = per_head(const("sin", NT, 32)[:, t, :], n, 32)
                    ch.add(V.tensor_tensor(ta[:, :, 0:32], x1, cos, ALU.mult))
                    ch.add(V.tensor_tensor(tb[:, :, 0:32], x2, sin, ALU.mult))
                    ch.add(V.tensor_tensor(ta[:, :, 32:64], x2, cos, ALU.mult))
                    ch.step(V.tensor_tensor(tb[:, :, 32:64], x1, sin, ALU.mult))
                    V.tensor_tensor(x1, ta[:, :, 0:32], tb[:, :, 0:32], ALU.subtract)
                    V.tensor_tensor(x2, ta[:, :, 32:64], tb[:, :, 32:64], ALU.add).then_inc(sem("rope_done"), 1)

        def mix0_vector_lru(dve, ch):
            dve.wait_ge(sem("lru_at"), 4)
            gx = flat(lru_i)
            ch.add(V.tensor_tensor(gx, gx, flat(xcT), ALU.mult))
            ch.step(V.tensor_tensor(flat(lru_r), flat(lru_a), flat(lru_a), ALU.mult))
            V.scalar_tensor_tensor(flat(lru_t), flat(lru_r), 1.0, flat(lru_t), ALU.add, ALU.mult)\
                .then_inc(sem("lru_m"), 1)
            dve.wait_ge(sem("lru_root"), 1)
            ch.step(V.tensor_tensor(gx, gx, flat(lru_t), ALU.mult))
            for c in range(4):
                ch.add(V.tensor_tensor_scan(lru_r[:, c, :], lru_a[:, c, :], lru_i[:, c, :], 0.0, ALU.mult, ALU.add))
            ch.sync()
            V.tensor_tensor(mixT[:, 0:4, :], lru_r, gelT, ALU.mult).then_inc(sem("lru_y"), 1)

        def out_tensor(pe, base, ready, acts):
            ready(pe)
            for r in range(4):
                unit_ready(pe, base + r)
                last = product_rows(base + r, acts[:, 2 * r:2 * r + 2, :], r == 0, r == 3)
                last.then_inc(sem("unit_used"), 1)

        def add_product(dve, base_end):
            dve.wait_ge(sem("unit_used"), base_end)
            for t in range(NT):
                for c in range(2):
                    last = V.tensor_tensor(h[:, t, c * 512:(c + 1) * 512], h[:, t, c * 512:(c + 1) * 512],
                                           bank[4 + 2 * t + c][:, :], ALU.add)
                    if c:
                        last.then_inc(sem("h_done"), 1)

        NP = NT * GH
        LEVELS = 6
        NG = NP // 4
        g_q, g_k, g_v = bview(0, GH, S), bview(1, GH, S), bview(2, GH, S)
        g_gate = bview(3, NP, P)
        g_rows = bview(4, NP, P)
        g_qdT = g_rows
        g_eG = bview(5, NP, P)
        g_A = bview(6, NP, P)
        g_aT = bview(7, NP, P)
        g_T = bview(8, NP, P)
        g_TT = bview(9, NP, P)
        g_sq = [bview(8, GH, S), bview(9, GH, S)]
        g_diag = g_sq
        g_kb, g_kd = bview(10, NP, P), bview(11, NP, P)
        g_vb = flat(xn).rearrange("p (a b) -> p a b", b=P)
        g_YT = bview(0, NP, P)
        g_Ak = [bview(2, NP, P), bview(1, NP, P)]
        g_WT = bview(2, NP, P)
        g_U = bview(8, NP, P)
        g_S = xn[:, 0, :].rearrange("p (a b) -> p a b", b=P)
        g_osq = bview(9, NP, P)
        g_y = bview(10, NP, P)
        conv_out = [silu_c for silu_c in (small_conv[:, i * S:(i + 1) * S] for i in range(4))]
        ab = tin(NT, 16)
        sp_x, sp_out, g_g, g_beta, g_bk = tin(NP), tin(NP), tin(NP), tin(NP), tin(NP)
        sp_b = softplus_buffers(NP)
        ea = tin(GH)
        g_arg, g_exp = tin(2 * NP), tin(2 * NP)
        o_ssq, o_rstd = tin(NP), tin(NP)
        n_ssq, n_rnorm = tin(2 * NP), tin(2 * NP)

        def psum4(i):
            return bank[i][:, :].rearrange("p (a b) -> p a b", b=P)

        def gdn_in_tensor(pe):
            base = AT["gdn_in"]
            norm_ready(pe, 2)
            for t in range(NT):
                for part in (xnT_r, x_lo):
                    for k in range(KD):
                        last = MM(bank[6][:, 16 * t:16 * t + 16], part[:, k, t * P:(t + 1) * P].bitcast(F32),
                                  const("w_ab", KD, 16)[:, k, :], start=(part is xnT_r and k == 0),
                                  stop=(part is x_lo and k == KD - 1))
            last.then_inc(sem("ab_done"), 1)
            for i in range(24):
                n = base + i // 2
                split_ready(pe, "gdn_in", i // 2)
                if i >= 4:
                    pe.wait_ge(sem("gdn_conv"), i - 3)
                last = split_product_T("gdn_in", i // 2, i % 2, bank[i % 4][:, 0:S])
                last.then_inc(sem("unit_used" if i % 2 else "half_done"), 1)
            for i in range(8):
                n = base + 12 + i // 2
                split_ready(pe, "gdn_in", 12 + i // 2)
                if i >= 2:
                    pe.wait_ge(sem("gate_copied"), i - 1)
                last = split_product("gdn_in", 12 + i // 2, i % 2, bank[4 + i % 2][:, 0:256])
                last.then_inc(sem("unit_used" if i % 2 else "half_done"), 1)
                if i == 1:
                    norm_sums(pe)
                if i in (3, 5):
                    norm_rows(pe, (i - 3) // 2)

        def norm_sums(pe):
            for j in range(2):
                pe.wait_ge(sem("gdn_sq"), j + 1)
                for i in range(NP):
                    t, e = i // GH, i % GH
                    last = MM(bank[7][:, NP * j + i:NP * j + i + 1], g_sq[j][:, e, t * P:(t + 1) * P],
                              const("ones")[:, 0:1], start=True, stop=True)
            last.then_inc(sem("gdn_sums"), 1)

        def norm_rows(pe, j):
            pe.wait_ge(sem("gdn_diag"), j + 1)
            if j:
                pe.wait_ge(sem("qk_normed"), 1)
            else:
                pe.wait_ge(sem("gdn_conv"), 24)
            for c in range(4):
                last = MM(bank[c][:, :], const("ones"), flat(g_diag[j])[:, c * 512:(c + 1) * 512],
                          start=True, stop=True)
            last.then_inc(sem("gdn_norms"), 1)

        def norm_qk(dve, ch):
            dve.wait_ge(sem("gdn_sums"), 1)
            V.tensor_scalar(n_ssq, bank[7][:, 0:2 * NP], EPS, None, ALU.add).then_inc(sem("head_var"), 1)
            dve.wait_ge(sem("head_rstd"), 3)
            for j in range(2):
                for t in range(NT):
                    last = V.tensor_tensor(g_diag[j][:, :, t * P:(t + 1) * P], per_head(ident, GH, P),
                                           over_heads(n_rnorm[:, NP * j + GH * t:NP * j + GH * t + GH], GH, P),
                                           ALU.mult)
                last.then_inc(sem("gdn_diag"), 1)
            for j, src in enumerate((g_q, g_k)):
                dve.wait_ge(sem("gdn_norms"), j + 1)
                for c in range(4):
                    o = slice(c * 512, (c + 1) * 512)
                    last = V.scalar_tensor_tensor(flat(src)[:, o], flat(src)[:, o], 1.0 if j else P ** -0.5,
                                                  bank[c][:, :], ALU.mult, ALU.mult)
                last.then_inc(sem("qk_normed"), 1)

        def norm_pow_qk(pool):
            pool.wait_ge(sem("head_var"), 3)
            G.tensor_tensor(n_rnorm, n_ssq, minus_half[:, 0:1].broadcast_to([P, 2 * NP]), ALU.pow)\
                .then_inc(sem("head_rstd"), 1)

        def gdn_in_wait(eng, i, base):
            if i % 2:
                eng.wait_ge(sem("unit_used"), base + i // 2 + 1)
            else:
                half_done(eng, base + i // 2)

        def gdn_in_scalar(act):
            softplus_scalar(act, 2, sp_b)
            ACTV(ea, const("a_log"), ACT.Exp).then_inc(sem("gdn_ea_beta"), 1)
            act.wait_ge(sem("ab_copied"), 1)
            ACTV(g_beta.rearrange("p (t e) -> p t e", t=NT), ab[:, :, 8:16], ACT.Sigmoid).then_inc(sem("gdn_ea_beta"), 1)
            for i in range(24):
                if i % 2 and i // 2 + 5 < 16:
                    split_high(act, "gdn_in", i // 2 + 5)
                act.wait_ge(sem("gdn_conv"), i + 1)
                dst = (g_q, g_k, g_v)[i // 8][:, i % 8, :]
                ACTV(dst, conv_out[i % 4], ACT.Silu).then_inc(sem("gdn_silu"), 1)
            for i in range(8):
                gdn_in_wait(act, i, AT["gdn_in"] + 12)
                c = i // 2
                ACTV(g_gate[:, 8 * (i % 2) + 2 * c:8 * (i % 2) + 2 * c + 2, :],
                     bank[4 + i % 2][:, 0:256].rearrange("p (a b) -> p a b", b=P), ACT.Silu)\
                    .then_inc(sem("gate_copied"), 1)

        def gdn_in_vector(dve, ch):
            dve.wait_ge(sem("ab_done"), 1)
            V.tensor_copy(ab, bank[6][:, 0:32].rearrange("p (t e) -> p t e", t=NT)).then_inc(sem("ab_copied"), 1)
            dve.wait_ge(sem("ab_copied"), 1)
            ch.step(V.tensor_tensor(sp_x.rearrange("p (t e) -> p t e", t=NT), ab[:, :, 0:8],
                                    per_head(const("dt_bias"), NT, GH), ALU.add))
            softplus_vector_a(ch, sp_x, sp_b)
            softplus_vector_b(dve, ch, 2, sp_x, sp_b, sp_out)
            dve.wait_ge(sem("gdn_ea_beta"), 1)
            ch.step(V.scalar_tensor_tensor(g_g.rearrange("p (t e) -> p t e", t=NT),
                                           sp_out.rearrange("p (t e) -> p t e", t=NT), -1.0,
                                           per_head(ea, NT, GH), ALU.mult, ALU.mult))
            V.tensor_copy(g_rows, over_heads(g_g, NP, P)).then_inc(sem("g_done"), 1)
            for i in range(24):
                gdn_in_wait(dve, i, AT["gdn_in"])
                if i >= 4:
                    dve.wait_ge(sem("gdn_silu"), i - 3)
                conv(dve, ch, conv_out[i % 4], bank[i % 4][:, 0:S], const("gdn_conv", 24, CONV)[:, i, :], None)\
                    .then_inc(sem("gdn_conv"), 1)
                if i in (11, 19):
                    gdn_square(dve, (i - 11) // 8)
            norm_qk(dve, ch)

        def gdn_square(dve, i):
            dve.wait_ge(sem("gdn_silu"), 8 * (i + 1))
            V.tensor_tensor(flat(g_sq[i]), flat((g_q, g_k)[i]), flat((g_q, g_k)[i]), ALU.mult)\
                .then_inc(sem("gdn_sq"), 1)

        def gdn_splits(pool):
            pool.wait_ge(sem("split_low"), SPLITS["gdn_in"] + 2)
            for i in range(2, 16):
                split_low(pool, "gdn_in", i, G)
            norm_pow_qk(pool)

        def gdn_core_tensor(pe):
            pe.wait_ge(sem("g_done"), 1)
            for t in range(NT):
                MM(bank[6][:, 64 + 8 * t:72 + 8 * t], const("cum"), g_g[:, 8 * t:8 * t + 8], start=True, stop=True)
                last = MM(bank[6][:, 80 + 8 * t:88 + 8 * t], const("same"), g_g[:, 8 * t:8 * t + 8],
                          start=True, stop=True)
            last.then_inc(sem("gcol"), 1)
            for i in range(NP):
                if i == 0:
                    pe.wait_ge(sem("qk_normed"), 2)
                last = MM(bank[i // 4][:, (i % 4) * P:(i % 4 + 1) * P], g_rows[:, i, :], const("cum"),
                          start=True, stop=True)
                if i % 4 == 3:
                    last.then_inc(sem("grow"), 1)
            pe.wait_ge(sem("gate_copied"), 8)
            pe.wait_ge(sem("gcol_copied"), 1)
            pe.wait_ge(sem("grow_read"), 2)
            for i in range(NP):
                t, e = i // GH, i % GH
                kt = g_k[:, e, t * P:(t + 1) * P]
                last = MM(bank[i // 4][:, (i % 4) * P:(i % 4 + 1) * P], kt, kt, start=True, stop=True)
                if i % 4 == 3:
                    last.then_inc(sem("gdn_kk"), 1)
            for i in range(NP):
                t, e = i // GH, i % GH
                last = MM(bank[4 + i // 4][:, (i % 4) * P:(i % 4 + 1) * P], g_k[:, e, t * P:(t + 1) * P],
                          g_q[:, e, t * P:(t + 1) * P], start=True, stop=True)
                if i % 4 == 3:
                    last.then_inc(sem("gdn_qk"), 1)
            for j, src in enumerate((g_k, g_v)):
                for i in range(NP):
                    t, e = i // GH, i % GH
                    if i % 4 == 0:
                        pe.wait_ge(sem("gdn_aT" if j else "gdn_A"), i // 4 + 1)
                    last = nc.tensor.transpose(bank[4 * j + i // 4][:, (i % 4) * P:(i % 4 + 1) * P],
                                               src[:, e, t * P:(t + 1) * P], ident)
                    if i % 4 == 3:
                        last.then_inc(sem("gdn_kvT"), 1)
            pe.wait_ge(sem("gdn_level"), 1)
            for i in range(NP):
                if i % 4 == 0:
                    pe.wait_ge(sem("gdn_kv"), i // 4 + 1)
                last = nc.tensor.transpose(bank[i // 4][:, (i % 4) * P:(i % 4 + 1) * P], g_Ak[0][:, i, :], ident)
                if i % 4 == 3:
                    last.then_inc(sem("gdn_A0T"), 1)
            pe.wait_ge(sem("gdn_kv"), 8)
            for k in range(1, LEVELS):
                pe.wait_ge(sem("gdn_level"), k + 1)
                for g in range(NG):
                    pe.wait_ge(sem("gdn_T"), NG * (k - 1) + g + 1)
                    for i in range(4 * g, 4 * g + 4):
                        last = MM(bank[g][:, (i % 4) * P:(i % 4 + 1) * P], g_Ak[k % 2][:, i, :], g_TT[:, i, :],
                                  start=True, stop=True)
                    last.then_inc(sem("gdn_YT"), 1)
                for g in range(NG):
                    pe.wait_ge(sem("gdn_YT_copied"), NG * (k - 1) + g + 1)
                    if k > 1 or g >= 2:
                        pe.wait_ge(sem("gdn_T"), NG * k + g - 1)
                    for i in range(4 * g, 4 * g + 4):
                        o = slice((i % 4) * P, (i % 4 + 1) * P)
                        if k < LEVELS - 1:
                            MM(bank[4 + g % 2][:, o], g_YT[:, i, :], g_T[:, i, :], start=True, stop=True)
                        last = MM(bank[6 + g % 2][:, o], g_T[:, i, :], g_YT[:, i, :], start=True, stop=True)
                    last.then_inc(sem("gdn_Z"), 1)
            pe.wait_ge(sem("gdn_T"), NG * LEVELS)
            for i in range(NP):
                last = MM(bank[i // 4][:, (i % 4) * P:(i % 4 + 1) * P], g_kb[:, i, :], g_TT[:, i, :],
                          start=True, stop=True)
            last.then_inc(sem("gdn_WT"), 1)
            for i in range(NP):
                last = MM(bank[4 + i // 4][:, (i % 4) * P:(i % 4 + 1) * P], g_TT[:, i, :], g_vb[:, i, :],
                          start=True, stop=True)
            last.then_inc(sem("gdn_U"), 1)
            pe.wait_ge(sem("gdn_WT_copied"), 1)
            for c in range(4):
                t, r = c // 2, slice(CHUNK * (c % 2), CHUNK * (c % 2) + CHUNK)
                if c:
                    pe.wait_ge(sem("gdn_S"), c)
                    for e in range(GH):
                        last = MM(bank[e // 4][r, (e % 4) * P:(e % 4 + 1) * P], g_WT[:, GH * t + e, r], g_S[:, e, :],
                                  start=True, stop=True)
                    last.then_inc(sem("gdn_WS"), 1)
                pe.wait_ge(sem("gdn_vn"), c + 1)
                if c < 3:
                    for e in range(GH):
                        last = MM(bank[6 + e // 4][:, (e % 4) * P:(e % 4 + 1) * P], g_kd[r, GH * t + e, :],
                                  g_U[r, GH * t + e, :], start=True, stop=True)
                    last.then_inc(sem("gdn_kv_state"), 1)
                for e in range(GH):
                    i = GH * t + e
                    dst = bank[2 + 2 * t + e // 4][r, (e % 4) * P:(e % 4 + 1) * P]
                    if c:
                        MM(dst, g_qdT[:, i, r], g_S[:, e, :], start=True, stop=False)
                    last = MM(dst, g_aT[r, i, r], g_U[r, i, :], start=(c == 0), stop=True)
                last.then_inc(sem("gdn_O"), 1)
            for t in range(NT):
                pe.wait_ge(sem("gdn_y"), t + 1)
                for e in range(GH):
                    last = nc.tensor.transpose(bank[(0, 1, 6, 7)[e // 2]][:, (e % 2) * S + t * P:(e % 2) * S + t * P + P],
                                               g_y[:, GH * t + e, :], ident)
            last.then_inc(sem("gdn_yT"), 1)

        def gdn_core_scalar(act):
            act.wait_ge(sem("gcol_copied"), 1)
            ACTV(g_exp, g_arg, ACT.Exp).then_inc(sem("gdn_exp"), 1)
            for i in range(4):
                act.wait_ge(sem("grow"), i + 1)
                ACTV(g_eG[:, 4 * i:4 * i + 4, :], psum4(i), ACT.Exp).then_inc(sem("eG_done"), 1)
            act.wait_ge(sem("grow_read"), 1)
            ACTV(flat(g_A), flat(g_A), ACT.Exp, scale=-1.0)
            act.wait_ge(sem("grow_read"), 2)
            ACTV(flat(g_aT), flat(g_aT), ACT.Exp).then_inc(sem("decay_done"), 1)
            for k in range(1, LEVELS):
                for g in range(NG):
                    act.wait_ge(sem("gdn_YT"), NG * (k - 1) + g + 1)
                    ACTV(g_YT[:, 4 * g:4 * g + 4, :], psum4(g), ACT.Copy).then_inc(sem("gdn_YT_copied"), 1)
            act.wait_ge(sem("gdn_WT"), 1)
            for j in range(4):
                last = ACTV(g_WT[:, 4 * j:4 * j + 4, :], psum4(j), ACT.Copy)
            last.then_inc(sem("gdn_WT_copied"), 1)
            for t in range(NT):
                act.wait_ge(sem("gdn_O"), 2 * t + 2)
                for j in range(2):
                    last = ACTV(g_osq[:, GH * t + 4 * j:GH * t + 4 * j + 4, :], psum4(2 + 2 * t + j), ACT.Square)
                last.then_inc(sem("gdn_osq"), 1)
            act.wait_ge(sem("gdn_yT"), 1)
            for j in range(2):
                ACTV(mixT[:, 2 * j:2 * j + 2, :], bank[j][:, :].rearrange("p (a b) -> p a b", b=S), ACT.Copy)\
                    .then_inc(sem("gdn_mixT"), 1)

        def gdn_core_vector(dve, ch):
            dve.wait_ge(sem("gcol"), 1)
            ch.step(V.tensor_copy(g_arg, bank[6][:, 64:96]))
            V.tensor_tensor(g_arg[:, NP:2 * NP], g_arg[:, NP:2 * NP], g_arg[:, 0:NP], ALU.subtract)\
                .then_inc(sem("gcol_copied"), 1)
            dve.wait_ge(sem("gcol_copied"), 1)
            for j, (dst, name) in enumerate(((g_A, "low"), (g_aT, "up"))):
                for i in range(NP):
                    dve.wait_ge(sem("eG_done"), i // 4 + 1)
                    last = V.scalar_tensor_tensor(dst[:, i, :], psum4(i // 4)[:, i % 4, :], g_arg[:, i:i + 1],
                                                  const(name), ALU.subtract, ALU.add)
                last.then_inc(sem("grow_read"), 1)
            dve.wait_ge(sem("gdn_exp"), 1)
            dve.wait_ge(sem("gdn_ea_beta"), 2)
            ch.step(V.tensor_tensor(g_bk, g_beta, g_exp[:, 0:NP], ALU.mult))
            dve.wait_ge(sem("decay_done"), 1)
            for i in range(NP):
                dve.wait_ge(sem("gdn_kk"), i // 4 + 1)
                last = V.scalar_tensor_tensor(g_A[:, i, :], psum4(i // 4)[:, i % 4, :], g_beta[:, i:i + 1],
                                              g_A[:, i, :], ALU.mult, ALU.mult)
                if i % 4 == 3:
                    last.then_inc(sem("gdn_A"), 1)
            dve.wait_ge(sem("gdn_A"), 4)
            for j in range(4):
                dve.wait_ge(sem("gdn_qk"), j + 1)
                V.tensor_tensor(g_aT[:, 4 * j:4 * j + 4, :], psum4(4 + j), g_aT[:, 4 * j:4 * j + 4, :], ALU.mult)\
                    .then_inc(sem("gdn_aT"), 1)
            for j in range(4):
                dve.wait_ge(sem("gdn_kvT"), j + 1)
                V.tensor_tensor(g_kb[:, 4 * j:4 * j + 4, :], psum4(j), over_heads(g_bk[:, 4 * j:4 * j + 4], 4, P),
                                ALU.mult)
                V.tensor_tensor(g_kd[:, 4 * j:4 * j + 4, :], psum4(j),
                                over_heads(g_exp[:, NP + 4 * j:NP + 4 * j + 4], 4, P), ALU.mult)\
                    .then_inc(sem("gdn_kv"), 1)
            for j in range(4):
                dve.wait_ge(sem("gdn_kvT"), 4 + j + 1)
                V.tensor_tensor(g_vb[:, 4 * j:4 * j + 4, :], psum4(4 + j), over_heads(g_beta[:, 4 * j:4 * j + 4], 4, P),
                                ALU.mult).then_inc(sem("gdn_kv"), 1)
            for t in range(NT):
                if t == 0:
                    dve.wait_ge(sem("gdn_level"), 1)
                sl = slice(GH * t, GH * t + GH)
                ch.add(V.scalar_tensor_tensor(g_T[:, sl, :], g_Ak[0][:, sl, :], -1.0, per_head(ident, GH, P),
                                              ALU.mult, ALU.add))
                dve.wait_ge(sem("gdn_A0T"), 2 * t + 2)
                for j in range(2):
                    b = 2 * t + j
                    V.scalar_tensor_tensor(g_TT[:, 4 * b:4 * b + 4, :], psum4(b), -1.0, per_head(ident, 4, P),
                                           ALU.mult, ALU.add).then_inc(sem("gdn_T"), 1)
            for k in range(1, LEVELS):
                for g in range(NG):
                    dve.wait_ge(sem("gdn_Z"), NG * (k - 1) + g + 1)
                    dve.wait_ge(sem("gdn_T"), NG * k)
                    sl = slice(4 * g, 4 * g + 4)
                    if k < LEVELS - 1:
                        V.tensor_tensor(g_T[:, sl, :], g_T[:, sl, :], psum4(4 + g % 2), ALU.subtract)
                    V.tensor_tensor(g_TT[:, sl, :], g_TT[:, sl, :], psum4(6 + g % 2), ALU.subtract)\
                        .then_inc(sem("gdn_T"), 1)
            dve.wait_ge(sem("gdn_U"), 1)
            for j in range(4):
                last = V.tensor_copy(g_U[:, 4 * j:4 * j + 4, :], psum4(4 + j))
            last.then_inc(sem("gdn_vn"), 1)
            for c in range(4):
                t, r = c // 2, slice(CHUNK * (c % 2), CHUNK * (c % 2) + CHUNK)
                if c:
                    dve.wait_ge(sem("gdn_WS"), c)
                    for j in range(2):
                        sl = slice(GH * t + 4 * j, GH * t + 4 * j + 4)
                        last = V.tensor_tensor(g_U[r, sl, :], g_U[r, sl, :], psum4(j)[r, :, :], ALU.subtract)
                    last.then_inc(sem("gdn_vn"), 1)
                if c < 3:
                    dve.wait_ge(sem("gdn_kv_state"), c + 1)
                    if c == 0:
                        for j in range(2):
                            last = V.tensor_copy(g_S[:, 4 * j:4 * j + 4, :], psum4(6 + j))
                    else:
                        dve.wait_ge(sem("gdn_O"), c + 1)
                        for e in range(GH):
                            i = GH * t + e
                            end = CHUNK * (c % 2) + CHUNK - 1
                            last = V.scalar_tensor_tensor(g_S[:, e, :], g_S[:, e, :], g_eG[:, i, end:end + 1],
                                                          psum4(6 + e // 4)[:, e % 4, :], ALU.mult, ALU.add)
                    last.then_inc(sem("gdn_S"), 1)
                    dve.wait_ge(sem("gdn_S"), c + 1)
            for t in range(NT):
                sl = slice(GH * t, GH * t + GH)
                dve.wait_ge(sem("gdn_osq"), t + 1)
                ch.step(V.tensor_reduce(o_ssq[:, sl], g_osq[:, sl, :], AX.X, ALU.add))
                V.tensor_scalar(o_ssq[:, sl], o_ssq[:, sl], 1.0 / P, EPS, ALU.mult, ALU.add)\
                    .then_inc(sem("head_var"), 1)
                dve.wait_ge(sem("head_rstd"), t + 4)
                for j in range(2):
                    s4 = slice(GH * t + 4 * j, GH * t + 4 * j + 4)
                    ch.add(V.tensor_tensor(g_y[:, s4, :], psum4(2 + 2 * t + j), over_heads(o_rstd[:, s4], 4, P),
                                           ALU.mult))
                ch.sync()
                ch.step(V.tensor_tensor(g_y[:, sl, :], g_y[:, sl, :], per_head(const("out_norm"), GH, P), ALU.mult))
                V.tensor_tensor(g_y[:, sl, :], g_y[:, sl, :], g_gate[:, sl, :], ALU.mult).then_inc(sem("gdn_y"), 1)
            dve.wait_ge(sem("gdn_yT"), 1)
            for j in range(2):
                V.tensor_copy(mixT[:, 4 + 2 * j:6 + 2 * j, :], bank[6 + j][:, :].rearrange("p (a b) -> p a b", b=S))\
                    .then_inc(sem("gdn_mixT"), 1)

        def gdn_core_pool(pool):
            pool.wait_ge(sem("qk_normed"), 1)
            pool.wait_ge(sem("eG_done"), 4)
            for t in range(NT):
                G.tensor_tensor(g_qdT[:, GH * t:GH * t + GH, :], g_q[:, :, t * P:(t + 1) * P],
                                g_eG[:, GH * t:GH * t + GH, :], ALU.mult)
            pool.wait_ge(sem("rest_in"), 16)
            pool.wait_ge(sem("later_in"), 16)
            pool.wait_ge(sem("gdn_A"), 4)
            for k in range(LEVELS):
                if k < 2:
                    pool.wait_ge(sem("gdn_kvT"), 8)
                elif k == 2:
                    pool.wait_ge(sem("gdn_A0T"), 4)
                    pool.wait_ge(sem("gdn_T"), NG)
                else:
                    pool.wait_ge(sem("gdn_YT"), NG * (k - 2))
                G.tensor_tensor(g_Ak[k % 2], g_A, per_head(level[:, k, :], NP, P), ALU.mult)\
                    .then_inc(sem("gdn_level"), 1)
            for t in range(NT):
                pool.wait_ge(sem("head_var"), t + 4)
                G.tensor_tensor(o_rstd[:, GH * t:GH * t + GH], o_ssq[:, GH * t:GH * t + GH], minus_half, ALU.pow)\
                    .then_inc(sem("head_rstd"), 1)

        sel = tin(NT, EXPERTS + 1)
        logits, top8, m_ge, m_gt = tin(NT, 8), tin(NT, 8), tin(NT, 8), tin(NT, 8)
        m_eq, m_cum, gates, n_gt = tin(NT, 8), tin(NT, 8), tin(NT, 8), tin(NT, 4)

        def router_tensor(pe):
            norm_ready(pe, 3)
            for t in range(NT):
                for k in range(KD):
                    last = MM(bank[0][:, 8 * t:8 * t + 8], xnT[:, k, t * P:(t + 1) * P],
                              const("router", KD, EXPERTS)[:, k, :], start=(k == 0), stop=(k == KD - 1))
            last.then_inc(sem("logits"), 1)

        def router_scalar(act):
            act.wait_ge(sem("top_diff"), 1)
            ACTV(gates, gates, ACT.Exp).then_inc(sem("top_exp"), 1)

        def router_vector(dve, ch):
            dve.wait_ge(sem("logits"), 1)
            ch.step(V.tensor_copy(logits, bank[0][:, 0:16].rearrange("p (t e) -> p t e", t=NT)))
            for t in range(NT):
                ch.add(V.max(top8[:, t, :], logits[:, t, :]))
            ch.sync()
            for t in range(NT):
                l, v1, v2 = logits[:, t, :], top8[:, t, 0:1], top8[:, t, 1:2]
                ch.add(V.tensor_scalar(gates[:, t, :], l, v1, None, ALU.subtract))
                ch.add(V.tensor_scalar(m_gt[:, t, :], l, v2, None, ALU.is_gt))
                ch.add(V.tensor_scalar(m_eq[:, t, :], l, v2, None, ALU.is_equal))
            ch.sync()
            V.tensor_copy(m_ge[:, :, 0:1], m_eq[:, :, 0:1]).then_inc(sem("top_diff"), 1)
            dve.wait_ge(sem("top_diff"), 1)
            for t in range(NT):
                ch.add(V.tensor_reduce(n_gt[:, t, 0:1], m_gt[:, t, :], AX.X, ALU.add))
                ch.add(V.tensor_tensor_scan(m_cum[:, t, :], const("ones")[:, 0:8], m_eq[:, t, :], 0.0,
                                            ALU.mult, ALU.add))
            ch.sync()
            for t in range(NT):
                ch.add(V.tensor_scalar(m_ge[:, t, :], m_cum[:, t, :], n_gt[:, t, 0:1], 2.0, ALU.add, ALU.is_le))
            ch.sync()
            ch.step(V.tensor_tensor(m_eq, m_eq, m_ge, ALU.mult))
            ch.add(V.memset(sel[:, :, 8:9], 0.0))
            V.tensor_tensor(sel[:, :, 0:8], m_eq, m_gt, ALU.add).then_inc(sem("sel_done"), 1)
            dve.wait_ge(sem("sel_done"), 1)
            dve.wait_ge(sem("top_exp"), 1)
            ch.step(V.tensor_tensor(gates, gates, sel[:, :, 0:8], ALU.mult))
            for t in range(NT):
                ch.add(V.tensor_reduce(n_gt[:, t, 1:2], gates[:, t, :], AX.X, ALU.add))
            ch.sync()
            ch.step(V.reciprocal(n_gt[:, :, 1:2], n_gt[:, :, 1:2]))
            for t in range(NT):
                ch.add(V.tensor_scalar(gates[:, t, :], gates[:, t, :], n_gt[:, t, 1:2], None, ALU.mult))
            ch.sync()

        def unit_ready_in(pe, base, e, i):
            n = base + i
            pe.wait_ge(sem(f"unit_in{n % RING}"), e * (16 * FFE_UNITS // RING) + 16 * (n // RING + 1))

        hidT = bview(0, 4, S)
        silu_g = bview(1, 2, S)

        def gate_up_T(n, q, dst, acts):
            for k in range(KD):
                w = ring[(n + k // 4) % RING][:, :].rearrange("p (k c) -> p k c", k=4)
                last = MM(dst, w[:, k % 4, q * P:(q + 1) * P], acts[:, k, :], start=(k == 0), stop=(k == KD - 1))
            return last

        def moe_tensor(pe):
            base, steps = AT["moe"], FFE_STEPS
            gate, down = swiglu_order(steps)
            with pe.Fori(0, EXPERTS) as e:
                def down_product(s):
                    unit_ready_in(pe, base, e, down[s])
                    pe.wait_ge(sem("moe_hidden"), e * (2 * steps) + (2 * s + 2))
                    if s == 0:
                        pe.wait_ge(sem("moe_added"), e + 1)
                    product_rows(base + down[s], hidT[:, 2 * (s % 2):2 * (s % 2) + 2, :], s == 0, s == steps - 1)\
                        .then_inc(sem("unit_used"), 1)

                for s in range(steps):
                    for u in range(2):
                        unit_ready_in(pe, base, e, gate[s] + u)
                    for which in range(2):
                        for j in range(2):
                            if s and not which:
                                pe.wait_ge(sem("moe_hidden"), e * (2 * steps) + (2 * s - 1 + j))
                            last = gate_up_T(base + gate[s], 2 * which + j, bank[2 * which + j][:, 0:S], xnT)
                            if which and j:
                                last.then_inc(sem("unit_used"), 2)
                            else:
                                last.then_inc(sem("moe_up" if which else "moe_gate"), 1)
                    if s:
                        down_product(s - 1)
                down_product(steps - 1)

        def moe_scalar(act):
            base, steps = AT["moe"], FFE_STEPS
            gate, _ = swiglu_order(steps)
            with act.Fori(0, EXPERTS) as e:
                for s in range(steps):
                    for j in range(2):
                        act.wait_ge(sem("moe_gate"), e * (2 * steps) + (2 * s + j + 1))
                        if s or j:
                            act.wait_ge(sem("moe_hidden"), e * (2 * steps) + max(2 * s + j - 1, 1))
                        else:
                            act.wait_ge(sem("moe_added"), e + 1)
                        ACTV(silu_g[:, j, :], bank[j][:, 0:S], ACT.Silu).then_inc(sem("moe_silu"), 1)
                ACTV(counts[:, 1:2], counts[:, 0:1], ACT.Copy).then_inc(sem("split_high"), FFE_UNITS)
            dense_done(act)
            for i in range(AHEAD):
                split_high_in(act, EXPERTS - 1, FFE_UNITS + i)

        def moe_vector(dve, ch):
            base, steps = AT["moe"], FFE_STEPS
            gate, down = swiglu_order(steps)
            with dve.Fori(0, EXPERTS) as e:
                for s in range(steps):
                    for j in range(2):
                        dve.wait_ge(sem("moe_silu"), e * (2 * steps) + (2 * s + j + 1))
                        if j == 0:
                            dve.wait_ge(sem("moe_up"), e * steps + (s + 1))
                        else:
                            dve.wait_ge(sem("unit_used"), e * FFE_UNITS + (base + gate[s] + 2))
                        if s >= 2:
                            dve.wait_ge(sem("unit_used"), e * FFE_UNITS + (base + down[s - 2] + 1))
                        V.tensor_tensor(hidT[:, 2 * (s % 2) + j, :], silu_g[:, j, :], bank[2 + j][:, 0:S], ALU.mult)\
                            .then_inc(sem("moe_hidden"), 1)
                dve.wait_ge(sem("unit_used"), e * FFE_UNITS + (base + FFE_UNITS))
                for t in range(NT):
                    for c in range(2):
                        o = slice(c * 512, (c + 1) * 512)
                        last = V.scalar_tensor_tensor(h[:, t, o], bank[4 + 2 * t + c][:, :],
                                                      gates[:, t, bass.ds(e, 1)], h[:, t, o], ALU.mult, ALU.add)
                last.then_inc(sem("moe_added"), 1)
                V.tensor_copy(counts[:, 2:3], counts[:, 0:1]).then_inc(sem("split_low"), FFE_UNITS)
            dense_done(dve)
            for i in range(AHEAD):
                split_low_in(dve, EXPERTS - 1, FFE_UNITS + i)

        def dense_done(eng):
            eng.wait_ge(sem("moe_added"), EXPERTS + 1)

        slot_of, counts = tin(NT, EXPERTS + 1), tin(EXPERTS + 1)
        s_xT = bview_r(3, KD, P), bview_r(3, KD, P, off=1024)
        s_x = bview(3, KD, P, off=1024)
        s_pick = bview(4, NT, P)
        s_gpick = bview(4, NT, P, off=256)
        s_gpickT = bview(4, NT, P, off=512)
        s_hid = bview(4, 2, 256, off=1024)
        s_silu = bview(4, 2, 256, off=1536)
        s_hidT = bview_r(5, 4, P), bview_r(5, 4, P, off=512)
        s_y = bview(5, D, off=1024)
        GU_UNITS = [swiglu_order(FFE_STEPS)[0][s] for s in range(FFE_STEPS)]
        DOWN_UNITS = swiglu_order(FFE_STEPS)[1]

        def slots_tensor(pe):
            pe.wait_ge(sem("sel_done"), 1)
            MM(bank[1][:, 0:8], const("before"), sel[:, 0, 0:8], start=True, stop=True)
            MM(bank[1][:, 8:16], const("ones"), sel[:, 0, 0:8], start=True, stop=False)
            MM(bank[1][:, 8:16], const("before"), sel[:, 1, 0:8], start=False, stop=True)
            MM(bank[1][:, 16:24], const("ones"), sel[:, 0, 0:8], start=True, stop=False)
            MM(bank[1][:, 16:24], const("ones"), sel[:, 1, 0:8], start=False, stop=True).then_inc(sem("slots"), 1)

        def slots_vector(dve, ch):
            dve.wait_ge(sem("slots"), 1)
            ch.add(V.tensor_copy(slot_of[:, :, 0:8], bank[1][:, 0:16].rearrange("p (t e) -> p t e", t=NT)))
            ch.step(V.tensor_reduce(counts[:, 0:1], bank[1][:, 16:24], AX.X, ALU.max))
            V.tensor_scalar(crowded[:, :], counts[:, 0:1], float(P), None, ALU.is_gt).then_inc(sem("crowded"), 1)

        def is_crowded(eng):
            eng.wait_ge(sem("crowded"), 1)
            return eng.value_load(crowded[0:1, 0:1], min_val=0, max_val=1)

        def pick(dst, e, weight):
            for t in range(NT):
                last = V.tensor_scalar(dst[:, t, :], const("iota"), slot_of[:, t, bass.ds(e, 1)],
                                       weight[:, t, bass.ds(e, 1)], ALU.is_equal, ALU.mult)
            return last

        def gather(pe):
            for k in range(KD):
                for t in range(NT):
                    last = MM(bank[6 + k // 4][:, (k % 4) * P:(k % 4 + 1) * P], xn[:, t, k * P:(k + 1) * P],
                              s_pick[:, t, :], start=(t == 0), stop=(t == NT - 1))
            last.then_inc(sem("sp_gathered"), 1)

        def gathered(dve, e):
            dve.wait_ge(sem("sp_gathered"), e + 1)
            hi, lo = s_xT
            for j in range(2):
                V.tensor_tensor(s_x[:, 4 * j:4 * j + 4, :], psum4(6 + j),
                                over_heads(const("gain", 8, KD)[:, 3, 4 * j:4 * j + 4], 4, P), ALU.mult)\
                    .then_inc(sem("sp_x_scaled"), 1)
            dve.wait_ge(sem("sp_x_scaled"), e * 3 + 2)
            V.tensor_copy(hi, s_x).then_inc(sem("sp_x_scaled"), 1)
            dve.wait_ge(sem("sp_x_scaled"), e * 3 + 3)
            V.tensor_tensor(lo, s_x, hi.bitcast(F32), ALU.subtract).then_inc(sem("sp_xT"), 1)

        def split_high_in(act, e, i):
            n = AT["moe"] + i
            unit_ready_in(act, AT["moe"], e, i)
            act.wait_ge(sem("unit_used"), e * FFE_UNITS + (n - len(HI["moe"]) + 1))
            ACTV(high_room("moe", i), ring[n % RING][:, :], ACT.Copy)\
                .then_inc(sem("split_high"), 1)

        def split_low_in(dve, e, i):
            n = AT["moe"] + i
            dve.wait_ge(sem("split_high"), e * FFE_UNITS + (SPLITS["moe"] + i + 1))
            V.tensor_tensor(ring_r[n % RING][:, :], ring[n % RING][:, :], high_room("moe", i).bitcast(F32),
                            ALU.subtract).then_inc(sem("split_low"), 1)

        def split_ready_in(pe, e, i):
            pe.wait_ge(sem("split_low"), e * FFE_UNITS + (SPLITS["moe"] + i + 1))

        SCATTER_STEPS = (1, 2)

        def scatter(pe, e, t):
            if t == 0:
                pe.wait_ge(sem("sp_y"), 2 * e + 2)
                pe.wait_ge(sem("sp_xT"), e + 1)
            else:
                pe.wait_ge(sem("sp_added"), 2 * e + 2)
            for c in range(2):
                last = MM(bank[6 + c][:, :], s_gpickT[:, t, :], s_y[:, c * 512:(c + 1) * 512], start=True, stop=True)
            last.then_inc(sem("sp_scattered"), 1)

        def add_scattered(dve, e, t):
            dve.wait_ge(sem("sp_scattered"), 2 * e + (t + 1))
            for c in range(2):
                o = slice(c * 512, (c + 1) * 512)
                last = V.tensor_tensor(h[:, t, o], h[:, t, o], bank[6 + c][:, :], ALU.add)
            last.then_inc(sem("sp_added"), 1)

        def sparse_tensor(pe):
            base, steps = AT["moe"], FFE_STEPS
            pe.wait_ge(sem("sp_pick"), 1)
            gather(pe)
            with pe.Fori(0, EXPERTS) as e:
                def gate_up(s, k0):
                    i = GU_UNITS[s] + k0 // 4
                    split_ready_in(pe, e, i)
                    hi, lo = high("moe", i, 4), low("moe", i, 4)
                    for k in range(4):
                        last = three_passes(bank[s % 2][:, :], [a[:, k0 + k, :] for a in s_xT],
                                            (hi[:, k, :], lo[:, k, :]), k0 + k == 0, k0 + k == KD - 1)
                    last.then_inc(sem("unit_used"), 1)

                def hidden_T(s):
                    pe.wait_ge(sem("sp_hid"), e * steps + (s + 2))
                    for f in range(2):
                        last = nc.tensor.transpose(bank[2][:, (2 * (s % 2) + f) * P:(2 * (s % 2) + f + 1) * P],
                                                   s_hid[:, s % 2, f * P:(f + 1) * P], ident)
                    last.then_inc(sem("sp_hidT"), 1)

                def down(s):
                    i = DOWN_UNITS[s]
                    split_ready_in(pe, e, i)
                    hi, lo = high("moe", i, 2), low("moe", i, 2)
                    pe.wait_ge(sem("sp_hidT_low"), e * steps + (s + 1))
                    if s == 0:
                        pe.wait_ge(sem("sp_y"), 2 * e + 2)
                    for f in range(2):
                        for c in range(2):
                            o = slice(c * 512, (c + 1) * 512)
                            last = three_passes(bank[4 + c][:, :],
                                                [a[:, 2 * (s % 2) + f, :] for a in s_hidT],
                                                (hi[:, f, o], lo[:, f, o]), s == 0 and f == 0,
                                                s == steps - 1 and f == 1)
                    last.then_inc(sem("unit_used"), 1)

                for s in range(steps):
                    if s == 0:
                        pe.wait_ge(sem("sp_xT"), e + 1)
                    gate_up(s, 0)
                    if s:
                        hidden_T(s - 1)
                    gate_up(s, 4)
                    if s:
                        down(s - 1)
                    if s in SCATTER_STEPS:
                        scatter(pe, e, s - 1)
                    if s == 4:
                        pe.wait_ge(sem("sp_gpick"), e + 1)
                        for t in range(NT):
                            last = nc.tensor.transpose(bank[3][:, t * P:(t + 1) * P], s_gpick[:, t, :], ident)
                        last.then_inc(sem("sp_gpickT"), 1)
                    if s == 9:
                        pe.wait_ge(sem("sp_pick"), e + 2)
                        pe.wait_ge(sem("sp_added"), 2 * e + 3)
                        gather(pe)
                hidden_T(steps - 1)
                down(steps - 1)
            for t in range(NT):
                scatter(pe, EXPERTS, t)

        def sparse_scalar(act):
            base, steps = AT["moe"], FFE_STEPS
            for i in range(AHEAD):
                split_high_in(act, 0, i)
            with act.Fori(0, EXPERTS) as e:
                def hidden_high(s):
                    act.wait_ge(sem("sp_hidT"), e * steps + (s + 1))
                    ACTV(s_hidT[0][:, 2 * (s % 2):2 * (s % 2) + 2, :],
                         psum4(2)[:, 2 * (s % 2):2 * (s % 2) + 2, :], ACT.Copy).then_inc(sem("sp_hidT_high"), 1)

                for s in range(steps):
                    split_high_in(act, e, GU_UNITS[s] + AHEAD)
                    if s:
                        hidden_high(s - 1)
                    split_high_in(act, e, GU_UNITS[s] + 1 + AHEAD)
                    act.wait_ge(sem("unit_used"), e * FFE_UNITS + (base + GU_UNITS[s] + 2))
                    if s >= 2:
                        act.wait_ge(sem("sp_hid"), e * steps + s)
                    ACTV(s_silu[:, s % 2, :], bank[s % 2][:, 0:256], ACT.Silu).then_inc(sem("sp_silu"), 1)
                    if s:
                        split_high_in(act, e, DOWN_UNITS[s - 1] + AHEAD)
                    if s == 6:
                        act.wait_ge(sem("sp_gpickT"), e + 1)
                        ACTV(s_gpickT, psum4(3)[:, 0:NT, :], ACT.Copy)
                hidden_high(steps - 1)
                split_high_in(act, e, DOWN_UNITS[steps - 1] + AHEAD)
                act.wait_ge(sem("unit_used"), e * FFE_UNITS + (base + FFE_UNITS))
                ACTV(s_y[:, 0:512], bank[4][:, :], ACT.Copy).then_inc(sem("sp_y"), 1)

        def sparse_vector(dve, ch):
            base, steps = AT["moe"], FFE_STEPS
            for t in range(NT):
                last = V.tensor_scalar(s_pick[:, t, :], const("iota"), slot_of[:, t, 0:1], sel[:, t, 0:1],
                                       ALU.is_equal, ALU.mult)
            last.then_inc(sem("sp_pick"), 1)
            split_low_in(dve, 0, 0)
            gathered(dve, 0)
            for i in range(1, AHEAD):
                split_low_in(dve, 0, i)
            with dve.Fori(0, EXPERTS) as e:
                def hidden_low(s):
                    dve.wait_ge(sem("sp_hidT_high"), e * steps + (s + 1))
                    o = slice(2 * (s % 2), 2 * (s % 2) + 2)
                    V.tensor_tensor(s_hidT[1][:, o, :], psum4(2)[:, o, :], s_hidT[0][:, o, :].bitcast(F32),
                                    ALU.subtract).then_inc(sem("sp_hidT_low"), 1)

                for s in range(steps):
                    split_low_in(dve, e, GU_UNITS[s] + AHEAD)
                    if s:
                        hidden_low(s - 1)
                    split_low_in(dve, e, GU_UNITS[s] + 1 + AHEAD)
                    dve.wait_ge(sem("sp_silu"), e * steps + (s + 1))
                    if s >= 2:
                        dve.wait_ge(sem("sp_hidT"), e * steps + (s - 1))
                    V.tensor_tensor(s_hid[:, s % 2, :], s_silu[:, s % 2, :], bank[s % 2][:, 256:512], ALU.mult)\
                        .then_inc(sem("sp_hid"), 1)
                    if s == steps - 1:
                        gathered(dve, e + 1)
                        hidden_low(s)
                    if s:
                        split_low_in(dve, e, DOWN_UNITS[s - 1] + AHEAD)
                    if s in SCATTER_STEPS:
                        add_scattered(dve, e, s - 1)
                    if s == 3:
                        pick(s_gpick, e, gates).then_inc(sem("sp_gpick"), 1)
                    if s == 6:
                        pick(s_pick, e + 1, sel).then_inc(sem("sp_pick"), 1)
                split_low_in(dve, e, DOWN_UNITS[steps - 1] + AHEAD)
                dve.wait_ge(sem("unit_used"), e * FFE_UNITS + (base + FFE_UNITS))
                V.tensor_copy(s_y[:, 512:1024], bank[5][:, :]).then_inc(sem("sp_y"), 1)
            for t in range(NT):
                add_scattered(dve, EXPERTS, t)

        def experts_tensor(pe):
            slots_tensor(pe)
            with pe.If(is_crowded(pe)):
                moe_tensor(pe)
            with pe.Else():
                sparse_tensor(pe)

        def experts_scalar(act):
            with act.If(is_crowded(act)):
                moe_scalar(act)
            with act.Else():
                sparse_scalar(act)

        def experts_vector(dve, ch):
            slots_vector(dve, ch)
            for i, name in enumerate(("sp_hid", "sp_added", "moe_added")):
                V.memset(counts[:, i + 1:i + 2], 0.0).then_inc(sem(name), 1)
            for room in (s_y, s_gpickT):
                V.memset(room, 0.0).then_inc(sem("sp_y"), 1)
            ch.add(V.memset(slot_of[:, :, 8:9], 0.0))
            ch.sync()
            dve.wait_ge(sem("moe_added"), 1)
            with dve.If(is_crowded(dve)):
                moe_vector(dve, ch)
                V.tensor_copy(n_gt[:, :, 2:3], n_gt[:, :, 1:2]).then_inc(sem("h_done"), NT)
            with dve.Else():
                sparse_vector(dve, ch)
                dve.wait_ge(sem("sp_added"), 2 * EXPERTS + 3)
                V.tensor_copy(n_gt[:, :, 2:3], n_gt[:, :, 1:2]).then_inc(sem("h_done"), NT)

        mem_rows = bview(8, NT, D)
        memT = bview(7, KD, S)
        mem_kT = bview(3, MH, S)
        mem_v = bview(3, NT, 512, off=1024)
        hg_q, hg_k = bview(0, MH, S), bview(0, MH, S, off=1024)
        hg_qs, hg_b = bview(1, MH, S), bview(1, MH, S, off=1024)
        hg_ks, hg_kl = bview(2, MH, S), bview(2, MH, S, off=1024)
        hg_kl_rows, hg_scores = bview(4, 8, P), bview(4, 8, P, off=1024)
        hg_v, hg_gate = bview(5, NT, 512), bview(5, NT, 512, off=1024)
        hg_sq, hg_y = bview(2, 8, P), bview(2, 8, P, off=1024)
        hg_S = [buf[11][:, i * 512:(i + 1) * 512].rearrange("p (a b) -> p a b", b=P) for i in range(3)]
        xn_a = xn[:, 0, :].rearrange("p (a b) -> p a b", b=S)
        xn_b = xn[:, 1, :].rearrange("p (a b) -> p a b", b=S)
        dil_q = [bview(6, MH, S), bview(7, MH, S, off=1024), xn_a]
        dil_k = [bview(6, MH, S, off=1024), bview(8, MH, S), xn_b]
        dil_v = [bview(7, NT, 512), bview(8, NT, 512, off=1024), bview(10, NT, 512)]
        mem_q = bview(10, MH, S, off=1024)
        y_hgT, y_dilT, y_memT = bview(0, MH, S, off=1024), bview(4, MH, S), bview(5, MH, S)
        gl = [bview(6 + i, KD, S) for i in range(3)]
        mixed = bview(10, KD, S)
        mix_t = bview(11, 2, S)
        lb, one_lb, lg_d, lg_e = tin(MH), tin(MH), tin(2 * MH), tin(2 * MH)
        hg_ssq, hg_rstd = tin(8), tin(8)

        def product_any(n, kind, j, dst, acts):
            return product_T(n, j, dst, acts) if kind == "T" else product(n, j, dst, acts)

        def in_jobs(base, parts):
            jobs = []
            for kind, units in parts:
                for u in range(units):
                    for j in range(2):
                        jobs.append((base, kind, j))
                    base += 1
            return jobs

        def jobs_tensor(pe, past, jobs, acts, banks, stage=None):
            for i, (n, kind, j) in enumerate(jobs):
                if stage:
                    split_ready(pe, stage, i // 2)
                else:
                    unit_ready(pe, n)
                if i >= len(banks):
                    pe.wait_ge(sem("job_read"), past + i - len(banks) + 1)
                dst = bank[banks[i % len(banks)]][:, 0:S]
                if stage:
                    last = (split_product_T if kind == "T" else split_product)(stage, i // 2, j, dst)
                else:
                    last = product_any(n, kind, j, dst, acts)
                last.then_inc(sem("unit_used" if j else "half_done"), 1)

        def jobs_scalar(act, past, jobs, banks, first, outs, stage=None):
            for i, (dst, func, scale, bias) in enumerate(outs, first):
                n, _, j = jobs[i]
                if stage and j and i // 2 + len(HI[stage]) < len(jobs) // 2:
                    split_high(act, stage, i // 2 + len(HI[stage]))
                if j:
                    act.wait_ge(sem("unit_used"), n + 1)
                else:
                    half_done(act, n)
                src = bank[banks[i % len(banks)]][:, 0:S]
                if bias is None:
                    ins = ACTV(dst, src, func, scale=scale)
                else:
                    ins = ACTV(dst, src, func, scale=scale, bias=bias)
                ins.then_inc(sem("job_read"), 1)

        def outs_T(dst, func=ACT.Copy, scale=1.0):
            return [(dst[:, c, :], func, scale, None) for c in range(MH)]

        def outs_rows(dst, func=ACT.Copy):
            return [(dst[:, t, u * 256:(u + 1) * 256], func, 1.0, None) for u in range(2) for t in range(NT)]

        kv_jobs = in_jobs(AT["mem_kv"], [("T", 2), ("rows", 2)])
        kv_outs = outs_T(mem_kT) + outs_rows(mem_v)
        hg_jobs = in_jobs(AT["hg_in"], [("T", 4), ("rows", 4)] + [("T", 4), ("rows", 2)] * DIL + [("T", 2)])
        hg_outs = outs_T(hg_q, ACT.Silu) + outs_T(hg_k, ACT.Sigmoid) + outs_rows(hg_v) + outs_rows(hg_gate, ACT.Sigmoid)
        dil_outs = []
        for g in range(DIL):
            dil_outs += outs_T(dil_q[g], scale=P ** -0.5) + outs_T(dil_k[g]) + outs_rows(dil_v[g])
        dil_outs += outs_T(mem_q, scale=P ** -0.5)
        gl_jobs = in_jobs(AT["gl_in"], [("T", 12)])
        gl_outs = [(gl[i // KD][:, i % KD, :], ACT.Sigmoid, 1.0, const("b_gate")[:, i:i + 1]) for i in range(24)]
        FOUR = (0, 1, 2, 3)
        JOBS_KV, JOBS_HG, JOBS_GL = 0, len(kv_jobs), len(kv_jobs) + len(hg_jobs)

        def chunks(a):
            return flat(a).rearrange("p (a b) -> p a b", b=CHUNK)

        def hg_prepare(dve, ch):
            l = const("hg_logits")
            ch.step(V.tensor_tensor(lb, l[:, 0:MH], l[:, MH:2 * MH], ALU.max))
            ch.step(V.tensor_tensor(lg_d[:, 0:MH], l[:, 0:MH], lb, ALU.subtract))
            V.tensor_tensor(lg_d[:, MH:2 * MH], l[:, MH:2 * MH], lb, ALU.subtract).then_inc(sem("lb_arg"), 1)
            dve.wait_ge(sem("lb_exp"), 1)
            ch.step(V.tensor_tensor(one_lb, lg_e[:, 0:MH], lg_e[:, MH:2 * MH], ALU.add))
            ch.step(V.reciprocal(one_lb, one_lb))
            ch.step(V.tensor_tensor(lb, lg_e[:, 0:MH], one_lb, ALU.mult))
            ch.step(V.tensor_scalar(one_lb, lb, -1.0, 1.0, ALU.mult, ALU.add))

        def hg_prepare_scalar(act):
            act.wait_ge(sem("lb_arg"), 1)
            ACTV(lg_e, lg_d, ACT.Exp).then_inc(sem("lb_exp"), 1)

        def hg_decay_scalar(act):
            act.wait_ge(sem("hg_f"), 1)
            ACTV(flat(hg_qs), flat(hg_k), ACT.Ln).then_inc(sem("hg_ln"), 1)
            act.wait_ge(sem("hg_sums"), 1)
            ACTV(flat(hg_ks), flat(hg_qs), ACT.Exp, scale=-1.0).then_inc(sem("hg_exp"), 1)
            ACTV(flat(hg_kl), flat(hg_kl), ACT.Exp).then_inc(sem("hg_exp"), 1)
            act.wait_ge(sem("hg_exp"), 1)
            ACTV(flat(hg_qs), flat(hg_qs), ACT.Exp).then_inc(sem("hg_exp"), 1)
            ACTV(flat(hg_b), flat(hg_b), ACT.Exp).then_inc(sem("hg_exp"), 1)

        def hg_decay_vector(dve, ch):
            dve.wait_ge(sem("job_read"), JOBS_HG + 16)
            for c in range(MH):
                last = V.tensor_scalar(hg_k[:, c, :], hg_k[:, c, :], one_lb[:, c:c + 1], lb[:, c:c + 1],
                                       ALU.mult, ALU.add)
            last.then_inc(sem("hg_f"), 1)
            dve.wait_ge(sem("hg_ln"), 1)
            ch.add(V.tensor_scalar(flat(hg_k), flat(hg_k), -1.0, 1.0, ALU.mult, ALU.add))
            for c in range(MH):
                ch.add(V.tensor_tensor_scan(hg_b[:, c, :], const("reset"), hg_qs[:, c, :], 0.0, ALU.mult, ALU.add))
            ch.sync()
            b = chunks(hg_b)
            mid = b[:, :, CHUNK // 2 - 1:CHUNK // 2].broadcast_to([P, 16, CHUNK])
            end = b[:, :, CHUNK - 1:CHUNK].broadcast_to([P, 16, CHUNK])
            V.tensor_tensor(chunks(hg_qs), b, mid, ALU.subtract)
            V.tensor_tensor(chunks(hg_kl), end, b, ALU.subtract).then_inc(sem("hg_sums"), 1)
            dve.wait_ge(sem("hg_exp"), 1)
            ch.add(V.tensor_tensor(flat(hg_ks), flat(hg_ks), flat(hg_k), ALU.mult))
            dve.wait_ge(sem("hg_exp"), 2)
            ch.add(V.tensor_tensor(flat(hg_kl), flat(hg_kl), flat(hg_k), ALU.mult))
            dve.wait_ge(sem("hg_exp"), 3)
            ch.add(V.tensor_tensor(flat(hg_qs), flat(hg_qs), flat(hg_q), ALU.mult))
            dve.wait_ge(sem("hg_exp"), 4)
            ch.sync()
            V.tensor_tensor(flat(hg_q), flat(hg_q), flat(hg_b), ALU.mult).then_inc(sem("hg_factors"), 1)

        def hg_tensor(pe):
            pe.wait_ge(sem("hg_factors"), 1)
            pe.wait_ge(sem("job_read"), JOBS_HG + len(hg_jobs))
            for i in range(8):
                t, e = i // MH, i % MH
                last = nc.tensor.transpose(bank[i // 4][:, e * P:(e + 1) * P], hg_kl[:, e, t * P:(t + 1) * P], ident)
            last.then_inc(sem("hg_klT"), 1)
            for i in range(8):
                t, e = i // MH, i % MH
                last = MM(bank[2 + i // 4][:, e * P:(e + 1) * P], hg_ks[:, e, t * P:(t + 1) * P],
                          hg_qs[:, e, t * P:(t + 1) * P], start=True, stop=True)
            last.then_inc(sem("hg_ST"), 1)
            pe.wait_ge(sem("hg_kl_rows"), 1)
            for c in range(3):
                t, r = c // 2, slice(CHUNK * (c % 2), CHUNK * (c % 2) + CHUNK)
                for e in range(MH):
                    last = MM(bank[4 + c][:, e * P:(e + 1) * P], hg_kl_rows[r, MH * t + e, :],
                              hg_v[r, t, e * P:(e + 1) * P], start=True, stop=True)
            last.then_inc(sem("hg_kv"), 1)
            pe.wait_ge(sem("hg_masked"), 1)
            pe.wait_ge(sem("hg_states"), 1)
            for i in range(8):
                t, e = i // MH, i % MH
                dst = bank[t][:, e * P:(e + 1) * P]
                MM(dst, hg_scores[:, i, :], hg_v[:, t, e * P:(e + 1) * P], start=True, stop=True)
                for c in (2 * t, 2 * t + 1):
                    if c:
                        r = slice(CHUNK * (c % 2), CHUNK * (c % 2) + CHUNK)
                        last = MM(bank[t][r, e * P:(e + 1) * P],
                                  hg_q[:, e, c * CHUNK:(c + 1) * CHUNK], hg_S[c - 1][:, e, :],
                                  start=False, stop=True, skip_group_check=True)
            last.then_inc(sem("hg_o"), 1)
            pe.wait_ge(sem("hg_y"), 1)
            for i in range(8):
                t, e = i // MH, i % MH
                last = nc.tensor.transpose(bank[2 + e // 2][:, (e % 2) * S + t * P:(e % 2) * S + (t + 1) * P],
                                           hg_y[:, i, :], ident)
            last.then_inc(sem("hg_yT"), 1)

        def hg_scalar(act):
            act.wait_ge(sem("hg_o"), 1)
            for t in range(NT):
                last = ACTV(hg_sq[:, MH * t:MH * t + MH, :], psum4(t), ACT.Square)
            last.then_inc(sem("hg_osq"), 1)

        def hg_vector(dve, ch):
            dve.wait_ge(sem("job_read"), JOBS_HG + len(hg_jobs))
            ch.step(V.memset(flat(hg_scores), 0.0))
            dve.wait_ge(sem("hg_klT"), 1)
            for j in range(2):
                last = V.tensor_copy(hg_kl_rows[:, 4 * j:4 * j + 4, :], psum4(j))
            last.then_inc(sem("hg_kl_rows"), 1)
            dve.wait_ge(sem("hg_ST"), 1)
            mask = per_head(const("cum").bitcast(U32), 4, P)
            for j in range(2):
                last = V.copy_predicated(hg_scores[:, 4 * j:4 * j + 4, :], mask, psum4(2 + j))
            last.then_inc(sem("hg_masked"), 1)
            dve.wait_ge(sem("hg_kv"), 1)
            ch.step(V.tensor_copy(hg_S[0], psum4(4)))
            for c in (1, 2):
                for e in range(MH):
                    end = (c + 1) * CHUNK - 1
                    last = V.scalar_tensor_tensor(hg_S[c][:, e, :], hg_S[c - 1][:, e, :], hg_b[:, e, end:end + 1],
                                                  psum4(4 + c)[:, e, :], ALU.mult, ALU.add)
                    if c == 1:
                        ch.add(last)
                ch.sync()
            last.then_inc(sem("hg_states"), 1)
            dve.wait_ge(sem("hg_osq"), 1)
            ch.step(V.tensor_reduce(hg_ssq, hg_sq, AX.X, ALU.add))
            V.tensor_scalar(hg_ssq, hg_ssq, 1.0 / P, EPS, ALU.mult, ALU.add).then_inc(sem("head_var"), 1)
            dve.wait_ge(sem("head_rstd"), NT + 4)
            for t in range(NT):
                ch.add(V.tensor_tensor(hg_y[:, MH * t:MH * t + MH, :], psum4(t),
                                       over_heads(hg_rstd[:, MH * t:MH * t + MH], MH, P), ALU.mult))
            ch.sync()
            ch.step(V.tensor_tensor(hg_y, hg_y, per_head(const("hg_norm"), 8, P), ALU.mult))
            V.tensor_tensor(hg_y, hg_y, flat(hg_gate).rearrange("p (a b) -> p a b", b=P), ALU.mult)\
                .then_inc(sem("hg_y"), 1)
            dve.wait_ge(sem("hg_yT"), 1)
            for j in range(2):
                V.tensor_copy(y_hgT[:, 2 * j:2 * j + 2, :], bank[2 + j][:, :].rearrange("p (a b) -> p a b", b=S))\
                    .then_inc(sem("hg_out"), 1)

        def hg_pool(pool):
            pool.wait_ge(sem("head_var"), NT + 4)
            G.tensor_tensor(hg_rstd, hg_ssq, minus_half, ALU.pow).then_inc(sem("head_rstd"), 1)

        def att2_units():
            units = []
            for t in range(NT):
                w = (t + 1) * P
                q = slice(t * P, (t + 1) * P)
                for e in range(MH):
                    units.append(dict(
                        score=[(g * w, w, dil_q[g][:, e, q], dil_k[g][:, e, 0:w]) for g in range(DIL)],
                        mask=[(g * w, w, dist[:, g, 2 * P - w:2 * P], SLOPES[MH * g + e])
                              for g in range(DIL)],
                        spans=[(0, DIL * w)], block=lambda b: b * P, sink=None,
                        values=[dil_v[g][:, b, e * P:(e + 1) * P] for g in range(DIL) for b in range(t + 1)],
                        rows=(0, P), out=y_dilT[:, e, q]))
                    units.append(dict(
                        score=[(0, S, mem_q[:, e, q], mem_kT[:, e, :])], mask=[(0, S, None, None)],
                        spans=[(0, S)], block=lambda b: b * P, sink=None,
                        values=[mem_v[:, b, e * P:(e + 1) * P] for b in range(2)],
                        rows=(0, P), out=y_memT[:, e, q]))
            return units

        att2 = att2_units()

        def att2_before(pe):
            pe.wait_ge(sem("hg_out"), 2)

        def branch_tensor(pe):
            pe.wait_ge(sem("att_out"), len(att0) + len(att2))
            for i in range(24):
                b, d = i // KD, i % KD
                n = AT["branch"] + i // 4
                unit_ready(pe, n)
                w = ring[n % RING][:, :].rearrange("p (k c) -> p k c", k=4)
                if i >= 4:
                    pe.wait_ge(sem("branch_read"), i - 3)
                else:
                    pe.wait_ge(sem("job_read"), JOBS_GL + 24)
                acts = (y_hgT, y_dilT, y_memT)[b]
                for k in range(4):
                    last = MM(bank[i % 4][:, 0:S], w[:, k, (i % 4) * P:(i % 4 + 1) * P], acts[:, k, :],
                              start=(k == 0), stop=(k == 3))
                last.then_inc(sem("unit_used" if i % 4 == 3 else "branch_done"), 1)

        def branch_vector(dve, ch):
            dve.wait_ge(sem("job_read"), JOBS_GL + 24)
            for i in range(24):
                b, d = i // KD, i % KD
                if i % 4 == 3:
                    dve.wait_ge(sem("unit_used"), AT["branch"] + i // 4 + 1)
                else:
                    dve.wait_ge(sem("branch_done"), 3 * (i // 4) + i % 4 + 1)
                if b == 0:
                    V.tensor_tensor(mixed[:, d, :], gl[b][:, d, :], bank[i % 4][:, 0:S], ALU.mult)\
                        .then_inc(sem("branch_read"), 1)
                else:
                    ins = V.tensor_tensor(mix_t[:, i % 2, :], gl[b][:, d, :], bank[i % 4][:, 0:S], ALU.mult)
                    ins.then_inc(sem("branch_read"), 1)
                    dve.wait_ge(sem("branch_read"), i + 1)
                    ins = V.tensor_tensor(mixed[:, d, :], mixed[:, d, :], mix_t[:, i % 2, :], ALU.add)
                    if b == 2:
                        ins.then_inc(sem("mixed_done"), 1)
                    else:
                        ch.add(ins)
                if i % KD == KD - 1:
                    ch.sync()

        def load_later(act, i):
            act.dma_start(later(6), post_d[3 + i, :, 0:6 * P].rearrange("p (a b) -> p a b", b=P))\
                .then_inc(sem("later_in"), 16)

        def load_post(act, i):
            act.dma_start(post_gain, post_d[i, :, :]).then_inc(sem("post_in"), 16)

        block = ctx.enter_context(nc.Block())

        @block.sync
        def _(sp):
            sp.dma_start(h[:, :, :], x_d.rearrange("(t p) d -> p t d", p=P)).then_inc(sem("x_in"), 16)
            sp.dma_start(small[:, 0:FIRST], small_d[:, 0:FIRST]).then_inc(sem("small_in"), 16)
            for s in range(RING):
                sp.dma_start(ring[s][:, :], w_d[s, :, :]).then_inc(sem(f"unit_in{s}"), 16)
                if s == 1:
                    sp.dma_start(small[:, FIRST:], small_d[:, FIRST:]).then_inc(sem("rest_in"), 16)
            whole = UNITS // RING
            with sp.Fori(1, whole) as g:
                for s in range(RING):
                    sp.wait_ge(sem("unit_used"), g * RING + (s + 1 - RING))
                    sp.dma_start(ring[s][:, :], w_d[g * RING + s, :, :]).then_inc(sem(f"unit_in{s}"), 16)
            for n in range(whole * RING, UNITS):
                sp.wait_ge(sem("unit_used"), n - RING + 1)
                sp.dma_start(ring[n % RING][:, :], w_d[n, :, :]).then_inc(sem(f"unit_in{n % RING}"), 16)
            for t in range(NT):
                sp.wait_ge(sem("h_done"), NT * (SUBLAYERS - 1) + t + 1)
                sp.dma_start(out_d[t * P:(t + 1) * P, :], h[:, t, :]).then_inc(sem("out_written"), 16)
            sp.wait_ge(sem("out_written"), 16 * NT)

        @block.tensor
        def _(pe):
            pe.wait_ge(sem("small_in"), 16)
            norm_transpose(pe, 0)
            mix0_tensor(pe)
            att_tensor(pe, 0, att0, att0_before)

            def mix0_ready(pe):
                pe.wait_ge(sem("att_out"), len(att0))
                pe.wait_ge(sem("lru_y"), 1)
            out_tensor(pe, AT["mix0_out"], mix0_ready, mixT)
            norm_transpose(pe, 1)
            norm_ready(pe, 1)
            ffn_tensor(pe, PAST["ffn0"], "ffn0", (xnT_r, x_lo))
            norm_transpose(pe, 2)
            gdn_in_tensor(pe)
            gdn_core_tensor(pe)
            out_tensor(pe, AT["gdn_out"], lambda pe: pe.wait_ge(sem("gdn_mixT"), 4), mixT)
            norm_transpose(pe, 3)
            router_tensor(pe)
            experts_tensor(pe)
            norm_transpose(pe, 4)
            norm_ready(pe, 4)
            ffn_tensor(pe, PAST["ffn1"], "ffn1", (xnT_r, x_lo))
            norm_transpose(pe, 5)
            norm_ready(pe, 5)
            jobs_tensor(pe, JOBS_KV, kv_jobs, memT, FOUR)
            pe.wait_ge(sem("job_read"), len(kv_jobs))
            norm_transpose(pe, 6)
            norm_ready(pe, 6)
            jobs_tensor(pe, JOBS_HG, hg_jobs, None, FOUR, "hg_in")
            hg_tensor(pe)
            att_tensor(pe, len(att0), att2, att2_before)
            pe.wait_ge(sem("att_out"), len(att0) + len(att2))
            jobs_tensor(pe, JOBS_GL, gl_jobs, None, FOUR, "gl_in")
            branch_tensor(pe)
            out_tensor(pe, AT["mix2_out"], lambda pe: pe.wait_ge(sem("mixed_done"), KD), mixed)
            norm_transpose(pe, 7)
            norm_ready(pe, 7)
            ffn_tensor(pe, PAST["ffn2"], "ffn2", (xnT_r, x_lo))

        @block.scalar
        def _(act):
            act.wait_ge(sem("small_in"), 16)
            softplus_scalar(act, 1, lam_b)
            h_ready(act, 0)
            norm_square(act, 0, h)
            split_high(act, "mix0_in", 0)
            norm_high(act, 0, 0)
            for i in range(1, 7):
                split_high(act, "mix0_in", i)
            act.wait_ge(sem("rest_in"), 16)
            mix0_scalar(act)
            att_scalar(act, 0, att0)
            act.wait_ge(sem("att_out"), len(att0))
            for i in range(AHEAD):
                split_high(act, "ffn0", i)
            norm_square(act, 1, h, 1)
            for i in range(AHEAD, FIRST_SPLITS):
                split_high(act, "ffn0", i)
            norm_high(act, 1, 1)
            ffn_scalar(act, PAST["ffn0"], "ffn0")
            for i in (0, 1):
                split_high(act, "gdn_in", i)
            load_later(act, 0)
            norm_square(act, 2, h, 2)
            split_high(act, "gdn_in", 2)
            norm_high(act, 2, 2)
            for i in (3, 4):
                split_high(act, "gdn_in", i)
            gdn_in_scalar(act)
            gdn_core_scalar(act)
            h_ready(act, 3)
            act.dma_start(mem_rows, mem_d.rearrange("(t p) d -> p t d", p=P)).then_inc(sem("mem_in"), 16)
            load_post(act, 0)
            load_later(act, 1)
            norm_square(act, 3, h, 3)
            norm_out_act(act, 3, 3, xnT)
            router_scalar(act)
            experts_scalar(act)
            h_ready(act, 4)
            norm_square(act, 4, h)
            for i in range(AHEAD, FIRST_SPLITS):
                split_high(act, "ffn1", i)
            norm_high(act, 4, 4)
            ffn_scalar(act, PAST["ffn1"], "ffn1")
            act.wait_ge(sem("mem_in"), 16)
            norm_square(act, 5, mem_rows)
            norm_out_act(act, 5, 7, memT)
            post_square(act, 0, AT["mem_kv"])
            hg_prepare_scalar(act)
            jobs_scalar(act, JOBS_KV, kv_jobs, FOUR, 0, kv_outs[:2])
            norm_square(act, 6, h, 5)
            load_post(act, 1)
            jobs_scalar(act, JOBS_KV, kv_jobs, FOUR, 2, kv_outs[2:6])
            for i in range(3):
                split_high(act, "hg_in", i)
            jobs_scalar(act, JOBS_KV, kv_jobs, FOUR, 6, kv_outs[6:])
            norm_high(act, 6, 5)
            jobs_scalar(act, JOBS_HG, hg_jobs, FOUR, 0, hg_outs, "hg_in")
            hg_decay_scalar(act)
            jobs_scalar(act, JOBS_HG, hg_jobs, FOUR, len(hg_outs), dil_outs, "hg_in")
            hg_scalar(act)
            att_scalar(act, len(att0), att2)
            for i in (0, 1):
                split_high(act, "gl_in", i)
            act.wait_ge(sem("att_out"), len(att0) + len(att2))
            for i in (2, 3):
                split_high(act, "gl_in", i)
            jobs_scalar(act, JOBS_GL, gl_jobs, FOUR, 0, gl_outs, "gl_in")
            act.wait_ge(sem("mixed_done"), KD)
            for i in range(AHEAD):
                split_high(act, "ffn2", i)
            post_square(act, 1, AT["ffn2"])
            norm_square(act, 7, h, 6)
            load_post(act, 2)
            for i in range(AHEAD, FIRST_SPLITS):
                split_high(act, "ffn2", i)
            norm_high(act, 7, 6)
            ffn_scalar(act, PAST["ffn2"], "ffn2")
            post_square(act, 2, AT["end"])

        @block.vector
        def _(dve):
            ch = Chain(dve, "dve_step")
            V.memset(minus_half, -0.5).then_inc(sem("half_set"), 1)
            dve.wait_ge(sem("small_in"), 16)
            softplus_vector_a(ch, const("lam"), lam_b)
            dve.wait_ge(sem("softplus_z"), 1)
            neg_lam = lam_b[0]
            ch.step(V.tensor_scalar(neg_lam, const("lam"), -1.0, None, ALU.mult))
            softplus_vector_b(dve, ch, 1, neg_lam, lam_b, lam_s)
            ch.step(V.tensor_scalar(neg_s, lam_s, -8.0, None, ALU.mult))
            V.tensor_scalar(pos_s, lam_s, 8.0, None, ALU.mult).then_inc(sem("lam_done"), 1)
            dve.wait_ge(sem("x_in"), 16)
            norm_scale(dve, 0, h)
            split_low(dve, "mix0_in", 0)
            norm_low(dve, 0, 0)
            for i in (1, 2):
                split_low(dve, "mix0_in", i)
            dve.wait_ge(sem("rest_in"), 16)
            mix0_vector(dve, ch)
            mix0_vector_lru(dve, ch)
            att_vector(dve, ch, 0, att0)
            for i in range(AHEAD):
                split_low(dve, "ffn0", i)
            add_product(dve, AT["mix0_out"] + 4)
            dve.wait_ge(sem("h_done"), NT)
            norm_scale(dve, 1, h)
            norm_low(dve, 1, 1)
            for i in range(AHEAD, FIRST_SPLITS):
                split_low(dve, "ffn0", i)
            ffn_vector(dve, ch, PAST["ffn0"], "ffn0")
            for i in (0, 1):
                split_low(dve, "gdn_in", i)
            add_product(dve, AT["gdn_in"])
            dve.wait_ge(sem("h_done"), 2 * NT)
            norm_scale(dve, 2, h)
            norm_low(dve, 2, 2)
            gdn_in_vector(dve, ch)
            gdn_core_vector(dve, ch)
            add_product(dve, AT["moe"])
            dve.wait_ge(sem("h_done"), 3 * NT)
            norm_scale(dve, 3, h)
            norm_out_dve(dve, 3, 3, xnT)
            router_vector(dve, ch)
            experts_vector(dve, ch)
            dve.wait_ge(sem("h_done"), 4 * NT)
            norm_scale(dve, 4, h)
            norm_low(dve, 4, 4)
            for i in range(AHEAD, FIRST_SPLITS):
                split_low(dve, "ffn1", i)
            ffn_vector(dve, ch, PAST["ffn1"], "ffn1")
            dve.wait_ge(sem("mem_in"), 16)
            norm_scale(dve, 5, mem_rows)
            norm_out_dve(dve, 5, 7, memT)
            post_add(dve, ch, 0, 0.5)
            hg_prepare(dve, ch)
            dve.wait_ge(sem("h_done"), 5 * NT)
            norm_scale(dve, 6, h)
            for i in range(3):
                split_low(dve, "hg_in", i)
            norm_low(dve, 6, 5)
            for i in range(3, 11):
                split_low(dve, "hg_in", i)
            hg_decay_vector(dve, ch)
            for i in range(11, 28):
                split_low(dve, "hg_in", i)
            hg_vector(dve, ch)
            dve.wait_ge(sem("later_in"), 32)
            att_vector(dve, ch, len(att0), att2)
            for i in range(12):
                split_low(dve, "gl_in", i)
            branch_vector(dve, ch)
            for i in range(AHEAD):
                split_low(dve, "ffn2", i)
            post_add(dve, ch, 1, 1.0)
            dve.wait_ge(sem("h_done"), 6 * NT)
            norm_scale(dve, 7, h)
            norm_low(dve, 7, 6)
            for i in range(AHEAD, FIRST_SPLITS):
                split_low(dve, "ffn2", i)
            ffn_vector(dve, ch, PAST["ffn2"], "ffn2")
            post_add(dve, ch, 2, 0.5)

        @block.gpsimd
        def _(pool):
            pool.wait_ge(sem("half_set"), 1)
            norm_pow(pool, 0)
            for part, o in enumerate((slice(0, 16), slice(16, 20))):
                pool.wait_ge(sem("head_var"), part + 1)
                G.tensor_tensor(qk_rstd[:, o], qk_var[:, o], minus_half[:, 0:1].broadcast_to([P, o.stop - o.start]),
                                ALU.pow).then_inc(sem("head_rstd"), 1)
            norm_pow(pool, 1)
            norm_pow(pool, 2)
            gdn_splits(pool)
            gdn_core_pool(pool)
            norm_pow(pool, 3)
            norm_pow(pool, 4)
            norm_pow(pool, 5)
            post_pow(pool, 0)
            norm_pow(pool, 6)
            hg_pool(pool)
            post_pow(pool, 1)
            norm_pow(pool, 7)
            post_pow(pool, 2)


def col(v):
    return v.reshape(-1, P).T


def row(v):
    return np.broadcast_to(v.reshape(1, -1), (P, v.size))


def rows_of(w):
    k, n = w.shape
    return w.reshape(k // P, P, n).transpose(1, 0, 2).reshape(P, -1)


def block_diagonal(w):
    out = np.zeros((4, P, P), w.dtype)
    out[:, 0:64, 0:64] = w[0::2]
    out[:, 64:128, 64:128] = w[1::2]
    return out.transpose(1, 0, 2).reshape(P, -1)


def shape_constants():
    f = np.float32
    i = np.arange(P)
    p, c = i[:, None], i[None, :]
    same = (p // CHUNK) == (c // CHUNK)
    q2, k2 = P + p, np.arange(2 * P)[None, :]
    dist = q2 - k2
    inv = (f(10000.0) ** (-np.arange(32, dtype=f) / f(32))).astype(f)
    ang = np.arange(S, dtype=f)[:, None] * inv[None, :]
    return {
        "ident": np.eye(P), "cum": same & (p <= c), "same": same, "ones": np.ones((P, P)),
        "before": p < c, "iota": row(np.arange(P)),
        "low": np.where(same & (p >= c), 0, BIG), "up": np.where(same & (p <= c), 0, -BIG),
        "band": np.where((dist >= 0) & (dist < P), 0, -BIG),
        "cos": rows_of(np.cos(ang)), "sin": rows_of(np.sin(ang)), "reset": row((np.arange(S) % CHUNK != 0) * 1.0),
    }


def late_constants():
    i = np.arange(P)
    p, c = i[:, None], i[None, :]
    level = [(((p >> k) & 1) == 1) & ((p >> k) == (c >> k) + 1) for k in range(6)]
    d = P + p - np.arange(2 * P)[None, :]
    steps = [(d >= 0) & (d <= 128), (d >= 0) & (d % 4 == 0), (d >= 0) & (d % 16 == 0)]
    return np.concatenate(level, 1), np.concatenate([np.where(m, -d, -BIG) for m in steps], 1)


def pack_small(a):
    heads = [h for c in range(4) for h in (c, c + 4)]
    tiles = dict(shape_constants())
    tiles["gain"] = np.concatenate([col(v) for v in (
        a["ln_mix"][0], a["ln_ffn"][0], a["ln_mix"][1], a["ln_ffn"][1], a["ffn1_pre_w_2"][0], a["mix_pre_w_2"][0],
        a["ffn2_pre_w_2"][0], a["mem_norm_w_2"][0])], 1)
    tiles["lru_w"] = rows_of(np.ascontiguousarray(a["e_lru_conv_w"][0].T))
    tiles["lru_b"] = col(a["e_lru_conv_b"][0])
    tiles["lru_wa"] = block_diagonal(a["e_lru_w_a"][0])
    tiles["lru_wi"] = block_diagonal(a["e_lru_w_i"][0])
    tiles["lru_ba"], tiles["lru_bi"] = col(a["e_lru_b_a"][0]), col(a["e_lru_b_i"][0])
    tiles["lam"] = col(a["e_lru_lambda"][0])
    tiles["q_norm"], tiles["k_norm"] = row(a["e_q_norm"][0]), row(a["e_k_norm"][0])
    tiles["sinks"] = row(a["e_sinks"][0][heads])
    tiles["gdn_conv"] = rows_of(np.ascontiguousarray(a["o_conv_w"][0].T))
    tiles["w_ab"] = rows_of(a["o_w_in"][0][:, 4096:])
    tiles["a_log"], tiles["dt_bias"] = row(a["o_a_log"][0]), row(a["o_dt_bias"][0])
    tiles["out_norm"] = row(a["o_out_norm"][0])
    tiles["router"] = rows_of(a["o_router"][0])
    tiles["b_gate"] = col(a["b_gate_2"][0])
    tiles["hg_logits"] = np.concatenate([col(a["hg_lb_logits_2"][0]), col(a["hg_lb_logits_2"][1])], 1)
    tiles["hg_norm"] = row(a["hg_norm_w_2"][0])
    out = np.empty((P, SMALL), np.float32)
    for name, (o, width) in COLS.items():
        assert tiles[name].shape == (P, width), (name, tiles[name].shape, width)
        out[:, o:o + width] = tiles[name]
    return out


def pack_post(a):
    out = np.zeros((5, P, D), np.float32)
    for i, k in enumerate(("ffn1_post_w_2", "mix_post_w_2", "ffn2_post_w_2")):
        out[i] = row(a[k][0])
    level, dist = late_constants()
    out[3, :, 0:6 * P], out[4, :, 0:6 * P] = level, dist
    return out


def pack_weights(a):
    out = np.empty((UNITS, P, UNIT), np.float32)
    at = [0]

    def cols(w, perm=None):
        k, n = w.shape
        m = n // 256
        out[at[0]:at[0] + m].reshape(m, P, k // P, 256)[:] = w.reshape(k // P, P, m, 256).transpose(2, 1, 0, 3)
        at[0] += m

    def rows(w):
        k, n = w.shape
        m = k // 256
        out[at[0]:at[0] + m].reshape(m, P, 2, n)[:] = w.reshape(m, 2, P, n).transpose(0, 2, 1, 3)
        at[0] += m

    def half_cols(w):
        out[at[0]:at[0] + 2].reshape(2, P, 4, 512)[:] = w.reshape(4, P, 2, 512).transpose(2, 1, 0, 3)
        at[0] += 2

    def swiglu(gate, up, down):
        steps = down.shape[0] // 256
        for s in range(steps):
            for i, w in enumerate((gate, up)):
                out[at[0]:at[0] + 2].reshape(2, P, 4, 2, 256)[:, :, :, i] = \
                    w[:, s * 256:(s + 1) * 256].reshape(2, 4, P, 256).transpose(0, 2, 1, 3)
            at[0] += 2
            if s:
                rows(down[(s - 1) * 256:s * 256])
        rows(down[(steps - 1) * 256:])

    heads = [h for c in range(4) for h in (c, c + 4)]
    w = a["e_w_in"][0]
    q = w[:, 1024:1536].reshape(D, 8, 64)[:, heads].reshape(D, 512)
    cols(w[:, 0:1024])
    cols(q)
    cols(w[:, 1536:])
    w = a["e_w_out"][0]
    rows(w[0:512])
    rows(w[512:].reshape(8, 64, D)[heads].reshape(512, D))
    swiglu(a["e_ffn_w_gate"][0], a["e_ffn_w_up"][0], a["e_ffn_w_down"][0])
    assert at[0] == AT["gdn_in"]
    cols(a["o_w_in"][0][:, 0:4096])
    rows(a["o_w_out"][0])
    for e in range(EXPERTS):
        swiglu(a["o_moe_w_gate"][0, e], a["o_moe_w_up"][0, e], a["o_moe_w_down"][0, e])
    assert at[0] == AT["ffn1"]
    swiglu(a["ffn1_w_gu_2"][0][:, :FF], a["ffn1_w_gu_2"][0][:, FF:], a["ffn1_w_down_2"][0])
    cols(a["w_mem_kv_2"][0])
    cols(a["w_in_2"][0])
    assert at[0] == AT["branch"]
    for name in ("w_br_hg_2", "w_br_dil_2", "w_br_mem_2"):
        half_cols(a[name][0])
    rows(a["w_out_2"][0])
    swiglu(a["ffn2_w_gu_2"][0][:, :FF], a["ffn2_w_gu_2"][0][:, FF:], a["ffn2_w_down_2"][0])
    assert at[0] == UNITS
    return out


def kernel(**inputs):
    import concourse.bacc as bacc
    from concourse.bass_utils import run_bass_kernel_spmd

    a = {k: np.asarray(v) for k, v in inputs.items()}
    arrays = {"small": pack_small(a), "post": pack_post(a), "weights": pack_weights(a), "x": a["x"][0], "mem": a["mem_2"][0]}
    nc = bacc.Bacc("TRN2", target_bir_lowering=False, num_devices=1)
    args = [nc.dram_tensor(n, v.shape, F32, kind="ExternalInput").ap() for n, v in arrays.items()]
    out = nc.dram_tensor("out", (S, D), F32, kind="ExternalOutput").ap()
    build(nc, *args, out)
    r = run_bass_kernel_spmd(nc, [arrays], core_ids=[0])
    return r.results[0]["out"].reshape(1, S, D)
```
